# Optimizing a Trainium2 kernel written in Bass

```python
import math
import jax, jax.numpy as jnp
from jax import lax
import numpy as np

D_MODEL = 1024
BATCH = 1
SEQ = 512
DEPTH = 1

ATTN_HEADS = 8
ATTN_HEAD_DIM = 64
ATTN_WIDTH = ATTN_HEADS * ATTN_HEAD_DIM
IDX_HEADS = 8
IDX_DIM = 64
TOPK_MAX = 256
Q_BLOCK = 128
REL_BUCKETS = 32
REL_MAX_DISTANCE = 128
RWKV_HEADS = 8
RWKV_HEAD_DIM = 64
RWKV_WIDTH = RWKV_HEADS * RWKV_HEAD_DIM
DECAY_LORA = 64
AAA_LORA = 64
GATE_LORA = 160
FFN_HIDDEN = ((8 * D_MODEL + 3 * 256 - 1) // (3 * 256)) * 256

RMS_EPS = 1e-6
GN_EPS = 64e-5

ATTN_SPLITS = (ATTN_WIDTH, ATTN_WIDTH, ATTN_WIDTH, IDX_HEADS * IDX_DIM, IDX_DIM, IDX_HEADS)
RWKV_SPLITS = (RWKV_WIDTH, RWKV_WIDTH, RWKV_WIDTH, DECAY_LORA, AAA_LORA, GATE_LORA)
ATTN_IN = sum(ATTN_SPLITS)
RWKV_IN = sum(RWKV_SPLITS)
GATE_IN = 2 * D_MODEL
IN_WIDTH = ATTN_IN + RWKV_IN + GATE_IN


def _split(z, sizes):
    return jnp.split(z, [int(o) for o in np.cumsum(sizes)[:-1]], axis=-1)

def _rms_norm(x, gain):
    xf = x.astype(jnp.float32)
    y = xf * lax.rsqrt(jnp.mean(xf * xf, axis=-1, keepdims=True) + RMS_EPS)
    return (y * gain.astype(jnp.float32)).astype(x.dtype)

def _t5_bucket(dist):
    max_exact = REL_BUCKETS // 2
    d = jnp.maximum(dist, 0)
    log_ratio = jnp.log(jnp.maximum(d, 1).astype(jnp.float32) / max_exact) / math.log(REL_MAX_DISTANCE / max_exact)
    large = jnp.minimum(max_exact + (log_ratio * (REL_BUCKETS - max_exact)).astype(jnp.int32), REL_BUCKETS - 1)
    return jnp.where(d < max_exact, d, large)

def _sparse_attention(q, k, v, q_idx, k_idx, w_idx, rel_bias, topk):
    B, S, H, Dh = q.shape
    f32 = jnp.float32
    n_blocks = S // Q_BLOCK
    key_pos = jnp.arange(S, dtype=jnp.int32)
    batch_ix = jnp.arange(B)[:, None, None]
    k_idx32 = k_idx.astype(f32)
    rel_bias32 = rel_bias.astype(f32)
    scale = Dh ** -0.5

    def block(i):
        start = i * Q_BLOCK
        qb = lax.dynamic_slice_in_dim(q, start, Q_BLOCK, axis=1)
        qib = lax.dynamic_slice_in_dim(q_idx, start, Q_BLOCK, axis=1).astype(f32)
        wib = lax.dynamic_slice_in_dim(w_idx, start, Q_BLOCK, axis=1).astype(f32)
        q_pos = start + jnp.arange(Q_BLOCK, dtype=jnp.int32)
        head_scores = jax.nn.relu(jnp.einsum('bqhd,bsd->bqhs', qib, k_idx32) * IDX_DIM ** -0.5)
        scores = jnp.einsum('bqhs,bqh->bqs', head_scores, wib) * IDX_HEADS ** -0.5
        causal = key_pos[None, :] <= q_pos[:, None]
        scores = jnp.where(causal[None], scores, -jnp.inf)
        _, sel = lax.top_k(scores, topk)
        valid = sel <= q_pos[None, :, None]
        k_sel = k[batch_ix, sel]
        v_sel = v[batch_ix, sel]
        logits = jnp.einsum('bqhd,bqkhd->bhqk', qb, k_sel).astype(f32) * scale
        bias = rel_bias32[_t5_bucket(q_pos[None, :, None] - sel)]
        logits = logits + jnp.transpose(bias, (0, 3, 1, 2))
        logits = jnp.where(valid[:, None], logits, -jnp.inf)
        probs = jax.nn.softmax(logits, axis=-1).astype(v.dtype)
        return jnp.einsum('bhqk,bqkhd->bqhd', probs, v_sel)

    out = lax.map(block, jnp.arange(n_blocks, dtype=jnp.int32))
    return jnp.moveaxis(out, 0, 1).reshape(B, S, H * Dh)

def _rwkv7_time_mix(z, mu, w0, w2, a0, a2, g2, k_k, k_a, r_k, ln_w, ln_b):
    B, S, _ = z.shape
    H, N = RWKV_HEADS, RWKV_HEAD_DIM
    f32 = jnp.float32
    z = z.astype(f32)
    z_prev = jnp.pad(z, ((0, 0), (1, 0), (0, 0)))[:, :-1]
    z = z + mu * (z_prev - z)
    r, k, v, w_lo, a_lo, g_lo = _split(z, RWKV_SPLITS)
    w = -jax.nn.softplus(-(w0 + jnp.tanh(w_lo) @ w2)) - 0.5
    a = jax.nn.sigmoid(a0 + a_lo @ a2)
    g = jax.nn.sigmoid(g_lo) @ g2
    kk = (k * k_k).reshape(B, S, H, N)
    kk = kk / jnp.maximum(jnp.sqrt(jnp.sum(kk * kk, axis=-1, keepdims=True)), 1e-12)
    k = k * (1.0 + (a - 1.0) * k_a)

    def heads(t):
        return t.reshape(B, S, H, N)

    r_h, k_h, v_h, a_h = heads(r), heads(k), heads(v), heads(a)
    decay = jnp.exp(-jnp.exp(heads(w)))
    b_h = kk * a_h

    def step(state, inp):
        r_t, d_t, k_t, v_t, kk_t, b_t = inp
        s_a = jnp.einsum('bhvk,bhk->bhv', state, -kk_t)
        state = state * d_t[:, :, None, :] + s_a[..., None] * b_t[:, :, None, :] + v_t[..., None] * k_t[:, :, None, :]
        return state, jnp.einsum('bhvk,bhk->bhv', state, r_t)

    xs = tuple(jnp.moveaxis(t, 1, 0) for t in (r_h, decay, k_h, v_h, kk, b_h))
    _, y = lax.scan(step, jnp.zeros((B, H, N, N), f32), xs)
    y = jnp.moveaxis(y, 0, 1)
    mean = jnp.mean(y, axis=-1, keepdims=True)
    var = jnp.mean(jnp.square(y - mean), axis=-1, keepdims=True)
    y = ((y - mean) * lax.rsqrt(var + GN_EPS)).reshape(B, S, RWKV_WIDTH) * ln_w + ln_b
    bonus = jnp.sum(r_h * k_h * r_k, axis=-1, keepdims=True) * v_h
    y = y + bonus.reshape(B, S, RWKV_WIDTH)
    return y * g

def first_inputs(seed: int = 0) -> dict:
    key = jax.random.key(seed)
    ks = jax.random.split(key, 24)
    L = DEPTH

    def nrm(k, shape, scale):
        return jax.random.normal(k, shape, jnp.float32) * scale

    return {
        'x': nrm(ks[0], (BATCH, SEQ, D_MODEL), 1.0),
        'mix_norm': 1.0 + nrm(ks[1], (L, D_MODEL), 0.02),
        'w_in': nrm(ks[2], (L, D_MODEL, IN_WIDTH), D_MODEL ** -0.5),
        'attn_q_norm': 1.0 + nrm(ks[3], (L, ATTN_HEAD_DIM), 0.02),
        'attn_k_norm': 1.0 + nrm(ks[4], (L, ATTN_HEAD_DIM), 0.02),
        'rel_bias': nrm(ks[5], (REL_BUCKETS, ATTN_HEADS), 0.5),
        'rwkv_mu': jax.random.uniform(ks[6], (L, RWKV_IN), jnp.float32, 0.0, 1.0),
        'rwkv_w0': nrm(ks[7], (L, RWKV_WIDTH), 0.5),
        'rwkv_w2': nrm(ks[8], (L, DECAY_LORA, RWKV_WIDTH), 0.1),
        'rwkv_a0': nrm(ks[9], (L, RWKV_WIDTH), 0.1),
        'rwkv_a2': nrm(ks[10], (L, AAA_LORA, RWKV_WIDTH), 0.1),
        'rwkv_g2': nrm(ks[11], (L, GATE_LORA, RWKV_WIDTH), GATE_LORA ** -0.5),
        'rwkv_k_k': 0.85 + nrm(ks[12], (L, RWKV_WIDTH), 0.02),
        'rwkv_k_a': 1.0 + nrm(ks[13], (L, RWKV_WIDTH), 0.02),
        'rwkv_r_k': nrm(ks[14], (L, RWKV_HEADS, RWKV_HEAD_DIM), 0.1),
        'rwkv_ln_w': 1.0 + nrm(ks[15], (L, RWKV_WIDTH), 0.02),
        'rwkv_ln_b': nrm(ks[16], (L, RWKV_WIDTH), 0.02),
        'w_branch_attn': nrm(ks[17], (L, ATTN_WIDTH, D_MODEL), ATTN_WIDTH ** -0.5),
        'w_branch_rwkv': nrm(ks[18], (L, RWKV_WIDTH, D_MODEL), RWKV_WIDTH ** -0.5),
        'w_out': nrm(ks[19], (L, D_MODEL, D_MODEL), D_MODEL ** -0.5),
        'ffn_norm': 1.0 + nrm(ks[20], (L, D_MODEL), 0.02),
        'w_gate_up': nrm(ks[21], (L, D_MODEL, 2 * FFN_HIDDEN), D_MODEL ** -0.5),
        'w_down': nrm(ks[22], (L, FFN_HIDDEN, D_MODEL), FFN_HIDDEN ** -0.5),
    }

def first_block(x, mix_norm, w_in, attn_q_norm, attn_k_norm, rel_bias, rwkv_mu, rwkv_w0, rwkv_w2,
              rwkv_a0, rwkv_a2, rwkv_g2, rwkv_k_k, rwkv_k_a, rwkv_r_k, rwkv_ln_w, rwkv_ln_b,
              w_branch_attn, w_branch_rwkv, w_out, ffn_norm, w_gate_up, w_down):
    B, S, _ = x.shape
    topk = min(TOPK_MAX, S // 4)
    h = x
    for l in range(DEPTH):
        xn = _rms_norm(h, mix_norm[l])
        proj = xn @ w_in[l]
        attn_cols, rwkv_cols, gate_cols = _split(proj, (ATTN_IN, RWKV_IN, GATE_IN))
        q, k, v, q_idx, k_idx, w_idx = _split(attn_cols, ATTN_SPLITS)
        q = _rms_norm(q.reshape(B, S, ATTN_HEADS, ATTN_HEAD_DIM), attn_q_norm[l])
        k = _rms_norm(k.reshape(B, S, ATTN_HEADS, ATTN_HEAD_DIM), attn_k_norm[l])
        v = v.reshape(B, S, ATTN_HEADS, ATTN_HEAD_DIM)
        y_attn = _sparse_attention(q, k, v, q_idx.reshape(B, S, IDX_HEADS, IDX_DIM), k_idx, w_idx,
                                   rel_bias, topk)
        y_rwkv = _rwkv7_time_mix(rwkv_cols, rwkv_mu[l], rwkv_w0[l], rwkv_w2[l], rwkv_a0[l], rwkv_a2[l],
                                 rwkv_g2[l], rwkv_k_k[l], rwkv_k_a[l], rwkv_r_k[l], rwkv_ln_w[l],
                                 rwkv_ln_b[l]).astype(x.dtype)
        gate_attn, gate_rwkv = _split(gate_cols, (D_MODEL, D_MODEL))
        merged = (jax.nn.sigmoid(gate_attn) * (y_attn @ w_branch_attn[l])
                  + jax.nn.sigmoid(gate_rwkv) * (y_rwkv @ w_branch_rwkv[l]))
        h = h + merged @ w_out[l]
        hn = _rms_norm(h, ffn_norm[l])
        gate, up = _split(hn @ w_gate_up[l], (FFN_HIDDEN, FFN_HIDDEN))
        h = h + (jax.nn.silu(gate) * up) @ w_down[l]
    return h


_first_inputs = first_inputs


def first_inputs(seed=0):
    import zlib

    import numpy as np

    out = dict(_first_inputs(seed))
    spreads = {}
    factors = {'mix_norm': 3.059,
     'attn_q_norm': 8.0,
     'attn_k_norm': 26.79,
     'rwkv_a0': 3.681,
     'rwkv_k_k': 64.0,
     'rwkv_k_a': 7.411,
     'rwkv_ln_w': 64.0,
     'rwkv_ln_b': 64.0,
     'ffn_norm': 14.893,
     'rel_bias': 7.893}
    for name, (base, spread) in spreads.items():
        noise = np.random.default_rng([zlib.crc32(name.encode()), seed]).standard_normal(out[name].shape)
        drawn = base * np.exp(spread * noise) if base else spread * noise
        out[name] = __import__('jax').numpy.asarray(drawn.astype(out[name].dtype))
    for name, factor in factors.items():
        out[name] = (out[name] * factor).astype(out[name].dtype)
    return out


_narrow_inputs = first_inputs


def first_inputs(seed=0):

    out = dict(_narrow_inputs(seed))
    wider = {'attn_q_norm': 3.38, 'attn_k_norm': 4.03, 'rel_bias': 4.65, 'rwkv_k_k': 9.41}
    for name, times in wider.items():
        mean = out[name].mean()
        out[name] = (mean + times * (out[name] - mean)).astype(out[name].dtype)
    return out


CHUNK = 64
D_RNN = 1280
RNN_HEADS = 20
RNN_HEAD_DIM = D_RNN // RNN_HEADS
CONV_WIDTH = 4
LRU_C = 8.0
D_SGU = 1024
SGU_GROUPS = 8
SGU_GROUP_DIM = D_SGU // SGU_GROUPS
SGU_BLOCK = 128
N_BRANCH = 2
D_FF = 4 * D_MODEL
D_IN = 2 * D_RNN + 2 * D_SGU + N_BRANCH * D_MODEL
EPS = 1e-6


def rmsnorm(x, g):
    xf = x.astype(jnp.float32)
    y = xf * lax.rsqrt(jnp.mean(xf * xf, axis=-1, keepdims=True) + EPS)
    return (y * g.astype(jnp.float32)).astype(x.dtype)

def layernorm(x, g, b):
    xf = x.astype(jnp.float32)
    mu = jnp.mean(xf, axis=-1, keepdims=True)
    xc = xf - mu
    y = xc * lax.rsqrt(jnp.mean(xc * xc, axis=-1, keepdims=True) + EPS)
    return (y * g.astype(jnp.float32) + b.astype(jnp.float32)).astype(x.dtype)

def causal_depthwise_conv(x, w, b):
    s = x.shape[1]
    xp = jnp.pad(x, ((0, 0), (CONV_WIDTH - 1, 0), (0, 0)))
    y = b
    for k in range(CONV_WIDTH):
        y = y + xp[:, k:k + s, :] * w[k]
    return y

def rg_lru(x, w_a, b_a, w_x, b_x, lam):
    bsz, s, _ = x.shape
    xh = x.reshape(bsz, s, RNN_HEADS, RNN_HEAD_DIM)
    r = jax.nn.sigmoid(jnp.einsum('bshi,hij->bshj', xh, w_a) + b_a).reshape(bsz, s, D_RNN)
    i = jax.nn.sigmoid(jnp.einsum('bshi,hij->bshj', xh, w_x) + b_x).reshape(bsz, s, D_RNN)
    log_a = (-LRU_C * r.astype(jnp.float32)) * jax.nn.softplus(-lam.astype(jnp.float32))
    a = jnp.exp(log_a)
    norm = jnp.sqrt(-jnp.expm1(2.0 * log_a))
    u = norm * (i * x).astype(jnp.float32)

    def combine(left, right):
        a_l, b_l = left
        a_r, b_r = right
        return a_l * a_r, a_r * b_l + b_r

    _, h = lax.associative_scan(combine, (a, u), axis=1)
    return h.astype(x.dtype)

def spatial_gating(u, v, w_s, b_s, ln_g, ln_b):
    bsz, s, _ = u.shape
    nblk = s // SGU_BLOCK
    v = layernorm(v, ln_g, ln_b)
    vb = v.reshape(bsz, nblk, SGU_BLOCK, SGU_GROUPS, SGU_GROUP_DIM)
    chunk_id = jnp.arange(SGU_BLOCK) // CHUNK
    mask = (chunk_id[:, None] >= chunk_id[None, :]).astype(w_s.dtype)
    mixed = jnp.einsum('gts,bnsgc->bntgc', w_s * mask, vb)
    mixed = mixed + jnp.transpose(b_s)[None, None, :, :, None]
    return u * mixed.reshape(bsz, s, D_SGU)

def hybrid_layer(x, norm_mix_g, w_in, conv_w, conv_b, lru_w_a, lru_b_a, lru_w_x, lru_b_x,
                 lru_lambda, sgu_ln_g, sgu_ln_b, sgu_w_s, sgu_b_s, w_branch_a, w_branch_b,
                 w_out, norm_ffn_g, w_up, w_down):
    h = rmsnorm(x, norm_mix_g)
    proj = jnp.einsum('bsd,de->bse', h, w_in)
    cuts = np.cumsum([D_RNN, D_RNN, D_SGU, D_SGU, D_MODEL])
    x_rnn, g_rnn, u, v, gate_a, gate_b = jnp.split(proj, cuts, axis=-1)

    xr = causal_depthwise_conv(x_rnn, conv_w, conv_b)
    ya = rg_lru(xr, lru_w_a, lru_b_a, lru_w_x, lru_b_x, lru_lambda) * jax.nn.gelu(g_rnn)
    ya = jnp.einsum('bsr,rd->bsd', ya, w_branch_a)

    yb = spatial_gating(jax.nn.gelu(u), jax.nn.gelu(v), sgu_w_s, sgu_b_s, sgu_ln_g, sgu_ln_b)
    yb = jnp.einsum('bsc,cd->bsd', yb, w_branch_b)

    merged = jax.nn.sigmoid(gate_a) * ya + jax.nn.sigmoid(gate_b) * yb
    x = x + jnp.einsum('bsd,de->bse', merged, w_out)

    h2 = rmsnorm(x, norm_ffn_g)
    f = jnp.square(jax.nn.relu(jnp.einsum('bsd,df->bsf', h2, w_up)))
    return x + jnp.einsum('bsf,fd->bsd', f, w_down)

def second_inputs(seed: int = 0) -> dict:
    key = jax.random.key(seed)
    ks = jax.random.split(key, 24)
    f32 = jnp.float32

    def nrm(k, shape, scale):
        return jax.random.normal(k, shape, f32) * scale

    a_c = jax.random.uniform(ks[7], (DEPTH, D_RNN), f32, 0.9, 0.999)
    a0 = a_c ** (1.0 / LRU_C)
    lru_lambda = jnp.log(a0) - jnp.log1p(-a0)

    return {
        "x": nrm(ks[0], (BATCH, SEQ, D_MODEL), 1.0),
        "norm_mix_g": 1.0 + nrm(ks[1], (DEPTH, D_MODEL), 0.02),
        "w_in": nrm(ks[2], (DEPTH, D_MODEL, D_IN), D_MODEL ** -0.5),
        "conv_w": nrm(ks[3], (DEPTH, CONV_WIDTH, D_RNN), CONV_WIDTH ** -0.5),
        "conv_b": nrm(ks[4], (DEPTH, D_RNN), 0.02),
        "lru_w_a": nrm(ks[5], (DEPTH, RNN_HEADS, RNN_HEAD_DIM, RNN_HEAD_DIM), RNN_HEAD_DIM ** -0.5),
        "lru_b_a": nrm(ks[6], (DEPTH, RNN_HEADS, RNN_HEAD_DIM), 0.02),
        "lru_w_x": nrm(ks[8], (DEPTH, RNN_HEADS, RNN_HEAD_DIM, RNN_HEAD_DIM), RNN_HEAD_DIM ** -0.5),
        "lru_b_x": nrm(ks[9], (DEPTH, RNN_HEADS, RNN_HEAD_DIM), 0.02),
        "lru_lambda": lru_lambda,
        "sgu_ln_g": 1.0 + nrm(ks[10], (DEPTH, D_SGU), 0.02),
        "sgu_ln_b": nrm(ks[11], (DEPTH, D_SGU), 0.02),
        "sgu_w_s": nrm(ks[12], (DEPTH, SGU_GROUPS, SGU_BLOCK, SGU_BLOCK), SGU_BLOCK ** -0.5),
        "sgu_b_s": 1.0 + nrm(ks[13], (DEPTH, SGU_GROUPS, SGU_BLOCK), 0.02),
        "w_branch_a": nrm(ks[14], (DEPTH, D_RNN, D_MODEL), D_RNN ** -0.5),
        "w_branch_b": nrm(ks[15], (DEPTH, D_SGU, D_MODEL), D_SGU ** -0.5),
        "w_out": nrm(ks[16], (DEPTH, D_MODEL, D_MODEL), D_MODEL ** -0.5),
        "norm_ffn_g": 1.0 + nrm(ks[17], (DEPTH, D_MODEL), 0.02),
        "w_up": nrm(ks[18], (DEPTH, D_MODEL, D_FF), D_MODEL ** -0.5),
        "w_down": nrm(ks[19], (DEPTH, D_FF, D_MODEL), D_FF ** -0.5),
        "final_norm_g": 1.0 + nrm(ks[20], (D_MODEL,), 0.02),
    }

def second_block(x, norm_mix_g, w_in, conv_w, conv_b, lru_w_a, lru_b_a, lru_w_x, lru_b_x,
              lru_lambda, sgu_ln_g, sgu_ln_b, sgu_w_s, sgu_b_s, w_branch_a, w_branch_b,
              w_out, norm_ffn_g, w_up, w_down, final_norm_g):
    for l in range(DEPTH):
        x = hybrid_layer(x, norm_mix_g[l], w_in[l], conv_w[l], conv_b[l], lru_w_a[l], lru_b_a[l],
                         lru_w_x[l], lru_b_x[l], lru_lambda[l], sgu_ln_g[l], sgu_ln_b[l],
                         sgu_w_s[l], sgu_b_s[l], w_branch_a[l], w_branch_b[l], w_out[l],
                         norm_ffn_g[l], w_up[l], w_down[l])
    return rmsnorm(x, final_norm_g)


_first_inputs_2 = second_inputs


def second_inputs(seed=0):
    import zlib

    import numpy as np

    out = dict(_first_inputs_2(seed))
    spreads = {}
    factors = {'norm_mix_g': 3.885,
     'lru_b_a': 60.502,
     'lru_b_x': 51.103,
     'sgu_ln_g': 36.175,
     'sgu_ln_b': 33.39,
     'sgu_b_s': 29.128,
     'norm_ffn_g': 14.147,
     'final_norm_g': 8.813,
     'conv_b': 7.129}
    for name, (base, spread) in spreads.items():
        noise = np.random.default_rng([zlib.crc32(name.encode()), seed]).standard_normal(out[name].shape)
        drawn = base * np.exp(spread * noise) if base else spread * noise
        out[name] = __import__('jax').numpy.asarray(drawn.astype(out[name].dtype))
    for name, factor in factors.items():
        out[name] = (out[name] * factor).astype(out[name].dtype)
    return out


_narrow_inputs_2 = second_inputs


def second_inputs(seed=0):

    out = dict(_narrow_inputs_2(seed))
    wider = {'conv_b': 3.97,
     'lru_b_a': 4.02,
     'lru_b_x': 4.13,
     'sgu_ln_g': 4.03,
     'sgu_ln_b': 4.03,
     'sgu_b_s': 4.01,
     'final_norm_g': 3.35}
    for name, times in wider.items():
        mean = out[name].mean()
        out[name] = (mean + times * (out[name] - mean)).astype(out[name].dtype)
    return out


N_HEADS = 4
HEAD_DIM = D_MODEL // 8
MIX_W = N_HEADS * HEAD_DIM
N_BRANCH_3 = 3
GLA_RANK = 16
GLA_TAU = 16
CONV_K = 4
D_FF_3 = 4 * D_MODEL


def _in_sizes():
    H, W = N_HEADS, MIX_W
    return [W, W, W, W, H, H,
            W, W, W, W, GLA_RANK,
            W, W, W, W, H, H,
            N_BRANCH_3 * D_MODEL]

def rmsnorm_3(x, g):
    x32 = x.astype(jnp.float32)
    y = x32 * lax.rsqrt(jnp.mean(x32 * x32, axis=-1, keepdims=True) + EPS)
    return (y * g.astype(jnp.float32)).astype(x.dtype)

def head_rmsnorm(h, g):
    B_, S_, _ = h.shape
    hh = h.reshape(B_, S_, N_HEADS, HEAD_DIM)
    hh = hh * lax.rsqrt(jnp.mean(hh * hh, axis=-1, keepdims=True) + EPS)
    return hh.reshape(B_, S_, MIX_W) * g.astype(jnp.float32)

def l2norm_heads(h):
    B_, S_, _ = h.shape
    hh = h.reshape(B_, S_, N_HEADS, HEAD_DIM)
    hh = hh * lax.rsqrt(jnp.sum(hh * hh, axis=-1, keepdims=True) + EPS)
    return hh.reshape(B_, S_, MIX_W)

def to_chunks(t):
    B_, S_, HD = t.shape
    t = t.reshape(B_, S_ // CHUNK, CHUNK, N_HEADS, HD // N_HEADS)
    return t.transpose(1, 0, 3, 2, 4)

def scalar_chunks(t):
    B_, S_, H_ = t.shape
    return t.reshape(B_, S_ // CHUNK, CHUNK, H_).transpose(1, 0, 3, 2)

def from_chunks(t):
    NC, B_, H_, L_, d = t.shape
    return t.transpose(1, 0, 3, 2, 4).reshape(B_, NC * L_, H_ * d)

def causal_conv(x, w):
    K = w.shape[0]
    xp = jnp.pad(x, ((0, 0), (K - 1, 0), (0, 0)))
    return lax.conv_general_dilated(xp, w[:, None, :], window_strides=(1,), padding='VALID',
                                    dimension_numbers=('NWC', 'WIO', 'NWC'),
                                    feature_group_count=x.shape[-1])

def mlstm_chunk(carry, xs):
    C, n, m = carry
    q, k, v, li, lf = xs
    causal = jnp.tril(jnp.ones((CHUNK, CHUNK), dtype=bool))
    b = jnp.cumsum(lf, axis=-1)
    D = jnp.where(causal, b[..., :, None] - b[..., None, :] + li[..., None, :], -jnp.inf)
    inter = b + m[..., None]
    m_t = jnp.maximum(inter, jnp.max(D, axis=-1))
    P = jnp.exp(D - m_t[..., None]) * jnp.einsum('bhtk,bhsk->bhts', q, k)
    w_inter = jnp.exp(inter - m_t)
    num = jnp.einsum('bhts,bhsv->bhtv', P, v) + w_inter[..., None] * jnp.einsum('bhtk,bhkv->bhtv', q, C)
    den = jnp.sum(P, axis=-1) + w_inter * jnp.einsum('bhtk,bhk->bht', q, n)
    h = num / jnp.maximum(jnp.abs(den), jnp.exp(-m_t))[..., None]
    bL = b[..., -1]
    g_s = bL[..., None] - b + li
    m_new = jnp.maximum(bL + m, jnp.max(g_s, axis=-1))
    w_s = jnp.exp(g_s - m_new[..., None])
    w_old = jnp.exp(bL + m - m_new)
    C = w_old[..., None, None] * C + jnp.einsum('bhsk,bhsv->bhkv', k * w_s[..., None], v)
    n = w_old[..., None] * n + jnp.einsum('bhs,bhsk->bhk', w_s, k)
    return (C, n, m_new), h

def mlstm(q, k, v, li, lf):
    B_ = q.shape[0]
    init = (jnp.zeros((B_, N_HEADS, HEAD_DIM, HEAD_DIM), jnp.float32),
            jnp.zeros((B_, N_HEADS, HEAD_DIM), jnp.float32),
            jnp.zeros((B_, N_HEADS), jnp.float32))
    xs = (to_chunks(q * HEAD_DIM ** -0.5), to_chunks(k), to_chunks(v), scalar_chunks(li), scalar_chunks(lf))
    _, hs = lax.scan(mlstm_chunk, init, xs)
    return from_chunks(hs)

def gla_chunk(S, xs):
    q, k, v, g = xs
    causal = jnp.tril(jnp.ones((CHUNK, CHUNK), dtype=bool))
    b = jnp.cumsum(g, axis=2)
    diff = b[:, :, :, None, :] - b[:, :, None, :, :]
    decay = jnp.exp(jnp.where(causal[:, :, None], diff, -jnp.inf))
    A = jnp.einsum('bhtsk,bhsk->bhts', q[:, :, :, None, :] * decay, k)
    o = jnp.einsum('bhts,bhsv->bhtv', A, v) + jnp.einsum('bhtk,bhkv->bhtv', q * jnp.exp(b), S)
    bL = b[:, :, -1:, :]
    S = jnp.exp(bL[:, :, 0, :])[..., None] * S + jnp.einsum('bhsk,bhsv->bhkv', k * jnp.exp(bL - b), v)
    return S, o

def gla(q, k, v, g):
    B_ = q.shape[0]
    init = jnp.zeros((B_, N_HEADS, HEAD_DIM, HEAD_DIM), jnp.float32)
    xs = (to_chunks(q * HEAD_DIM ** -0.5), to_chunks(k), to_chunks(v), to_chunks(g))
    _, os_ = lax.scan(gla_chunk, init, xs)
    return from_chunks(os_)

def gdn_chunk(S, xs):
    q, k, v, g, beta = xs
    causal = jnp.tril(jnp.ones((CHUNK, CHUNK), dtype=bool))
    strict = jnp.tril(jnp.ones((CHUNK, CHUNK), dtype=bool), -1)
    b = jnp.cumsum(g, axis=-1)
    decay = jnp.exp(jnp.where(causal, b[..., :, None] - b[..., None, :], -jnp.inf))
    kk = jnp.einsum('bhtk,bhsk->bhts', k, k)
    A = jnp.where(strict, beta[..., None] * kk * decay, 0.0)
    eye = jnp.eye(CHUNK, dtype=A.dtype)
    rhs = jnp.concatenate([beta[..., None] * k * jnp.exp(b)[..., None], beta[..., None] * v], axis=-1)
    sol = lax.linalg.triangular_solve(eye + A, rhs, left_side=True, lower=True, unit_diagonal=True)
    w, u = sol[..., :HEAD_DIM], sol[..., HEAD_DIM:]
    v_new = u - jnp.einsum('bhtk,bhkv->bhtv', w, S)
    qk = jnp.einsum('bhtk,bhsk->bhts', q, k) * decay
    o = jnp.einsum('bhtk,bhkv->bhtv', q * jnp.exp(b)[..., None], S) + jnp.einsum('bhts,bhsv->bhtv', qk, v_new)
    bL = b[..., -1]
    S = jnp.exp(bL)[..., None, None] * S + jnp.einsum('bhsk,bhsv->bhkv', k * jnp.exp(bL[..., None] - b)[..., None], v_new)
    return S, o

def gated_deltanet(q, k, v, g, beta):
    B_ = q.shape[0]
    init = jnp.zeros((B_, N_HEADS, HEAD_DIM, HEAD_DIM), jnp.float32)
    xs = (to_chunks(q), to_chunks(k), to_chunks(v), scalar_chunks(g), scalar_chunks(beta))
    _, os_ = lax.scan(gdn_chunk, init, xs)
    return from_chunks(os_)

def mixer_block(u, w_in, b_if, w_gla_lr, b_gla, conv_w, a_log, dt_bias, g_hm, g_hl, g_hd, w_up, w_out):
    f32 = jnp.float32
    proj = u @ w_in
    idx = [int(i) for i in np.cumsum(_in_sizes())[:-1]]
    (mq, mk, mv, mo, mi, mf, lq, lk, lv, lr, llr, dq, dk, dv, dz, dbeta, da, gates) = jnp.split(proj, idx, axis=-1)
    B_, S_, _ = u.shape
    b_if = b_if.astype(f32)
    li = mi.astype(f32) + b_if[:N_HEADS]
    lf = jax.nn.log_sigmoid(mf.astype(f32) + b_if[N_HEADS:])
    h_m = mlstm(mq.astype(f32), mk.astype(f32), mv.astype(f32), li, lf)
    h_m = head_rmsnorm(jax.nn.sigmoid(mo.astype(f32)) * h_m, g_hm)
    lg = jax.nn.log_sigmoid(llr.astype(f32) @ w_gla_lr.astype(f32) + b_gla.astype(f32)) / GLA_TAU
    h_l = gla(lq.astype(f32), lk.astype(f32), lv.astype(f32), lg)
    h_l = head_rmsnorm(h_l, g_hl) * jax.nn.silu(lr.astype(f32))
    qkv = jax.nn.silu(causal_conv(jnp.concatenate([dq, dk, dv], axis=-1).astype(f32), conv_w.astype(f32)))
    gq, gk, gv = jnp.split(qkv, 3, axis=-1)
    gq = l2norm_heads(gq) * HEAD_DIM ** -0.5
    gk = l2norm_heads(gk)
    g_dec = -jnp.exp(a_log.astype(f32)) * jax.nn.softplus(da.astype(f32) + dt_bias.astype(f32))
    beta = jax.nn.sigmoid(dbeta.astype(f32))
    h_d = gated_deltanet(gq, gk, gv, g_dec, beta)
    h_d = head_rmsnorm(h_d, g_hd) * jax.nn.silu(dz.astype(f32))
    branches = jnp.stack([h_m, h_l, h_d], axis=2).astype(u.dtype)
    up = jnp.einsum('bsnc,ncd->bsnd', branches, w_up)
    gate = jax.nn.sigmoid(gates.reshape(B_, S_, N_BRANCH_3, D_MODEL))
    return jnp.sum(gate * up, axis=2) @ w_out

def third_inputs(seed: int = 0) -> dict:
    key = jax.random.key(seed)
    ks = jax.random.split(key, 20)
    n_in = sum(_in_sizes())

    def nrm(k, shape, scale):
        return jax.random.normal(k, shape, jnp.float32) * scale

    x = nrm(ks[0], (BATCH, SEQ, D_MODEL), 1.0)
    w_in = nrm(ks[1], (DEPTH, D_MODEL, n_in), D_MODEL ** -0.5)
    f_bias = jnp.linspace(3.0, 6.0, N_HEADS, dtype=jnp.float32)
    b_if = jnp.concatenate([nrm(ks[2], (DEPTH, N_HEADS), 0.1),
                            f_bias + nrm(ks[3], (DEPTH, N_HEADS), 0.1)], axis=-1)
    w_gla_lr = nrm(ks[4], (DEPTH, GLA_RANK, MIX_W), GLA_RANK ** -0.5)
    b_gla = nrm(ks[5], (DEPTH, MIX_W), 0.1)
    conv_gdn = nrm(ks[6], (DEPTH, CONV_K, 3 * MIX_W), CONV_K ** -0.5)
    a_log = jnp.log(jax.random.uniform(ks[7], (DEPTH, N_HEADS), jnp.float32, 1.0, 16.0))
    dt = jnp.exp(jax.random.uniform(ks[8], (DEPTH, N_HEADS), jnp.float32, np.log(1e-3), np.log(1e-1)))
    dt_bias = dt + jnp.log(-jnp.expm1(-dt))
    g_norm_mix = 1.0 + nrm(ks[9], (DEPTH, D_MODEL), 0.02)
    g_norm_mlp = 1.0 + nrm(ks[10], (DEPTH, D_MODEL), 0.02)
    g_head_mlstm = 1.0 + nrm(ks[11], (DEPTH, MIX_W), 0.02)
    g_head_gla = 1.0 + nrm(ks[12], (DEPTH, MIX_W), 0.02)
    g_head_gdn = 1.0 + nrm(ks[13], (DEPTH, MIX_W), 0.02)
    w_up = nrm(ks[14], (DEPTH, N_BRANCH_3, MIX_W, D_MODEL), MIX_W ** -0.5)
    w_out = nrm(ks[15], (DEPTH, D_MODEL, D_MODEL), D_MODEL ** -0.5)
    w_mlp_in = nrm(ks[16], (DEPTH, D_MODEL, D_FF_3), D_MODEL ** -0.5)
    w_mlp_out = nrm(ks[17], (DEPTH, D_FF_3, D_MODEL), D_FF_3 ** -0.5)
    g_final = 1.0 + nrm(ks[18], (D_MODEL,), 0.02)
    return {'x': x, 'w_in': w_in, 'b_if': b_if, 'w_gla_lr': w_gla_lr, 'b_gla': b_gla,
            'conv_gdn': conv_gdn, 'a_log': a_log, 'dt_bias': dt_bias,
            'g_norm_mix': g_norm_mix, 'g_norm_mlp': g_norm_mlp,
            'g_head_mlstm': g_head_mlstm, 'g_head_gla': g_head_gla, 'g_head_gdn': g_head_gdn,
            'w_up': w_up, 'w_out': w_out, 'w_mlp_in': w_mlp_in, 'w_mlp_out': w_mlp_out,
            'g_final': g_final}

def third_block(x, w_in, b_if, w_gla_lr, b_gla, conv_gdn, a_log, dt_bias, g_norm_mix, g_norm_mlp,
              g_head_mlstm, g_head_gla, g_head_gdn, w_up, w_out, w_mlp_in, w_mlp_out, g_final):
    for l in range(DEPTH):
        u = rmsnorm_3(x, g_norm_mix[l])
        x = x + mixer_block(u, w_in[l], b_if[l], w_gla_lr[l], b_gla[l], conv_gdn[l], a_log[l], dt_bias[l],
                            g_head_mlstm[l], g_head_gla[l], g_head_gdn[l], w_up[l], w_out[l]).astype(x.dtype)
        u = rmsnorm_3(x, g_norm_mlp[l])
        x = x + jnp.square(jax.nn.relu(u @ w_mlp_in[l])) @ w_mlp_out[l]
    return rmsnorm_3(x, g_final)


_first_inputs_3 = third_inputs


def third_inputs(seed=0):
    import zlib

    import numpy as np

    out = dict(_first_inputs_3(seed))
    spreads = {}
    factors = {'b_gla': 4.439,
     'g_norm_mlp': 3.593,
     'g_head_mlstm': 5.775,
     'g_head_gla': 8.0,
     'g_head_gdn': 8.0,
     'g_final': 2.918}
    for name, (base, spread) in spreads.items():
        noise = np.random.default_rng([zlib.crc32(name.encode()), seed]).standard_normal(out[name].shape)
        drawn = base * np.exp(spread * noise) if base else spread * noise
        out[name] = __import__('jax').numpy.asarray(drawn.astype(out[name].dtype))
    for name, factor in factors.items():
        out[name] = (out[name] * factor).astype(out[name].dtype)
    return out


_narrow_inputs_3 = third_inputs


def third_inputs(seed=0):

    out = dict(_narrow_inputs_3(seed))
    wider = {'g_head_mlstm': 4.25, 'g_head_gla': 5.44, 'g_head_gdn': 5.16, 'g_final': 3.28}
    for name, times in wider.items():
        mean = out[name].mean()
        out[name] = (mean + times * (out[name] - mean)).astype(out[name].dtype)
    return out


def setup_inputs(seed=0):
    out = dict(first_inputs(seed))
    for name, value in second_inputs(seed + 1).items():
        if name != "x":
            out[name + "_2"] = value
    for name, value in third_inputs(seed + 2).items():
        if name != "x":
            out[name + "_3"] = value
    return out


def reference(
    x, mix_norm, w_in, attn_q_norm, attn_k_norm, rel_bias, rwkv_mu, rwkv_w0, rwkv_w2, rwkv_a0,
    rwkv_a2, rwkv_g2, rwkv_k_k, rwkv_k_a, rwkv_r_k, rwkv_ln_w, rwkv_ln_b, w_branch_attn,
    w_branch_rwkv, w_out, ffn_norm, w_gate_up, w_down, norm_mix_g_2, w_in_2, conv_w_2, conv_b_2,
    lru_w_a_2, lru_b_a_2, lru_w_x_2, lru_b_x_2, lru_lambda_2, sgu_ln_g_2, sgu_ln_b_2, sgu_w_s_2,
    sgu_b_s_2, w_branch_a_2, w_branch_b_2, w_out_2, norm_ffn_g_2, w_up_2, w_down_2,
    final_norm_g_2, w_in_3, b_if_3, w_gla_lr_3, b_gla_3, conv_gdn_3, a_log_3, dt_bias_3,
    g_norm_mix_3, g_norm_mlp_3, g_head_mlstm_3, g_head_gla_3, g_head_gdn_3, w_up_3, w_out_3,
    w_mlp_in_3, w_mlp_out_3, g_final_3,
):
    x = first_block(
        x, mix_norm, w_in, attn_q_norm, attn_k_norm, rel_bias, rwkv_mu, rwkv_w0, rwkv_w2,
        rwkv_a0, rwkv_a2, rwkv_g2, rwkv_k_k, rwkv_k_a, rwkv_r_k, rwkv_ln_w, rwkv_ln_b,
        w_branch_attn, w_branch_rwkv, w_out, ffn_norm, w_gate_up, w_down,
    )
    x = second_block(
        x, norm_mix_g_2, w_in_2, conv_w_2, conv_b_2, lru_w_a_2, lru_b_a_2, lru_w_x_2, lru_b_x_2,
        lru_lambda_2, sgu_ln_g_2, sgu_ln_b_2, sgu_w_s_2, sgu_b_s_2, w_branch_a_2, w_branch_b_2,
        w_out_2, norm_ffn_g_2, w_up_2, w_down_2, final_norm_g_2,
    )
    return third_block(
        x, w_in_3, b_if_3, w_gla_lr_3, b_gla_3, conv_gdn_3, a_log_3, dt_bias_3, g_norm_mix_3,
        g_norm_mlp_3, g_head_mlstm_3, g_head_gla_3, g_head_gdn_3, w_up_3, w_out_3, w_mlp_in_3,
        w_mlp_out_3, g_final_3,
    )


_drawn_inputs = setup_inputs


def setup_inputs(seed=0):
    import zlib

    import numpy as np

    out = dict(_drawn_inputs(seed))
    spreads = {}
    factors = {'norm_mix_g_2': 2.677,
     'lru_lambda_2': 82.104,
     'a_log_3': 2.977,
     'g_norm_mlp_3': 2.869,
     'conv_w_2': 26.448,
     'conv_b_2': 55.36,
     'lru_w_a_2': 29.344,
     'lru_b_a_2': 64.0,
     'lru_w_x_2': 25.672,
     'lru_b_x_2': 64.0,
     'w_branch_a_2': 8.0}
    for name, (base, spread) in spreads.items():
        noise = np.random.default_rng([zlib.crc32(name.encode()), seed]).standard_normal(out[name].shape)
        drawn = base * np.exp(spread * noise) if base else spread * noise
        out[name] = __import__('jax').numpy.asarray(drawn.astype(out[name].dtype))
    for name, factor in factors.items():
        out[name] = (out[name] * factor).astype(out[name].dtype)
    return out
```

```python
from contextlib import ExitStack

import numpy as np

import concourse.bass as bass
from concourse import mybir

F32 = mybir.dt.float32
ALU = mybir.AluOpType
ACT = mybir.ActivationFunctionType

P = 128
T = 512
NT = T // P
D = 1024
DC = D // P
HD = 64
RING = 4
SLAB = 18
NW = 62
TOPK = min(256, T // 4)
NEG = -1.0e30
PICKED = -3.0e38
EXPM05 = float(np.exp(-0.5))
LN2 = float(np.log(2.0))
FFN1 = ((8 * D + 3 * 256 - 1) // (3 * 256)) * 256 // P
FFN2 = 4 * D // P
RC = 1280 // P
NREL = T + P
BUCKETS = 32

VEC = {}
_at = 0
for _name, _n in [
    ("mix1", DC), ("qg", 1), ("kg", 1), ("mu", 16), ("w0", 4), ("a0", 4), ("kk", 4), ("ka", 4), ("rk", 4),
    ("lnw", 4), ("lnb", 4), ("ffn1", DC),
    ("mix2", DC), ("convb", RC), ("convw", 4 * RC), ("ba", RC), ("bx", RC), ("lam", RC), ("lng2", DC), ("lnb2", DC),
    ("ffn2", DC), ("fin2", DC),
    ("mix3", DC), ("bi", 1), ("bf", 1), ("bgla", 4), ("conv3", 48), ("alog", 1), ("dtb", 1), ("hm", 4), ("hl", 4),
    ("hd", 4), ("ffn3", DC), ("fin3", DC),
]:
    VEC[_name] = (_at, _n)
    _at += _n
NVEC = _at

CST = {}
_at = 0
for _name, _n in [("ident", P), ("ones", P), ("pair", P), ("flip", P), ("level", 7 * P), ("strict", P),
                  ("incl", P), ("caus", P), ("reset", T), ("sel", 4 * P)]:
    CST[_name] = (_at, _n)
    _at += _n
NCST = _at


def constants():
    c = np.zeros((P, NCST), np.float32)
    i = np.arange(P)

    def put(name, a):
        c[:, CST[name][0]:CST[name][0] + a.shape[1]] = a

    put("ident", np.eye(P))
    put("ones", np.ones((P, P)))
    put("pair", (i[:, None] // HD == i[None] // HD) * 1.0)
    put("flip", (i[:, None] + i[None] == P - 1) * 1.0)
    for n in range(7):
        h = 1 << n
        m = (i[:, None] // (2 * h) == i[None] // (2 * h)) & (i[:, None] % (2 * h) < h) & (i[None] % (2 * h) >= h)
        c[:, CST["level"][0] + n * P:CST["level"][0] + (n + 1) * P] = m
    put("strict", (i[:, None] < i[None]) * 1.0)
    put("incl", (i[:, None] <= i[None]) * 1.0)
    put("caus", np.where(i[None] <= i[:, None], 0.0, NEG))
    put("reset", np.broadcast_to((np.arange(T) % P != 0) * 1.0, (P, T)))
    sel = np.zeros((P, 4, P))
    for base in (0, 32):
        for h in range(4):
            sel[base + h, h] = 1.0
    put("sel", sel.reshape(P, 4 * P))
    return c


def bucket_table():
    d = np.maximum(T - 1 - np.arange(NREL), 0)
    half = BUCKETS // 2
    ratio = (np.log(np.maximum(d, 1).astype(np.float32) / half) / np.log(128 / half)).astype(np.float32)
    b = np.where(d < half, d, np.minimum(half + (ratio * half).astype(np.int32), BUCKETS - 1))
    return (np.arange(BUCKETS)[:, None] == b[None]).astype(np.float32)


class Count:

    def __init__(self):
        self.made, self.seen = {}, {}

    def up(self, sem):
        self.made[sem.name] = self.made.get(sem.name, 0) + 1
        return 1

    def own(self, sem):
        return self.made[sem.name]

    def next(self, sem, k=1):
        self.seen[sem.name] = self.seen.get(sem.name, 0) + k
        return self.seen[sem.name]


def program(nc, a, out):
    ctx = ExitStack()
    with ctx:
        xt = ctx.enter_context(nc.sbuf_tensor("xt", [P, DC, T], F32))
        xn = ctx.enter_context(nc.sbuf_tensor("xn", [P, DC, T], F32))
        ring = ctx.enter_context(nc.sbuf_tensor("ring", [P, RING, SLAB * P], F32))
        cst = ctx.enter_context(nc.sbuf_tensor("cst", [P, NCST], F32))
        vec = ctx.enter_context(nc.sbuf_tensor("vec", [P, NVEC], F32))
        small = ctx.enter_context(nc.sbuf_tensor("small", [P, 320], F32))
        work = ctx.enter_context(nc.sbuf_tensor("work", [P, NW * T], F32))
        bank = [ctx.enter_context(nc.psum_tensor(f"bank{i}", [P, T], F32)) for i in range(8)]
        sems = {}

        def S(name):
            if name not in sems:
                sems[name] = ctx.enter_context(nc.semaphore(name))
            return sems[name]

        psum_for = {"act": S("psum_for_act"), "dve": S("psum_for_dve")}
        evac_by = {"act": S("evac_by_act"), "dve": S("evac_by_dve")}
        landed = [S(f"slab_landed_{i}") for i in range(RING)]

        def W(i, n=1):
            return work[:, i * T:(i + n) * T]

        def W3(i, n):
            return W(i, n).rearrange("p (c t) -> p c t", c=n)

        def C(name, i=0, n=None):
            at, w = CST[name]
            return cst[:, at + i:at + i + (n or w)]

        def V(name, i=0):
            at = VEC[name][0] + i
            return vec[:, at:at + 1]

        def SM(i, n=1):
            return small[:, i:i + n]

        def dyn(ap3, i):
            if isinstance(i, int):
                return ap3[:, i, :]
            return ap3[:, bass.ds(i, 1), :].rearrange("p a t -> p (a t)")

        ident = C("ident")
        ones = C("ones")
        pair = C("pair")

        stream = [("w_in_a", 16, 16), ("w_merge1", 16, 0), ("w_out1", 4, 16), ("w_gu", FFN1, 16), ("w_down1", 16, 11),
                  ("w_in_b", RC, 16), ("w_uv", 8, 16), ("w_merge2", 16, 0), ("w_out2", 4, 16), ("w_up2", 16, 16),
                  ("w_down2", 16, 16),
                  ("w_in_m", 9, 16), ("w_in_l", 8, 16), ("w_in_d", 8, 16), ("w_merge3", 24, 0), ("w_out3", 4, 16),
                  ("w_up3", 16, 16), ("w_down3", 16, 16)]
        merge_slabs = {"w_merge1": [16, 8], "w_merge2": [16, RC + 8], "w_merge3": [16, 12, 8]}
        def gate_bank(nb, j, g):
            return (2 * nb * j + g) % 4

        handed_at = {}

        block = ctx.enter_context(nc.Block())

        @block.tensor
        def _(pe):
            n = Count()
            handed = {"act": 0, "dve": 0}
            last = [None] * 8
            slabs = [0]
            uses = [0] * RING
            begun = S("slab_begun")

            def hand(b, who):
                handed[who] += 1
                last[b] = (evac_by[who], handed[who])
                return 1

            def mark(stage):
                handed_at[stage] = dict(handed)

            def dense(stage, n_slabs, tiles, kc, moving, whos, split=1):
                handed_at[stage] = dict(handed)
                banks = RING // split
                per = RING * tiles // split
                who_of = [whos[p % len(whos)] for p in range(per)]
                each = {w: who_of.count(w) for w in ("act", "dve")}
                rank = [who_of[:p].count(who_of[p]) for p in range(per)]
                base, use0, hand0 = slabs[0], list(uses), dict(handed)

                def some(i, count, first):
                    for j in range(count):
                        slot = (base + j) % RING
                        pe.wait_ge(landed[slot], 16 * (use0[slot] + 1 + i))
                        for t in range(tiles):
                            p = (j * tiles + t) // split
                            b = p % banks
                            if j % split == 0:
                                if first and p < banks:
                                    if last[b]:
                                        pe.wait_ge(*last[b])
                                else:
                                    q, back = (p - banks, 0) if p >= banks else (p - banks + per, 1)
                                    pe.wait_ge(evac_by[who_of[p]], hand0[who_of[p]] + rank[q] + 1 +
                                               each[who_of[p]] * (i - back))
                            for k in range(kc):
                                at = (t * kc + k) * P
                                ins = pe.matmul(bank[b][:, :], ring[:, slot, at:at + P],
                                                moving(j % split * kc + k),
                                                start=(k == 0 and j % split == 0),
                                                stop=(k == kc - 1 and j % split == split - 1))
                                if t == 0 and k == 0:
                                    ins.then_inc(begun, 1)
                            if j % split == split - 1:
                                ins.then_inc(psum_for[who_of[p]], 1)

                whole, rest = divmod(n_slabs, RING)
                if whole:
                    some(0, RING, True)
                    if whole > 2:
                        with pe.Fori(1, whole) as i:
                            some(i, RING, False)
                    elif whole == 2:
                        some(1, RING, False)
                if rest:
                    some(whole, rest, whole == 0)
                for j in range(n_slabs):
                    uses[(base + j) % RING] += 1
                slabs[0] += n_slabs
                total = n_slabs * tiles // split
                for g in range(total):
                    w = who_of[g % per]
                    handed[w] += 1
                    last[g % banks] = (evac_by[w], handed[w])

            def slab():
                slot = slabs[0] % RING
                uses[slot] += 1
                slabs[0] += 1
                pe.wait_ge(landed[slot], 16 * uses[slot])
                return lambda k: ring[:, slot, k * P:(k + 1) * P]

            def merge(name, sources):
                layout = merge_slabs[name]
                nb = len(sources)
                mark(name)
                for j in range(DC):
                    todo = [("act", DC, lambda k: xn[:, k, :])] * nb + [("dve", len(s), lambda k, s=s: s[k]) for s in sources]
                    at, left, blocks = -1, 0, None
                    for g, (who, kc, mv) in enumerate(todo):
                        b = gate_bank(nb, j, g)
                        if last[b]:
                            pe.wait_ge(*last[b])
                        for k in range(kc):
                            if left == 0:
                                at += 1
                                left, pos = layout[at], 0
                                blocks = slab()
                                fresh = True
                            ins = pe.matmul(bank[b][:, :], blocks(pos), mv(k), start=(k == 0), stop=(k == kc - 1))
                            pos += 1
                            left -= 1
                            if fresh:
                                ins.then_inc(begun, 1)
                                fresh = False
                        ins.then_inc(psum_for[who], hand(b, who))

            def sum_tiles(tiles, b, who, lhsT, ready=None):
                if last[b]:
                    pe.wait_ge(*last[b])
                for k, t in enumerate(tiles):
                    if ready is not None:
                        pe.wait_ge(ready, n.next(ready))
                    ins = pe.matmul(bank[b][:, :], lhsT, t, start=(k == 0), stop=(k == len(tiles) - 1))
                ins.then_inc(psum_for[who], hand(b, who))
                return last[b]

            def turn(parts, b, who, row=0):
                if last[b]:
                    pe.wait_ge(*last[b])
                for in_, at in parts:
                    m, f = in_.shape[0], in_.shape[-1]
                    ins = pe.transpose(bank[b][0:f, at:at + m], in_, ident[row:row + m, row:row + m])
                ins.then_inc(psum_for[who], hand(b, who))
                return last[b]

            def norm(sq):
                sum_tiles([W(sq + c) for c in range(DC)], 4, "act", ones, S("squares_ready"))

            def merge_levels(group, heads, ready_x):
                am, x, xT, tt = group
                halves = heads // 4
                pe.wait_ge(ready_x, n.next(ready_x))
                waits = [turn([(xT(4 * hf + q), q * P) for q in range(4)], 4 + hf, "act") for hf in range(halves)]
                for lv in range(1, 7):
                    pe.wait_ge(S("level_masked"), n.next(S("level_masked")))
                    for w in waits:
                        pe.wait_ge(*w)
                    waits, products = [], []
                    for hf in range(halves):
                        if last[4 + hf]:
                            pe.wait_ge(*last[4 + hf])
                        for q in range(4):
                            h = 4 * hf + q
                            ins = pe.matmul(bank[4 + hf][:, q * P:(q + 1) * P], am(lv, h), x(h), start=True, stop=True)
                            if h == 0:
                                ins.then_inc(S("level_begun"), 1)
                        ins.then_inc(psum_for["act"], hand(4 + hf, "act"))
                        products.append(last[4 + hf])
                    for hf in range(halves):
                        pe.wait_ge(*products[hf])
                        for kind in ((1,) if lv == 6 else (0, 1)):
                            b = (6 if kind == 0 else 4) + hf
                            if last[b]:
                                pe.wait_ge(*last[b])
                            for q in range(4):
                                h = 4 * hf + q
                                if kind == 0:
                                    ins = pe.matmul(bank[b][:, q * P:(q + 1) * P], xT(h), tt(h), start=True, stop=True)
                                else:
                                    ins = pe.matmul(bank[b][:, q * P:(q + 1) * P], tt(h), xT(h), start=True, stop=True)
                            ins.then_inc(psum_for["dve"], hand(b, "dve"))
                            waits.append(last[b])
                for w in waits:
                    pe.wait_ge(*w)

            xnk = lambda k: xn[:, k, :]
            pe.wait_ge(S("loads_ready"), n.next(S("loads_ready"), 48))

            norm(0)
            pe.wait_ge(S("xn_ready"), n.next(S("xn_ready")))
            dense("in_a", 16, 2, DC, xnk, ["act"])
            pe.wait_ge(S("bias_loads"), n.next(S("bias_loads"), 32))
            for b, (at, w) in ((6, (0, T)), (7, (T, P))):
                if last[b]:
                    pe.wait_ge(*last[b])
                pe.matmul(bank[b][0:8, 0:w], W(61)[0:BUCKETS, 0:8], work[0:BUCKETS, 59 * T + at:59 * T + at + w],
                    start=True, stop=True)\
                    .then_inc(psum_for["act"], hand(b, "act"))
            for c in range(8):
                sum_tiles([W(48 + c)], 4 + c % 2, "act", pair, S("qk_square"))
            pe.wait_ge(S("table_back"), n.next(S("table_back"), 16))
            for h in range(8):
                if last[6 + h % 2]:
                    pe.wait_ge(*last[6 + h % 2])
                pe.matmul(bank[6 + h % 2][:, :], C("flip"), W(40 + h), start=True, stop=True)\
                    .then_inc(psum_for["act"], hand(6 + h % 2, "act"))
            mark("flipped")
            turn([(W(31)[:, t * P:(t + 1) * P], t * P) for t in range(NT)], 4, "dve")
            pe.wait_ge(S("qk_normed"), n.next(S("qk_normed"), 8))
            for t in range(NT):
                turn([(W(8 + c)[:, t * P:(t + 1) * P], c * P) for c in range(4)], 4 + t % 2, "act")
            mark("scores")
            for i in range(1, NT):
                for h in range(8):
                    r = slice(HD * (h % 2), HD * (h % 2) + HD)
                    if last[4 + h % 2]:
                        pe.wait_ge(*last[4 + h % 2])
                    pe.matmul(bank[4 + h % 2][:, 0:(i + 1) * P], W(12 + h // 2)[r, i * P:(i + 1) * P], W(30)[r,
                        0:(i + 1) * P], start=True, stop=True)\
                        .then_inc(psum_for["act"], hand(4 + h % 2, "act"))
            mark("attention")
            turned = {}
            steps = [(i, h) for i in range(NT) for h in range(8)]

            def logits(g):
                i, h = steps[g]
                r = slice(HD * (h % 2), HD * (h % 2) + HD)
                if last[4 + g % 2]:
                    pe.wait_ge(*last[4 + g % 2])
                pe.matmul(bank[4 + g % 2][:, 0:(i + 1) * P], W(h // 2)[r, i * P:(i + 1) * P], W(4 + h // 2)[r,
                    0:(i + 1) * P], start=True, stop=True)\
                    .then_inc(psum_for["dve"], hand(4 + g % 2, "dve"))

            def turn_probs(g):
                i, h = steps[g]
                pe.wait_ge(S("probs_ready"), n.next(S("probs_ready")))
                turned[g] = turn([(W(57 + g % 2)[:, s * P:(s + 1) * P], s * P) for s in range(i + 1)], 6, "act")

            def values(g):
                i, h = steps[g]
                r = slice(HD * (h % 2), HD * (h % 2) + HD)
                pe.wait_ge(*turned[g])
                if last[7]:
                    pe.wait_ge(*last[7])
                for s in range(i + 1):
                    ins = pe.matmul(bank[7][r, 0:P], W(48 + s)[:, h * HD:(h + 1) * HD],
                                    W(59 + g % 2)[:, s * P:(s + 1) * P], start=(s == 0), stop=(s == i))
                ins.then_inc(psum_for["act"], hand(7, "act"))

            logits(0)
            for g in range(len(steps) + 1):
                if g + 1 < len(steps):
                    logits(g + 1)
                if g < len(steps):
                    turn_probs(g)
                if g >= 1:
                    values(g - 1)

            mark("rwkv")
            pe.wait_ge(S("lora_ready"), n.next(S("lora_ready"), 3))
            pe.wait_ge(S("lora_loads"), n.next(S("lora_loads"), 48))
            for c in range(4):
                s = slice(c * P, (c + 1) * P)
                if last[4]:
                    pe.wait_ge(*last[4])
                pe.matmul(bank[4][:, :], W(59)[0:HD, s], W(28)[0:HD, :], start=True, stop=True)\
                    .then_inc(psum_for["act"], hand(4, "act"))
                if last[5]:
                    pe.wait_ge(*last[5])
                pe.matmul(bank[5][:, :], W(59)[HD:P, s], W(28)[HD:P, :], start=True, stop=True)\
                    .then_inc(psum_for["act"], hand(5, "act"))
                if last[6]:
                    pe.wait_ge(*last[6])
                pe.matmul(bank[6][:, :], W(60)[:, s], W(29), start=True, stop=False)
                pe.matmul(bank[6][:, :], W(61)[0:32, s], W(31)[0:32, :], start=False, stop=True)\
                    .then_inc(psum_for["act"], hand(6, "act"))
            mark("lora_end")
            for c in range(4):
                sum_tiles([W(28 + c)], 4 + c % 2, "dve", pair, S("kk_square"))
            for c in range(4):
                sum_tiles([W(28 + c)], 4 + c, "dve", pair, S("rk_ready"))
            pe.wait_ge(S("operands_ready"), n.next(S("operands_ready")))
            pe.wait_ge(S("operands_ready_2"), n.next(S("operands_ready_2")))
            ar = W(0, 8).rearrange("p (c n s t) -> p c n s t", c=4, n=NT, s=2)
            for ch in range(NT):
                cs = slice(ch * P, (ch + 1) * P)
                for src, b in ((8, 4), (12, 5), (24, 6)):
                    tokens = turn([(W(src + c)[:, cs], c * P) for c in range(4)], b, "act")
                for h in range(8):
                    r = slice(HD * (h % 2), HD * (h % 2) + HD)
                    b = 4 + h % 2
                    if last[b]:
                        pe.wait_ge(*last[b])
                    rhs = ar[r, h // 2, ch].rearrange("p s t -> p (s t)")
                    pe.matmul(bank[b][:, 0:2 * P], W(8 + h // 2)[r, cs], rhs, start=True, stop=True)
                    pe.matmul(bank[b][:, 2 * P:4 * P], W(12 + h // 2)[r, cs], rhs, start=True, stop=True)\
                        .then_inc(psum_for["dve"], hand(b, "dve"))
                v8 = lambda t, h: W(t, 2)[:, h * P:(h + 1) * P]
                merge_levels((lambda lv, h: v8(54 + 2 * (lv % 2), h), lambda h: v8(48, h), lambda h: v8(50, h),
                              lambda h: v8(52, h)), 8, S("inverse_start"))
                if ch:
                    pe.wait_ge(S("state_ready"), n.next(S("state_ready")))
                pe.wait_ge(*tokens)
                for par in range(2):
                    r = slice(HD * par, HD * par + HD)
                    if last[4 + par]:
                        pe.wait_ge(*last[4 + par])
                    for c in range(4):
                        h = 2 * c + par
                        o = bank[4 + par][:, c * HD:(c + 1) * HD]
                        if ch:
                            pe.matmul(o, ar[r, c, ch, 0, :], W(31)[r, c * HD:(c + 1) * HD], start=True, stop=False)
                        ins = pe.matmul(o, W(40 + h)[:, 2 * P:3 * P], W(30)[:, h * HD:(h + 1) * HD],
                                        start=(ch == 0), stop=True)
                    ins.then_inc(psum_for["dve"], hand(4 + par, "dve"))
                    rhs_token = last[4 + par]
                pe.wait_ge(*rhs_token)
                if last[6]:
                    pe.wait_ge(*last[6])
                for h in range(8):
                    ins = pe.matmul(bank[6][:, h * HD:(h + 1) * HD], v8(50, h), W(57)[:, h * HD:(h + 1) * HD],
                                    start=True, stop=True)
                ins.then_inc(psum_for["act"], hand(6, "act"))
                pe.wait_ge(*last[6])
                for par in range(2):
                    r = slice(HD * par, HD * par + HD)
                    if last[4 + par]:
                        pe.wait_ge(*last[4 + par])
                    for c in range(4):
                        h = 2 * c + par
                        hs = slice(h * HD, (h + 1) * HD)
                        o = bank[4 + par][r, c * P:(c + 1) * P]
                        if ch:
                            pe.matmul(o, W(31)[r, c * HD:(c + 1) * HD], ar[r, c, ch, 1, :], start=True, stop=False)
                        pe.matmul(o, W(56)[:, hs], W(40 + h)[:, P:2 * P], start=(ch == 0), stop=False)
                        ins = pe.matmul(o, W(30)[:, hs], W(40 + h)[:, 3 * P:4 * P], start=False, stop=True)
                    ins.then_inc(psum_for["act"], hand(4 + par, "act"))
                    y_token = last[4 + par]
                if ch < NT - 1:
                    if last[7]:
                        pe.wait_ge(*last[7])
                    for h in range(8):
                        r = slice(HD * (h % 2), HD * (h % 2) + HD)
                        hs = slice(h * HD, (h + 1) * HD)
                        o = bank[7][r, (h // 2) * HD:(h // 2 + 1) * HD]
                        pe.matmul(o, W(28)[:, hs], W(56)[:, hs], start=True, stop=False)
                        ins = pe.matmul(o, W(29)[:, hs], W(30)[:, hs], start=False, stop=True)
                    ins.then_inc(psum_for["dve"], hand(7, "dve"))
            pe.wait_ge(*y_token)
            mark("groupnorm")
            for c in range(4):
                if last[4 + c % 2]:
                    pe.wait_ge(*last[4 + c % 2])
                pe.matmul(bank[4 + c % 2][:, :], pair, W(58 + c), start=True, stop=True)\
                    .then_inc(psum_for["dve"], hand(4 + c % 2, "dve"))
            for c in range(4):
                sum_tiles([W(40 + c)], 6 + c % 2, "act", pair, S("y_square"))
            pe.wait_ge(S("branches_ready"), n.next(S("branches_ready")))
            merge("w_merge1", [[W(32 + c) for c in range(4)], [W(36 + c) for c in range(4)]])

            def tail(merged, sq, up_name, up_slabs, hidden, down_kc, whos):
                pe.wait_ge(S("merged_ready"), n.next(S("merged_ready")))
                dense(f"w_out{up_name}", 4, 2, DC, lambda k: W(merged + k), ["dve"])
                norm(sq)
                pe.wait_ge(S("xn_ready"), n.next(S("xn_ready")))
                dense(f"up{up_name}", up_slabs, 2, DC, xnk, whos)
                pe.wait_ge(S("hidden_ready"), n.next(S("hidden_ready")))
                dense(f"down{up_name}", 16, 1, down_kc, lambda k: W(hidden + k), ["dve"], split=2)

            tail(0, 40, "1", FFN1, 0, FFN1 // 2, ["act", "dve"])

            norm(40)
            pe.wait_ge(S("xn_ready"), n.next(S("xn_ready")))
            dense("in_b", RC, 2, DC, xnk, ["dve", "act"])
            pe.wait_ge(S("gate_loads"), n.next(S("gate_loads"), 64))
            pe.wait_ge(S("conv_done"), n.next(S("conv_done")))
            mark("lru")
            for c in range(RC):
                for w, b in ((51, 4), (56, 5)):
                    if last[b]:
                        pe.wait_ge(*last[b])
                    pe.matmul(bank[b][:, :], W(w, 5)[:, c * P:(c + 1) * P], W(21 + c), start=True, stop=True)\
                        .then_inc(psum_for["act"], hand(b, "act"))
            dense("uv", 8, 2, DC, xnk, ["act"])
            mark("sgu")
            pe.wait_ge(evac_by["act"], handed["act"])
            sum_tiles([W(29 + c) for c in range(8)], 4, "dve", ones)
            sum_tiles([W(37 + c) for c in range(8)], 5, "act", ones, S("v_square"))
            pe.wait_ge(S("v_normed"), n.next(S("v_normed")))
            pe.wait_ge(S("sgu_ready"), n.next(S("sgu_ready")))
            for t in range(NT):
                for hf in range(2):
                    v_token = turn([(W(29 + 4 * hf + q)[:, t * P:(t + 1) * P], q * P) for q in range(4)], 6 + hf, "act")
            pe.wait_ge(*v_token)
            for g in range(8):
                b = 4 + g % 2
                if last[b]:
                    pe.wait_ge(*last[b])
                for t in range(NT):
                    ins = pe.matmul(bank[b][:, t * P:(t + 1) * P], W(37 + 2 * t, 2)[:, g * P:(g + 1) * P],
                                    W(46, 2)[:, g * P:(g + 1) * P], start=True, stop=True)
                ins.then_inc(psum_for["dve"], hand(b, "dve"))
            pe.wait_ge(S("branches_ready"), n.next(S("branches_ready")))
            merge("w_merge2", [[W(11 + c) for c in range(RC)], [W(21 + c) for c in range(8)]])
            tail(37, 51, "2", 16, 0, 16, ["act"])
            norm(51)

            norm(51)
            pe.wait_ge(S("xn_ready"), n.next(S("xn_ready")))
            dense("in_m", 9, 2, DC, xnk, ["act"])
            pe.wait_ge(S("gates_ready"), n.next(S("gates_ready")))
            turn([(W(21)[0:4, t * P:(t + 1) * P], 4 * t) for t in range(NT)], 4, "act")
            mark("c_turned")
            for t in range(NT):
                turn([(W(8 + c)[:, t * P:(t + 1) * P], c * P) for c in range(4)], 4 + t % 2, "act")
            pe.wait_ge(S("decay_row"), n.next(S("decay_row")))
            for h in range(4):
                sel = C("sel", h * P, P)
                if last[5]:
                    pe.wait_ge(*last[5])
                pe.matmul(bank[5][:, :], sel[0:4, :], W(22)[0:4, :], start=True, stop=True)\
                    .then_inc(psum_for["dve"], hand(5, "dve"))
                for s in range(NT):
                    if last[6 + s % 2]:
                        pe.wait_ge(*last[6 + s % 2])
                    pe.matmul(bank[6 + s % 2][:, s * P:T], W(4 + h)[:, s * P:(s + 1) * P], W(h)[:, s * P:T],
                        start=True, stop=True)\
                        .then_inc(psum_for["dve"], hand(6 + s % 2, "dve"))
                if last[6]:
                    pe.wait_ge(*last[6])
                pe.matmul(bank[6][:, :], sel[0:4, :], W(24)[0:4, :], start=True, stop=True)\
                    .then_inc(psum_for["act"], hand(6, "act"))
                mark(f"floor{h}")
                pe.wait_ge(S("weights_ready"), n.next(S("weights_ready")))
                for lhs, b in ((ones, 5), (None, 4)):
                    if last[b]:
                        pe.wait_ge(*last[b])
                    for s in range(NT):
                        ins = pe.matmul(bank[b][:, s * P:T], W(25 + s)[:, h * P:(h + 1) * P] if lhs is None else lhs,
                                        W(33 + s)[:, s * P:T], start=(s == 0), stop=(s == NT - 1))
                    ins.then_inc(psum_for["dve"], hand(b, "dve"))
                pe.wait_ge(S("h_square"), n.next(S("h_square")))
                if last[7]:
                    pe.wait_ge(*last[7])
                pe.matmul(bank[7][:, :], ones, W(44), start=True, stop=True).then_inc(psum_for["act"], hand(7, "act"))

            dense("in_l", 8, 2, DC, xnk, ["act"])
            pe.wait_ge(S("gla_load"), n.next(S("gla_load"), 16))
            for c in range(4):
                if last[4 + c % 2]:
                    pe.wait_ge(*last[4 + c % 2])
                pe.matmul(bank[4 + c % 2][:, :], W(40)[64:80, c * P:(c + 1) * P], W(16)[64:80, :], start=True,
                    stop=True)\
                    .then_inc(psum_for["act"], hand(4 + c % 2, "act"))
            for t in range(NT):
                turn([(W(8 + c)[:, t * P:(t + 1) * P], c * P) for c in range(4)], 6 + t % 2, "act")
            lvl = 0
            for h in range(4):
                for half in (256, 128, 64, 32, 16, 8, 4, 2, 1, 0):
                    b = 4 + lvl % 2
                    qk = W(30 + lvl % 2)
                    if last[b]:
                        pe.wait_ge(*last[b])
                    if half:
                        pe.wait_ge(S("level_ready"), n.next(S("level_ready")))
                    if half == 256:
                        for s in range(2):
                            ins = pe.matmul(bank[b][:, s * 256:(s + 1) * 256], qk[:, s * P:(s + 1) * P], qk[:, 256:512],
                                            start=True, stop=True)
                    elif half == 128:
                        for s in range(2):
                            ins = pe.matmul(bank[b][:, s * P:(s + 1) * P], qk[:, 2 * s * P:(2 * s + 1) * P],
                                            qk[:, (2 * s + 1) * P:(2 * s + 2) * P], start=True, stop=True)
                    else:
                        for s in range(NT):
                            sl = slice(s * P, (s + 1) * P)
                            if half:
                                ins = pe.matmul(bank[b][:, sl], qk[:, sl], qk[:, sl], start=True, stop=True)
                            else:
                                ins = pe.matmul(bank[b][:, sl], W(4 + h)[:, sl], W(h)[:, sl], start=True, stop=True)
                    ins.then_inc(psum_for["dve"], hand(b, "dve"))
                    lvl += 1 if half else 0
                pe.wait_ge(S("weights_ready"), n.next(S("weights_ready")))
                if last[6]:
                    pe.wait_ge(*last[6])
                for s in range(NT):
                    ins = pe.matmul(bank[6][:, s * P:T], W(22 + s)[:, h * P:(h + 1) * P], W(32 + s)[:, s * P:T],
                                    start=(s == 0), stop=(s == NT - 1))
                ins.then_inc(psum_for["act"], hand(6, "act"))
                pe.wait_ge(S("h_square"), n.next(S("h_square")))
                if last[7]:
                    pe.wait_ge(*last[7])
                pe.matmul(bank[7][:, :], ones, W(42), start=True, stop=True).then_inc(psum_for["act"], hand(7, "act"))

            dense("in_d", 8, 2, DC, xnk, ["act"])
            mark("gdn")
            for c in range(8):
                sum_tiles([W(0 + c)], 4 + c % 2, "act", ones, S("qk_square"))
            pe.wait_ge(S("decay_row"), n.next(S("decay_row")))
            pe.wait_ge(S("beta_ready"), n.next(S("beta_ready")))
            turn([(W(48)[32:36, t * P:(t + 1) * P], 4 * t) for t in range(NT)], 4, "dve", row=32)
            for h in range(4):
                sel = C("sel", h * P, P)
                if last[5]:
                    pe.wait_ge(*last[5])
                pe.matmul(bank[5][:, :], sel[32:36, :], W(48)[32:36, :], start=True, stop=True)\
                    .then_inc(psum_for["dve"], hand(5, "dve"))
                if last[6 + h % 2]:
                    pe.wait_ge(*last[6 + h % 2])
                pe.matmul(bank[6 + h % 2][:, :], sel[32:36, :], W(17)[32:36, :], start=True, stop=True)\
                    .then_inc(psum_for["dve"], hand(6 + h % 2, "dve"))
            pe.wait_ge(S("operands_ready"), n.next(S("operands_ready")))
            kq = W(0, 8).rearrange("p (h n s t) -> p h n s t", h=4, n=NT, s=2)
            for t in range(NT):
                cs = slice(t * P, (t + 1) * P)
                turn([(W(34 + c)[:, cs], c * P) for c in range(4)], 4 + t % 2, "act")
            for t in range(NT):
                cs = slice(t * P, (t + 1) * P)
                tokens = turn([(W(26 + c)[:, cs], c * P) for c in range(4)], 4 + t % 2, "act")
            for h in range(4):
                for ch in range(NT):
                    m = h * NT + ch
                    b = 6 + m % 2
                    if last[b]:
                        pe.wait_ge(*last[b])
                    pe.matmul(bank[b][:, 0:2 * P], W(22 + h)[:, ch * P:(ch + 1) * P], kq[:, h,
                        ch].rearrange("p s t -> p (s t)"), start=True, stop=True)\
                        .then_inc(psum_for["dve"], hand(b, "dve"))
            for ch in range(NT):
                merge_levels((lambda lv, h: W(28 + lv % 2)[:, h * P:(h + 1) * P],
                              lambda h: W(26)[:, h * P:(h + 1) * P],
                              lambda h, ch=ch: W(22 + ch)[:, h * P:(h + 1) * P],
                              lambda h: W(27)[:, h * P:(h + 1) * P]), 4, S("inverse_start"))
            pe.wait_ge(*tokens)
            mats = W(42, 8).rearrange("p (h n s t) -> p h n s t", h=4, n=NT, s=2)
            for ch in range(NT):
                cs = slice(ch * P, (ch + 1) * P)
                hs = [slice(h * P, (h + 1) * P) for h in range(4)]
                if ch:
                    pe.wait_ge(*state)
                    if last[4]:
                        pe.wait_ge(*last[4])
                    for h in range(4):
                        ins = pe.matmul(bank[4][:, hs[h]], W(8 + h)[:, cs], W(41)[:, hs[h]], start=True, stop=True)
                    ins.then_inc(psum_for["dve"], hand(4, "dve"))
                    pe.wait_ge(*last[4])
                if last[5]:
                    pe.wait_ge(*last[5])
                for h in range(4):
                    ins = pe.matmul(bank[5][:, hs[h]], W(22 + ch)[:, hs[h]], (W(39) if ch else W(34 + ch))[:, hs[h]],
                                    start=True, stop=True)
                ins.then_inc(psum_for["act"], hand(5, "act"))
                pe.wait_ge(*last[5])
                if last[6]:
                    pe.wait_ge(*last[6])
                for h in range(4):
                    if ch:
                        pe.matmul(bank[6][:, hs[h]], W(41)[:, hs[h]], W(30 + h)[:, cs], start=True, stop=False)
                    ins = pe.matmul(bank[6][:, hs[h]], W(40)[:, hs[h]], mats[:, h, ch, 1, :], start=(ch == 0), stop=True)
                ins.then_inc(psum_for["act"], hand(6, "act"))
                if ch < NT - 1:
                    if last[7]:
                        pe.wait_ge(*last[7])
                    for h in range(4):
                        ins = pe.matmul(bank[7][:, hs[h]], W(18 + ch)[:, hs[h]], W(40)[:, hs[h]], start=True, stop=True)
                    ins.then_inc(psum_for["dve"], hand(7, "dve"))
                    state = last[7]
            for c in range(4):
                sum_tiles([W(42 + c)], 4 + c % 2, "act", ones, S("y_square"))
            pe.wait_ge(S("branches_ready"), n.next(S("branches_ready")))
            merge("w_merge3", [[W(50 + c) for c in range(4)], [W(54 + c) for c in range(4)], [W(58 + c) for c in range(4)]])
            tail(18, 26, "3", 16, 0, 16, ["act"])
            norm(51)

        @block.sync
        def _(sp):
            sp.dma_start(xt[:, :, :], a["x"]).then_inc(S("loads_ready"), 16)
            sp.dma_start(cst[:, :], a["cst"]).then_inc(S("loads_ready"), 16)
            sp.dma_start(vec[:, :], a["vec"]).then_inc(S("loads_ready"), 16)
            begun = S("slab_begun")
            count = 0
            for name, slabs, blocks in stream:
                w = a[name]
                if name in merge_slabs:
                    col = 0
                    sizes = merge_slabs[name]
                    for j in range(DC):
                        col = 0
                        for size in sizes:
                            if count >= RING:
                                sp.wait_ge(begun, count - RING + 2)
                            sp.dma_start(ring[:, count % RING, 0:size * P], w[j, :, col * P:(col + size) * P])\
                              .then_inc(landed[count % RING], 16)
                            count += 1
                            col += size
                    continue
                base = count

                def load(i, j):
                    slot = (base + j) % RING
                    idx = i * RING + j
                    if not (isinstance(i, int) and base + idx < RING):
                        sp.wait_ge(begun, idx + (base - RING + 2))
                    src = w[idx, :, :] if isinstance(idx, int) else \
                        w[bass.ds(idx, 1), :, :].rearrange("a p n -> (a p) n")
                    sp.dma_start(ring[:, slot, 0:blocks * P], src).then_inc(landed[slot], 16)

                whole, rest = divmod(slabs, RING)
                for j in range(RING if whole else 0):
                    load(0, j)
                if whole > 1:
                    with sp.Fori(1, whole) as i:
                        for j in range(RING):
                            load(i, j)
                for j in range(rest):
                    load(whole, j)
                count += slabs
            sp.wait_ge(S("result_ready"), 1)
            sp.dma_start(out, xt[:, :, :]).then_inc(S("result_stored"), 16)
            sp.wait_ge(S("result_stored"), 16)

        @block.scalar
        def _(act):
            n = Count()
            chain = S("act_chain")

            evac = evac_by["act"]

            def tiles(stage, total, fn, ring_banks=4):
                base = n.seen.get(psum_for["act"].name, 0)
                assert base == handed_at[stage]["act"], (stage, base, handed_at[stage])
                return base

            def copy_tiles(stage, total, dst, fn=None):
                base = tiles(stage, total, None)
                whole, rest = divmod(total, 4)

                def some(i, count):
                    for b in range(count):
                        act.wait_ge(psum_for["act"], i * 4 + (base + b + 1))
                        if fn is None:
                            ins = act.copy(dyn(dst, i * 4 + b), bank[b][:, :])
                        else:
                            ins = act.activation(dyn(dst, i * 4 + b), bank[b][:, :], fn)
                        ins.then_inc(evac, 1)

                with act.Fori(0, whole) as i:
                    some(i, 4)
                if rest:
                    some(whole, rest)
                n.seen[psum_for["act"].name] = base + total
                n.made[evac.name] = base + total
                act.wait_ge(evac, base + total)

            def norm(sq):
                for c in range(DC):
                    act.activation(W(sq + c), xt[:, c, :], ACT.Square)\
                        .then_inc(S("squares_ready"), n.up(S("squares_ready")))
                act.wait_ge(psum_for["act"], n.next(psum_for["act"]))
                act.activation(W(sq), bank[4][:, :], ACT.Ln, bias=eps[1e-06], scale=1.0 / D)\
                    .then_inc(evac, n.up(evac))
                act.wait_ge(evac, n.own(evac))
                act.activation(W(sq), W(sq), ACT.Exp, scale=-0.5).then_inc(S("rstd_ready"), n.up(S("rstd_ready")))
                act.wait_ge(S("rstd_ready"), n.own(S("rstd_ready")))

            eps = {}
            act.wait_ge(S("loads_ready"), n.next(S("loads_ready"), 48))
            act.wait_ge(S("small_consts"), n.next(S("small_consts")))
            eps[1e-6], eps[64e-6], eps[64e-5], eps["one"], eps["kk"] = SM(300), SM(301), SM(302), SM(303), SM(304)

            norm(0)
            copy_tiles("in_a", 32, W3(0, 32))
            for c in range(8):
                act.activation(W(48 + c), W(c), ACT.Square).then_inc(S("qk_square"), n.up(S("qk_square")))
            act.wait_ge(psum_for["act"], n.next(psum_for["act"]))
            act.copy(W(57)[0:8, :], bank[6][0:8, :]).then_inc(evac, n.up(evac))
            act.wait_ge(evac, n.own(evac))
            act.wait_ge(psum_for["act"], n.next(psum_for["act"]))
            act.copy(W(58)[0:8, 0:P], bank[7][0:8, 0:P]).then_inc(evac, n.up(evac))
            act.wait_ge(evac, n.own(evac))
            act.dma_start(a["scratch"], work[0:8, 57 * T:57 * T + NREL]).then_inc(S("table_out"), 16)
            act.wait_ge(S("table_out"), 16)
            act.dma_start(W3(40, 8), bass.AP(tensor=a["scratch"].tensor, offset=0, ap=[[1, P], [NREL, 8], [1, T]]))\
               .then_inc(S("table_back"), 16)
            for c in range(8):
                act.wait_ge(psum_for["act"], n.next(psum_for["act"]))
                if c < 4:
                    act.activation(W(48 + c), bank[4 + c % 2][:, :], ACT.Ln, bias=eps[6.4e-05], scale=1.0)\
                        .then_inc(evac, n.up(evac))
                    act.wait_ge(evac, n.own(evac))
                else:
                    act.activation(W(48 + c), bank[4 + c % 2][:, :], ACT.Ln, bias=eps[1e-06], scale=1.0 / HD)\
                        .then_inc(evac, n.up(evac))
                    act.wait_ge(evac, n.own(evac))
            for c in range(8):
                act.activation(W(48 + c), W(48 + c), ACT.Exp, scale=-0.5).then_inc(S("qk_rstd"), n.up(S("qk_rstd")))
            for h in range(8):
                act.wait_ge(psum_for["act"], n.next(psum_for["act"]))
                act.copy(W(40 + h), bank[6 + h % 2][:, :]).then_inc(S("evac_by_act"), n.up(S("evac_by_act")))
            act.wait_ge(S("qk_normed"), n.next(S("qk_normed"), 8))
            for t in range(NT):
                act.wait_ge(psum_for["act"], n.next(psum_for["act"]))
                act.copy(W(48 + t), bank[4 + t % 2][:, :]).then_inc(evac, n.up(evac))
            k = 0
            for i in range(1, NT):
                for h in range(8):
                    act.wait_ge(psum_for["act"], n.next(psum_for["act"]))
                    if k >= 2:
                        act.wait_ge(S("relu_used"), n.next(S("relu_used")))
                    act.activation(W(55 + h % 2)[:, 0:(i + 1) * P], bank[4 + h % 2][:, 0:(i + 1) * P], ACT.Relu)\
                        .then_inc(evac, n.up(evac))
                    k += 1
            steps = [(i, h) for i in range(NT) for h in range(8)]
            act.wait_ge(S("relu_used"), n.next(S("relu_used"), 2))

            def exps(g):
                i, h = steps[g]
                b = g % 2
                act.wait_ge(S("logits_ready"), n.next(S("logits_ready")))
                act.activation(W(57 + b)[:, 0:(i + 1) * P], W(57 + b)[:, 0:(i + 1) * P], ACT.Exp, bias=SM(200 + b),
                    accum_out=SM(204 + b))\
                    .then_inc(S("exps_ready"), n.up(S("exps_ready")))
                act.wait_ge(S("exps_ready"), n.own(S("exps_ready")))

            def turned(g):
                i, h = steps[g]
                act.wait_ge(psum_for["act"], n.next(psum_for["act"]))
                act.copy(W(59 + g % 2)[:, 0:(i + 1) * P], bank[6][:, 0:(i + 1) * P]).then_inc(evac, n.up(evac))
                act.wait_ge(evac, n.own(evac))

            def valued(g):
                i, h = steps[g]
                r = slice(HD * (h % 2), HD * (h % 2) + HD)
                act.wait_ge(psum_for["act"], n.next(psum_for["act"]))
                act.copy(W(32 + h // 2)[r, i * P:(i + 1) * P], bank[7][r, 0:P]).then_inc(evac, n.up(evac))

            for g in range(len(steps) + 2):
                if g < len(steps):
                    exps(g)
                if 1 <= g <= len(steps):
                    turned(g - 1)
                if g >= 2:
                    valued(g - 2)

            act.wait_ge(S("shift_done"), n.next(S("shift_done"), 15))
            act.activation(W(28)[0:HD, :], W(28)[0:HD, :], ACT.Tanh).then_inc(S("lora_ready"), n.up(S("lora_ready")))
            act.activation(W(29), W(29), ACT.Sigmoid).then_inc(S("lora_ready"), n.up(S("lora_ready")))
            act.activation(W(31)[0:32, :], W(31)[0:32, :], ACT.Sigmoid)\
                .then_inc(S("lora_ready"), n.up(S("lora_ready")))
            for c in range(4):
                act.wait_ge(psum_for["act"], n.next(psum_for["act"]))
                act.activation(W(40 + c), bank[4][:, :], ACT.Sigmoid, bias=V("w0", c)).then_inc(evac, n.up(evac))
                act.wait_ge(psum_for["act"], n.next(psum_for["act"]))
                act.activation(W(52 + c), bank[5][:, :], ACT.Sigmoid, bias=V("a0", c)).then_inc(evac, n.up(evac))
                act.wait_ge(psum_for["act"], n.next(psum_for["act"]))
                act.copy(W(36 + c), bank[6][:, :]).then_inc(evac, n.up(evac))
            for c in range(4):
                act.wait_ge(S("kk_raw"), n.next(S("kk_raw")))
                act.activation(W(28 + c), W(56 + c), ACT.Square).then_inc(S("kk_square"), n.up(S("kk_square")))
            for c in range(4):
                act.wait_ge(evac_by["dve"], handed_at["lora_end"]["dve"] + c + 1)
                act.activation(W(28 + c), W(28 + c), ACT.Ln).then_inc(chain, n.up(chain))
                act.wait_ge(chain, n.own(chain))
            for c in range(4):
                act.activation(W(28 + c), W(28 + c), ACT.Exp, bias=eps["kk"], scale=-0.5)\
                    .then_inc(S("kk_rstd"), n.up(S("kk_rstd")))
            act.wait_ge(S("decay_sums"), n.next(S("decay_sums")))
            act.activation(SM(0, 16).rearrange("p (c n) -> p c n", c=4), W(44, 4).rearrange("p (c n t) -> p c n t",
                c=4, n=NT)[:, :, :, 63], ACT.Exp, scale=-EXPM05)\
                .then_inc(chain, n.up(chain))
            act.wait_ge(chain, n.own(chain))
            act.activation(W(44, 4), W(48, 4), ACT.Exp, scale=-EXPM05).then_inc(chain, n.up(chain))
            act.wait_ge(chain, n.own(chain))
            act.activation(W(48, 4), W(48, 4), ACT.Exp, scale=EXPM05).then_inc(chain, n.up(chain))
            act.wait_ge(chain, n.own(chain))
            act.activation(W(40, 4), W(40, 4), ACT.Exp, scale=-EXPM05)\
                .then_inc(S("decays_ready"), n.up(S("decays_ready")))
            act.wait_ge(S("decays_ready"), n.own(S("decays_ready")))
            for ch in range(NT):
                for dst, b in ((28, 4), (29, 5), (30, 6)):
                    act.wait_ge(psum_for["act"], n.next(psum_for["act"]))
                    act.copy(W(dst), bank[b][:, :]).then_inc(evac, n.up(evac))
                for hf in range(2):
                    act.wait_ge(psum_for["act"], n.next(psum_for["act"]))
                    act.copy(W(48 + hf), bank[4 + hf][:, :]).then_inc(evac, n.up(evac))
                for lv in range(1, 7):
                    for hf in range(2):
                        act.wait_ge(psum_for["act"], n.next(psum_for["act"]))
                        act.copy(W(52 + hf), bank[4 + hf][:, :]).then_inc(evac, n.up(evac))
                        act.wait_ge(evac, n.own(evac))
                act.wait_ge(psum_for["act"], n.next(psum_for["act"]))
                act.mul(W(56), bank[6][:, :], -1.0).then_inc(evac, n.up(evac))
                act.wait_ge(evac, n.own(evac))
                yv = W(58, 4).rearrange("p (c t) -> p c t", c=4)
                for par in range(2):
                    r = slice(HD * par, HD * par + HD)
                    act.wait_ge(psum_for["act"], n.next(psum_for["act"]))
                    act.copy(yv[r, :, ch * P:(ch + 1) * P], bank[4 + par][r, :].rearrange("p (c t) -> p c t", c=4))\
                        .then_inc(evac, n.up(evac))
                    act.wait_ge(evac, n.own(evac))
            for c in range(4):
                act.wait_ge(evac_by["dve"], handed_at["groupnorm"]["dve"] + c + 1)
                act.activation(W(40 + c), W(58 + c), ACT.Square).then_inc(S("y_square"), n.up(S("y_square")))
            for c in range(4):
                act.wait_ge(psum_for["act"], n.next(psum_for["act"]))
                act.activation(W(44 + c), bank[6 + c % 2][:, :], ACT.Ln, bias=eps[0.00064], scale=1.0 / HD)\
                    .then_inc(evac, n.up(evac))
                act.wait_ge(evac, n.own(evac))
            for c in range(4):
                act.activation(W(44 + c), W(44 + c), ACT.Exp, scale=-0.5).then_inc(S("y_rstd"), n.up(S("y_rstd")))

            def merge(name, nb, sg):
                for j in range(DC):
                    for g in range(nb):
                        act.wait_ge(psum_for["act"], n.next(psum_for["act"]))
                        if j >= 2:
                            act.wait_ge(evac_by["dve"], handed_at[name]["dve"] + nb * (j - 2) + g + 1)
                        act.activation(W(sg + nb * (j % 2) + g), bank[gate_bank(nb, j, g)][:, :], ACT.Sigmoid)\
                            .then_inc(evac, n.up(evac))

            act.wait_ge(S("branches_ready"), n.next(S("branches_ready")))
            merge("w_merge1", 2, 8)
            act.wait_ge(S("x_ready"), n.next(S("x_ready")))
            norm(40)
            b0 = tiles("up1", FFN1, None)
            d0 = handed_at["up1"]["dve"]

            def silu(i, count, first=False):
                for q in range(count):
                    act.wait_ge(psum_for["act"], i * 2 + (b0 + q + 1))
                    if not first:
                        act.wait_ge(evac_by["dve"], i * 2 + (d0 + q - 1))
                    act.activation(W(50 + q), bank[2 * q][:, :], ACT.Silu).then_inc(evac, 1)

            silu(0, 2, True)
            with act.Fori(1, FFN1 // 2) as i:
                silu(i, 2)
            n.seen[psum_for["act"].name] = b0 + FFN1
            n.made[evac.name] = b0 + FFN1
            act.wait_ge(evac, b0 + FFN1)

            act.wait_ge(S("x_ready"), n.next(S("x_ready")))
            norm(40)
            b0 = tiles("in_b", RC, None)
            G = W3(11, RC)
            with act.Fori(0, RC // 2) as i:
                for q in range(2):
                    act.wait_ge(psum_for["act"], i * 2 + (b0 + q + 1))
                    act.activation(dyn(G, i * 2 + q), bank[2 * q + 1][:, :], ACT.Gelu_apprx_tanh).then_inc(evac, 1)
            n.seen[psum_for["act"].name] = b0 + RC
            n.made[evac.name] = b0 + RC
            act.wait_ge(evac, b0 + RC)
            act.activation(SM(0, RC), vec[:, VEC["lam"][0]:VEC["lam"][0] + RC], ACT.Abs).then_inc(chain, n.up(chain))
            act.wait_ge(chain, n.own(chain))
            act.activation(SM(0, RC), SM(0, RC), ACT.Exp, scale=-1.0).then_inc(S("lam_exp"), n.up(S("lam_exp")))
            act.wait_ge(S("lam_exp"), n.own(S("lam_exp")))
            act.wait_ge(S("conv_done"), n.next(S("conv_done")))
            for c in range(RC):
                act.wait_ge(psum_for["act"], n.next(psum_for["act"]))
                act.activation(W(31 + c), bank[4][:, :], ACT.Sigmoid, bias=V("ba", c)).then_inc(evac, n.up(evac))
                act.wait_ge(psum_for["act"], n.next(psum_for["act"]))
                act.activation(W(c), bank[5][:, :], ACT.Sigmoid, bias=V("bx", c)).then_inc(evac, n.up(evac))
            act.wait_ge(evac, n.own(evac))
            act.wait_ge(S("softplus_ready"), n.next(S("softplus_ready")))
            for c in range(RC):
                act.activation(W(41 + c), W(31 + c), ACT.Tanh, scale=SM(20 + c)).then_inc(chain, n.up(chain))
            act.wait_ge(chain, n.own(chain))
            for c in range(RC):
                act.activation(W(31 + c), W(31 + c), ACT.Exp, scale=SM(30 + c)).then_inc(chain, n.up(chain))
            act.wait_ge(chain, n.own(chain))
            for c in range(RC):
                act.activation(W(51 + c), W(31 + c), ACT.Square).then_inc(S("a_square"), n.up(S("a_square")))
            for c in range(RC):
                act.wait_ge(S("norm_square"), n.next(S("norm_square")))
                act.activation(W(41 + c), W(41 + c), ACT.Sqrt).then_inc(S("lru_norm"), n.up(S("lru_norm")))
            act.wait_ge(S("ya_ready"), n.next(S("ya_ready")))
            copy_tiles("uv", 16, W3(21, 16), ACT.Gelu_apprx_tanh)
            for c in range(8):
                act.wait_ge(S("v_centred"), n.next(S("v_centred")))
                act.activation(W(37 + c), W(29 + c), ACT.Square).then_inc(S("v_square"), n.up(S("v_square")))
            act.wait_ge(psum_for["act"], n.next(psum_for["act"]))
            act.activation(W(45), bank[5][:, :], ACT.Ln, bias=eps[1e-06], scale=1.0 / D).then_inc(evac, n.up(evac))
            act.wait_ge(evac, n.own(evac))
            act.activation(W(45), W(45), ACT.Exp, scale=-0.5).then_inc(S("v_rstd"), n.up(S("v_rstd")))
            act.wait_ge(S("v_rstd"), n.own(S("v_rstd")))
            for t in range(NT):
                for hf in range(2):
                    act.wait_ge(psum_for["act"], n.next(psum_for["act"]))
                    act.copy(W(37 + 2 * t + hf), bank[6 + hf][:, :]).then_inc(evac, n.up(evac))
            act.wait_ge(S("branches_ready"), n.next(S("branches_ready")))
            merge("w_merge2", 2, 51)
            act.wait_ge(S("x_ready"), n.next(S("x_ready")))
            norm(51)
            copy_tiles("up2", FFN2, W3(0, FFN2), ACT.Relu)
            act.wait_ge(S("x_ready"), n.next(S("x_ready")))
            norm(51)

            act.wait_ge(S("x_ready"), n.next(S("x_ready")))
            norm(51)
            copy_tiles("in_m", 18, W3(0, 18))
            act.activation(W(18)[0:4, :], W(16)[0:4, :], ACT.Identity, bias=V("bi")[0:4]).then_inc(chain, n.up(chain))
            act.activation(W(19)[0:4, :], W(17)[0:4, :], ACT.Identity, bias=V("bf")[0:4]).then_inc(chain, n.up(chain))
            act.wait_ge(chain, n.own(chain))
            act.activation(W(20)[0:4, :], W(19)[0:4, :], ACT.Abs).then_inc(chain, n.up(chain))
            act.wait_ge(chain, n.own(chain))
            act.activation(W(20)[0:4, :], W(20)[0:4, :], ACT.Exp, scale=-1.0).then_inc(chain, n.up(chain))
            act.wait_ge(chain, n.own(chain))
            act.activation(W(20)[0:4, :], W(20)[0:4, :], ACT.Ln, bias=eps["one"][0:4])\
                .then_inc(S("lf_parts"), n.up(S("lf_parts")))
            act.wait_ge(S("lf_parts"), n.own(S("lf_parts")))
            for c in range(4):
                act.activation(W(12 + c), W(12 + c), ACT.Sigmoid).then_inc(chain, n.up(chain))
            act.wait_ge(psum_for["act"], n.next(psum_for["act"]))
            act.copy(SM(100, 16), bank[4][:, 0:16]).then_inc(evac, n.up(evac))
            act.wait_ge(evac, n.own(evac))
            for t in range(NT):
                act.wait_ge(psum_for["act"], n.next(psum_for["act"]))
                act.copy(W(25 + t), bank[4 + t % 2][:, :]).then_inc(evac, n.up(evac))
                act.wait_ge(evac, n.own(evac))
            act.wait_ge(S("m_sum"), n.next(S("m_sum")))
            act.activation(W(24)[0:4, :], W(24)[0:4, :], ACT.Exp, scale=-1.0)\
                .then_inc(S("decay_row"), n.up(S("decay_row")))
            act.wait_ge(S("decay_row"), n.own(S("decay_row")))
            for h in range(4):
                for s in range(NT):
                    act.wait_ge(S("exponent_ready"), n.next(S("exponent_ready")))
                    act.activation(W(29 + s)[:, s * P:T], W(29 + s)[:, s * P:T], ACT.Exp, scale=-1.0)\
                        .then_inc(S("exps3_ready"), n.up(S("exps3_ready")))
                act.wait_ge(psum_for["act"], n.next(psum_for["act"]))
                act.copy(W(41), bank[6][:, :]).then_inc(evac, n.up(evac))
                act.wait_ge(evac, n.own(evac))
                act.wait_ge(S("h_ready"), n.next(S("h_ready")))
                act.activation(W(44), W(43), ACT.Square).then_inc(S("h_square"), n.up(S("h_square")))
                act.wait_ge(psum_for["act"], n.next(psum_for["act"]))
                act.activation(W(44), bank[7][:, :], ACT.Ln, bias=eps[1e-06], scale=1.0 / P)\
                    .then_inc(evac, n.up(evac))
                act.wait_ge(evac, n.own(evac))
                act.activation(W(44), W(44), ACT.Exp, scale=-0.5).then_inc(S("h_rstd"), n.up(S("h_rstd")))
                act.wait_ge(S("h_rstd"), n.own(S("h_rstd")))

            act.wait_ge(S("m_done"), n.next(S("m_done")))
            copy_tiles("in_l", 16, W3(0, 16))
            for c in range(4):
                act.wait_ge(psum_for["act"], n.next(psum_for["act"]))
                act.activation(W(26 + c), bank[4 + c % 2][:, :], ACT.Identity, bias=V("bgla", c))\
                    .then_inc(evac, n.up(evac))
                act.wait_ge(evac, n.own(evac))
            act.activation(W(18, 4), W(26, 4), ACT.Abs).then_inc(chain, n.up(chain))
            act.wait_ge(chain, n.own(chain))
            act.activation(W(18, 4), W(18, 4), ACT.Exp, scale=-1.0).then_inc(chain, n.up(chain))
            act.wait_ge(chain, n.own(chain))
            act.activation(W(18, 4), W(18, 4), ACT.Ln, bias=eps["one"]).then_inc(S("lf_parts"), n.up(S("lf_parts")))
            act.wait_ge(S("lf_parts"), n.own(S("lf_parts")))
            act.activation(W(12, 4), W(12, 4), ACT.Silu).then_inc(chain, n.up(chain))
            act.wait_ge(chain, n.own(chain))
            for t in range(NT):
                act.wait_ge(psum_for["act"], n.next(psum_for["act"]))
                act.copy(W(22 + t), bank[6 + t % 2][:, :]).then_inc(evac, n.up(evac))
                act.wait_ge(evac, n.own(evac))
            lvl = 0
            for h in range(4):
                for half in (256, 128, 64, 32, 16, 8, 4, 2, 1):
                    act.wait_ge(S("exponent_ready"), n.next(S("exponent_ready")))
                    e = W(28 + lvl % 2).rearrange("p (n s t) -> p n s t", s=2, t=half)
                    dd = W(26 + lvl % 2).rearrange("p (n s t) -> p n s t", s=2, t=half)
                    act.activation(e[:, :, 0, :], dd[:, :, 0, :], ACT.Exp, scale=-1.0 / 16)\
                        .then_inc(chain, n.up(chain))
                    act.activation(e[:, :, 1, :], dd[:, :, 1, :], ACT.Exp, scale=1.0 / 16)\
                        .then_inc(S("exps3_ready"), n.up(S("exps3_ready")))
                    lvl += 1
                act.wait_ge(psum_for["act"], n.next(psum_for["act"]))
                if h:
                    act.wait_ge(S("h_used"), n.next(S("h_used")))
                act.mul(W(41), bank[6][:, :], float(P) ** (-0.5)).then_inc(evac, n.up(evac))
                act.wait_ge(evac, n.own(evac))
                act.activation(W(42), W(41), ACT.Square).then_inc(S("h_square"), n.up(S("h_square")))
                act.wait_ge(psum_for["act"], n.next(psum_for["act"]))
                act.activation(W(43), bank[7][:, :], ACT.Ln, bias=eps[1e-06], scale=1.0 / P)\
                    .then_inc(evac, n.up(evac))
                act.wait_ge(evac, n.own(evac))
                act.activation(W(43), W(43), ACT.Exp, scale=-0.5).then_inc(S("h_rstd"), n.up(S("h_rstd")))
                act.wait_ge(S("h_rstd"), n.own(S("h_rstd")))

            act.wait_ge(S("h_used"), n.next(S("h_used")))
            copy_tiles("in_d", 16, W3(0, 16))
            act.activation(W(17)[32:36, :], W(17)[32:36, :], ACT.Sigmoid)\
                .then_inc(S("beta_ready"), n.up(S("beta_ready")))
            act.wait_ge(S("beta_ready"), n.own(S("beta_ready")))
            act.activation(W(48)[32:36, :], W(16)[32:36, :], ACT.Identity, bias=V("dtb")[32:36])\
                .then_inc(chain, n.up(chain))
            act.wait_ge(chain, n.own(chain))
            act.activation(W(49)[32:36, :], W(48)[32:36, :], ACT.Abs).then_inc(chain, n.up(chain))
            act.wait_ge(chain, n.own(chain))
            act.activation(W(49)[32:36, :], W(49)[32:36, :], ACT.Exp, scale=-1.0).then_inc(chain, n.up(chain))
            act.wait_ge(chain, n.own(chain))
            act.activation(W(49)[32:36, :], W(49)[32:36, :], ACT.Ln, bias=eps["one"][32:36])\
                .then_inc(chain, n.up(chain))
            act.wait_ge(chain, n.own(chain))
            act.activation(SM(60)[32:36], V("alog")[32:36], ACT.Exp).then_inc(S("lf_parts"), n.up(S("lf_parts")))
            act.wait_ge(S("lf_parts"), n.own(S("lf_parts")))
            act.wait_ge(S("conv3_done"), n.next(S("conv3_done")))
            act.activation(W(18, 12), W(18, 12), ACT.Silu).then_inc(chain, n.up(chain))
            act.wait_ge(chain, n.own(chain))
            for c in range(8):
                act.activation(W(c), W(18 + c), ACT.Square).then_inc(S("qk_square"), n.up(S("qk_square")))
            for c in range(8):
                act.wait_ge(psum_for["act"], n.next(psum_for["act"]))
                act.activation(W(c), bank[4 + c % 2][:, :], ACT.Ln, bias=eps[1e-06]).then_inc(evac, n.up(evac))
                act.wait_ge(evac, n.own(evac))
            for c in range(8):
                act.activation(W(c), W(c), ACT.Exp, scale=-0.5).then_inc(S("qk_rstd"), n.up(S("qk_rstd")))
            act.activation(W(12, 4), W(12, 4), ACT.Silu).then_inc(chain, n.up(chain))
            act.wait_ge(chain, n.own(chain))
            act.wait_ge(S("b_rows"), n.next(S("b_rows")))
            act.activation(W(42, 4), W(42, 4), ACT.Exp).then_inc(chain, n.up(chain))
            act.activation(W(46, 4), W(46, 4), ACT.Exp).then_inc(chain, n.up(chain))
            act.activation(W(38, 4), W(38, 4), ACT.Exp).then_inc(S("decays_ready"), n.up(S("decays_ready")))
            act.wait_ge(S("decays_ready"), n.own(S("decays_ready")))
            for t in range(NT):
                act.wait_ge(psum_for["act"], n.next(psum_for["act"]))
                act.copy(W(18 + t), bank[4 + t % 2][:, :]).then_inc(evac, n.up(evac))
                act.wait_ge(evac, n.own(evac))
            for t in range(NT):
                act.wait_ge(psum_for["act"], n.next(psum_for["act"]))
                act.copy(W(34 + t), bank[4 + t % 2][:, :]).then_inc(evac, n.up(evac))
                act.wait_ge(evac, n.own(evac))
            for ch in range(NT):
                act.wait_ge(psum_for["act"], n.next(psum_for["act"]))
                act.copy(W(26), bank[4][:, :]).then_inc(evac, n.up(evac))
                act.wait_ge(evac, n.own(evac))
                for lv in range(1, 7):
                    act.wait_ge(psum_for["act"], n.next(psum_for["act"]))
                    act.copy(W(27), bank[4][:, :]).then_inc(evac, n.up(evac))
                    act.wait_ge(evac, n.own(evac))
            for ch in range(NT):
                act.wait_ge(psum_for["act"], n.next(psum_for["act"]))
                act.copy(W(40), bank[5][:, :]).then_inc(evac, n.up(evac))
                act.wait_ge(evac, n.own(evac))
                act.wait_ge(psum_for["act"], n.next(psum_for["act"]))
                act.copy(W3(4, 4)[:, :, ch * P:(ch + 1) * P], bank[6][:, :].rearrange("p (c t) -> p c t", c=4))\
                    .then_inc(evac, n.up(evac))
                act.wait_ge(evac, n.own(evac))
            for c in range(4):
                act.activation(W(42 + c), W(4 + c), ACT.Square).then_inc(S("y_square"), n.up(S("y_square")))
            for c in range(4):
                act.wait_ge(psum_for["act"], n.next(psum_for["act"]))
                act.activation(W(c), bank[4 + c % 2][:, :], ACT.Ln, bias=eps[1e-06], scale=1.0 / P)\
                    .then_inc(evac, n.up(evac))
                act.wait_ge(evac, n.own(evac))
            for c in range(4):
                act.activation(W(c), W(c), ACT.Exp, scale=-0.5).then_inc(S("y_rstd"), n.up(S("y_rstd")))
            act.wait_ge(S("branches_ready"), n.next(S("branches_ready")))
            merge("w_merge3", 3, 26)
            act.wait_ge(S("x_ready"), n.next(S("x_ready")))
            norm(26)
            copy_tiles("up3", FFN2, W3(0, FFN2), ACT.Relu)
            act.wait_ge(S("x_ready"), n.next(S("x_ready")))
            norm(51)

        @block.vector
        def _(dve):
            n = Count()
            chain = S("dve_chain")
            evac = evac_by["dve"]

            def norm(gain, dst, sem):
                dve.wait_ge(S("rstd_ready"), n.next(S("rstd_ready")))
                for c in range(DC):
                    lastone = c == DC - 1
                    sig = S(sem) if lastone else chain
                    dve.scalar_tensor_tensor(dst[:, c, :], xt[:, c, :], V(gain, c), W(norm_at[0]), ALU.mult, ALU.mult)\
                        .then_inc(sig, n.up(sig))
                    if lastone:
                        dve.wait_ge(sig, n.own(sig))

            norm_at = [0]

            def loop_tiles(stage, total, per, fn):
                base = n.seen.get(psum_for["dve"].name, 0)
                assert base == handed_at[stage]["dve"], (stage, base, handed_at[stage])
                whole, rest = divmod(total, per)

                def some(i, count):
                    for b in range(count):
                        dve.wait_ge(psum_for["dve"], i * per + (base + b + 1))
                        fn(i, b).then_inc(evac, 1)

                with dve.Fori(0, whole) as i:
                    some(i, per)
                if rest:
                    some(whole, rest)
                n.seen[psum_for["dve"].name] = base + total
                n.made[evac.name] = base + total
                dve.wait_ge(evac, base + total)

            def residual(stage, banks):
                def add(i, b):
                    t = dyn(xt, i * banks + b)
                    return dve.tensor_tensor(t, t, bank[b][:, :], ALU.add)
                loop_tiles(stage, DC, banks, add)
                dve.memset(SM(312), 0.0).then_inc(S("x_ready"), n.up(S("x_ready")))
                dve.wait_ge(S("x_ready"), n.own(S("x_ready")))

            def merge(name, nb, sg, out_at, tmp):
                for j in range(DC):
                    for g in range(nb):
                        dve.wait_ge(evac_by["act"], handed_at[name]["act"] + nb * j + g + 1)
                        dve.wait_ge(psum_for["dve"], n.next(psum_for["dve"]))
                        b = gate_bank(nb, j, nb + g)
                        o = W(out_at + j) if g == 0 else W(tmp)
                        dve.tensor_tensor(o, W(sg + nb * (j % 2) + g), bank[b][:, :], ALU.mult)\
                            .then_inc(evac, n.up(evac))
                        dve.wait_ge(evac, n.own(evac))
                        if g:
                            end = j == DC - 1 and g == nb - 1
                            sig = S("merged_ready") if end else chain
                            dve.tensor_tensor(W(out_at + j), W(out_at + j), W(tmp), ALU.add).then_inc(sig, n.up(sig))
                            dve.wait_ge(sig, n.own(sig))

            def squared_relu(stage, hidden):
                base = handed_at[stage]["act"]
                h3 = W3(hidden, FFN2)
                with dve.Fori(0, FFN2 // 4) as i:
                    for b in range(4):
                        dve.wait_ge(evac_by["act"], i * 4 + (base + b + 1))
                        t = dyn(h3, i * 4 + b)
                        dve.tensor_tensor(t, t, t, ALU.mult)
                dve.memset(SM(312), 0.0).then_inc(S("hidden_ready"), n.up(S("hidden_ready")))
                dve.wait_ge(S("hidden_ready"), n.own(S("hidden_ready")))

            def inverse_start(at, xT, heads):
                lv = C("level", 0, P).unsqueeze(1).broadcast_to([P, heads, P])
                ts3 = ident.unsqueeze(1).broadcast_to([P, heads, P])
                dve.tensor_tensor(xT, at, lv, ALU.mult).then_inc(chain, n.up(chain))
                dve.wait_ge(chain, n.own(chain))
                dve.tensor_tensor(xT, ts3, xT, ALU.subtract).then_inc(S("inverse_start"), n.up(S("inverse_start")))
                dve.wait_ge(S("inverse_start"), n.own(S("inverse_start")))

            def inverse_levels(x, xT, halves):
                for lv in range(1, 7):
                    for hf in range(halves):
                        if lv < 6:
                            dve.wait_ge(psum_for["dve"], n.next(psum_for["dve"]))
                            dve.tensor_tensor(x(hf), x(hf), bank[6 + hf][:, :], ALU.subtract)\
                                .then_inc(evac, n.up(evac))
                            dve.wait_ge(evac, n.own(evac))
                        dve.wait_ge(psum_for["dve"], n.next(psum_for["dve"]))
                        dve.tensor_tensor(xT(hf), xT(hf), bank[4 + hf][:, :], ALU.subtract).then_inc(evac, n.up(evac))
                        dve.wait_ge(evac, n.own(evac))

            for col, val in ((300, 1e-6), (301, 64e-6), (302, 64e-5), (303, 1.0), (304, 15 * LN2)):
                dve.memset(SM(col), val).then_inc(chain, n.up(chain))
            dve.memset(SM(312), 0.0).then_inc(S("small_consts"), n.up(S("small_consts")))
            dve.wait_ge(S("small_consts"), n.own(S("small_consts")))
            dve.wait_ge(S("loads_ready"), n.next(S("loads_ready"), 48))

            norm("mix1", xn, "xn_ready")
            for c in range(8):
                dve.wait_ge(S("qk_rstd"), n.next(S("qk_rstd")))
                dve.scalar_tensor_tensor(W(c), W(c), V("qg" if c < 4 else "kg"), W(48 + c), ALU.mult, ALU.mult)\
                    .then_inc(S("qk_normed"), n.up(S("qk_normed")))
            dve.wait_ge(psum_for["dve"], n.next(psum_for["dve"]))
            dve.tensor_copy(SM(210, 32).rearrange("p (t h) -> p t h", t=NT), bank[4][:,
                :].rearrange("p (t c) -> p t c", t=NT)[:, :, 32:40])\
                .then_inc(evac, n.up(evac))
            dve.wait_ge(evac, n.own(evac))
            k = 0
            mask_at = {1: 52 * T, 2: 52 * T + 256, 3: 52 * T + 640}
            for i in range(1, NT):
                w = (i + 1) * P
                sc = W(57)[:, 0:w]
                for h in range(8):
                    k += 1
                    dve.wait_ge(evac_by["act"], handed_at["scores"]["act"] + k)
                    if h == 0:
                        dve.tensor_scalar(sc, W(55)[:, 0:w], SM(210 + 8 * i), None, ALU.mult)\
                            .then_inc(S("relu_used"), n.up(S("relu_used")))
                        dve.wait_ge(S("relu_used"), n.own(S("relu_used")))
                    else:
                        dve.scalar_tensor_tensor(sc, W(55 + h % 2)[:, 0:w], SM(210 + 8 * i + h), sc, ALU.mult,
                            ALU.add)\
                            .then_inc(S("relu_used"), n.up(S("relu_used")))
                        dve.wait_ge(S("relu_used"), n.own(S("relu_used")))
                dve.tensor_tensor(sc[:, i * P:w], sc[:, i * P:w], C("caus"), ALU.add).then_inc(chain, n.up(chain))
                dve.wait_ge(chain, n.own(chain))
                for _ in range(TOPK // 8):
                    dve.max(SM(250, 8), sc).then_inc(chain, n.up(chain))
                    dve.wait_ge(chain, n.own(chain))
                    dve.match_replace(sc, SM(250, 8), sc, PICKED).then_inc(chain, n.up(chain))
                    dve.wait_ge(chain, n.own(chain))
                dve.tensor_scalar(work[:, mask_at[i]:mask_at[i] + w], sc, PICKED / 3 * 2, NEG, ALU.is_gt, ALU.mult)\
                    .then_inc(S("mask_ready"), n.up(S("mask_ready")))
                dve.wait_ge(S("mask_ready"), n.own(S("mask_ready")))
            steps = [(i, h) for i in range(NT) for h in range(8)]

            def add_max(g):
                i, h = steps[g]
                w, b = (i + 1) * P, g % 2
                dve.wait_ge(psum_for["dve"], n.next(psum_for["dve"]))
                dve.wait_ge(S("bias_ready"), n.next(S("bias_ready")))
                dve.tensor_tensor_reduce(out=W(57 + b)[:, 0:w], in0=bank[4 + b][:, 0:w], in1=W(55 + b)[:, 0:w],
                    scale=1.0, scalar=-3e+38, op0=ALU.add, op1=ALU.max, accum_out=SM(208 + b))\
                    .then_inc(evac, n.up(evac))
                dve.wait_ge(evac, n.own(evac))
                dve.tensor_scalar(SM(200 + b), SM(208 + b), -1.0, None, ALU.mult)\
                    .then_inc(S("logits_ready"), n.up(S("logits_ready")))
                dve.wait_ge(S("logits_ready"), n.own(S("logits_ready")))

            def scale_probs(g):
                i, h = steps[g]
                w, b = (i + 1) * P, g % 2
                dve.wait_ge(S("exps_ready"), n.next(S("exps_ready")))
                dve.reciprocal(SM(202 + b), SM(204 + b)).then_inc(chain, n.up(chain))
                dve.wait_ge(chain, n.own(chain))
                dve.tensor_scalar(W(57 + b)[:, 0:w], W(57 + b)[:, 0:w], SM(202 + b), None, ALU.mult)\
                    .then_inc(S("probs_ready"), n.up(S("probs_ready")))

            add_max(0)
            for g in range(len(steps)):
                if g + 1 < len(steps):
                    add_max(g + 1)
                scale_probs(g)

            for k, t in enumerate(list(range(16, 30)) + [31]):
                dve.wait_ge(S("shift_diff"), n.next(S("shift_diff")))
                dve.scalar_tensor_tensor(W(t), W(38 + k % 2), V("mu", t - 16), W(t), ALU.mult, ALU.add)\
                    .then_inc(S("shift_done"), n.up(S("shift_done")))
            dve.wait_ge(evac_by["act"], handed_at["rwkv"]["act"] + 12)
            for c in range(4):
                dve.tensor_tensor_scan(W(44 + c), C("reset"), W(40 + c), 0.0, ALU.mult, ALU.add)\
                    .then_inc(chain, n.up(chain))
                dve.wait_ge(chain, n.own(chain))
            c4 = lambda i: W(i, 4).rearrange("p (c n t) -> p c n t", c=4, n=NT)
            dve.tensor_tensor(c4(48), c4(44), c4(44)[:, :, :, 63:64].broadcast_to([P, 4, NT, P]), ALU.subtract)\
                .then_inc(chain, n.up(chain))
            dve.wait_ge(chain, n.own(chain))
            dve.tensor_tensor(W(40, 4), W(48, 4), W(40, 4), ALU.subtract)\
                .then_inc(S("decay_sums"), n.up(S("decay_sums")))
            dve.wait_ge(S("decay_sums"), n.own(S("decay_sums")))
            for c in range(4):
                dve.tensor_scalar(W(56 + c), W(20 + c), V("kk", c), None, ALU.mult)\
                    .then_inc(S("kk_raw"), n.up(S("kk_raw")))
            for c in range(4):
                dve.wait_ge(psum_for["dve"], n.next(psum_for["dve"]))
                dve.tensor_scalar(W(28 + c), bank[4 + c % 2][:, :], 1e-24, 2.0 ** 30, ALU.max, ALU.mult)\
                    .then_inc(evac, n.up(evac))
            dve.tensor_scalar(SM(40, 4), vec[:, VEC["ka"][0]:VEC["ka"][0] + 4], -1.0, 1.0, ALU.mult, ALU.add)\
                .then_inc(chain, n.up(chain))
            dve.wait_ge(chain, n.own(chain))
            for c in range(4):
                dve.wait_ge(S("kk_rstd"), n.next(S("kk_rstd")))
                dve.tensor_tensor(W(56 + c), W(56 + c), W(28 + c), ALU.mult).then_inc(chain, n.up(chain))
                dve.wait_ge(chain, n.own(chain))
                dve.tensor_scalar(W(60 + c % 2), W(52 + c), V("ka", c), SM(40 + c), ALU.mult, ALU.add)\
                    .then_inc(chain, n.up(chain))
                dve.wait_ge(chain, n.own(chain))
                dve.tensor_tensor(W(20 + c), W(20 + c), W(60 + c % 2), ALU.mult).then_inc(chain, n.up(chain))
                dve.wait_ge(chain, n.own(chain))
                dve.tensor_tensor(W(52 + c), W(56 + c), W(52 + c), ALU.mult).then_inc(chain, n.up(chain))
                dve.wait_ge(chain, n.own(chain))
                dve.scalar_tensor_tensor(W(28 + c), W(16 + c), V("rk", c), W(20 + c), ALU.mult, ALU.mult)\
                    .then_inc(S("rk_ready"), n.up(S("rk_ready")))
            dve.memset(SM(312), 0.0).then_inc(S("kb_ready"), n.up(S("kb_ready")))
            dve.wait_ge(S("kb_ready"), n.own(S("kb_ready")))
            dve.wait_ge(S("decays_ready"), n.next(S("decays_ready")))
            ar = W(0, 8).rearrange("p (c n s t) -> p c n s t", c=4, n=NT, s=2)
            for c in range(4):
                w3 = lambda i: W(i).rearrange("p (n t) -> p n t", n=NT)
                dve.tensor_tensor(ar[:, c, :, 0, :], w3(56 + c), w3(40 + c), ALU.mult).then_inc(chain, n.up(chain))
                dve.tensor_tensor(ar[:, c, :, 1, :], w3(16 + c), w3(44 + c), ALU.mult).then_inc(chain, n.up(chain))
            dve.tensor_tensor(SM(20, 12).rearrange("p (c n) -> p c n", c=4), c4(44)[:, :, 0:3, 127], SM(0,
                16).rearrange("p (c n) -> p c n", c=4)[:, :, 1:4], ALU.mult)\
                .then_inc(S("operands_ready"), n.up(S("operands_ready")))
            dve.wait_ge(S("operands_ready"), n.own(S("operands_ready")))
            for c in range(4):
                dve.wait_ge(psum_for["dve"], n.next(psum_for["dve"]))
                dve.tensor_tensor(W(16 + c), bank[4 + c][:, :], W(24 + c), ALU.mult).then_inc(evac, n.up(evac))
                dve.wait_ge(evac, n.own(evac))
            two = lambda name: C(name, 0, 2 * P).unsqueeze(1).broadcast_to([P, 2, 2 * P])
            s3 = W(31)[:, 0:4 * HD].rearrange("p (c v) -> p c v", c=4)
            for ch in range(NT):
                for h in range(8):
                    dve.wait_ge(psum_for["dve"], n.next(psum_for["dve"]))
                    dve.tensor_tensor(W(40 + h).rearrange("p (a b) -> p a b", a=2), bank[4 + h % 2][:,
                        :].rearrange("p (a b) -> p a b", a=2), two("strict"), ALU.mult)\
                        .then_inc(evac, n.up(evac))
                dve.wait_ge(evac, n.made[evac.name])
                at = W3(40, 8)[:, :, 0:P]
                inverse_start(at, W(50, 2).rearrange("p (h t) -> p h t", h=8), 8)
                inverse_levels(lambda hf: W(48 + hf), lambda hf: W(50 + hf), 2)
                r4 = W(57).rearrange("p (c s v) -> p c s v", c=4, s=2)
                for par in range(2):
                    dve.wait_ge(psum_for["dve"], n.next(psum_for["dve"]))
                    dve.tensor_copy(r4[:, :, par, :], bank[4 + par][:, 0:4 * HD].rearrange("p (c v) -> p c v", c=4))\
                        .then_inc(evac, n.up(evac))
                if ch < NT - 1:
                    dve.wait_ge(psum_for["dve"], n.next(psum_for["dve"]))
                    u3 = bank[7][:, 0:4 * HD].rearrange("p (c v) -> p c v", c=4)
                    gg = SM(20, 12).rearrange("p (c n) -> p c n", c=4)[:, :, ch:ch + 1].broadcast_to([P, 4, HD])
                    if ch == 0:
                        dve.tensor_copy(s3, u3).then_inc(evac, n.up(evac))
                        dve.wait_ge(evac, n.own(evac))
                    else:
                        dve.tensor_tensor(s3, s3, u3, ALU.add).then_inc(evac, n.up(evac))
                        dve.wait_ge(evac, n.own(evac))
                    dve.tensor_tensor(s3, s3, gg, ALU.mult).then_inc(S("state_ready"), n.up(S("state_ready")))
                    dve.wait_ge(S("state_ready"), n.own(S("state_ready")))
            for c in range(4):
                dve.wait_ge(psum_for["dve"], n.next(psum_for["dve"]))
                dve.scalar_tensor_tensor(W(58 + c), bank[4 + c % 2][:, :], -1.0 / HD, W(58 + c), ALU.mult, ALU.add)\
                    .then_inc(evac, n.up(evac))
                dve.wait_ge(evac, n.own(evac))
            for c in range(4):
                dve.wait_ge(S("y_rstd"), n.next(S("y_rstd")))
                dve.scalar_tensor_tensor(W(58 + c), W(58 + c), V("lnw", c), W(44 + c), ALU.mult, ALU.mult)\
                    .then_inc(chain, n.up(chain))
                dve.wait_ge(chain, n.own(chain))
                dve.scalar_tensor_tensor(W(58 + c), W(58 + c), V("lnb", c), W(16 + c), ALU.add, ALU.add)\
                    .then_inc(chain, n.up(chain))
                dve.wait_ge(chain, n.own(chain))
                sig = S("branches_ready") if c == 3 else chain
                dve.tensor_tensor(W(36 + c), W(58 + c), W(36 + c), ALU.mult).then_inc(sig, n.up(sig))
                dve.wait_ge(sig, n.own(sig))

            merge("w_merge1", 2, 8, 0, 12)
            residual("w_out1", 4)
            norm_at[0] = 40
            norm("ffn1", xn, "xn_ready")
            a0 = handed_at["up1"]["act"]

            def gated(i, b):
                dve.wait_ge(evac_by["act"], i * 2 + (a0 + b + 1))
                return dve.tensor_tensor(dyn(W3(0, FFN1), i * 2 + b), W(50 + b), bank[2 * b + 1][:, :], ALU.mult)

            loop_tiles("up1", FFN1, 2, gated)
            dve.memset(SM(312), 0.0).then_inc(S("hidden_ready"), n.up(S("hidden_ready")))
            dve.wait_ge(S("hidden_ready"), n.own(S("hidden_ready")))
            residual("down1", 2)

            norm("mix2", xn, "xn_ready")
            xr = work[:, 0:RC * 515].rearrange("p (c t) -> p c t", c=RC)
            dve.memset(xr[:, :, 0:3], 0.0).then_inc(chain, n.up(chain))

            def put_x(i, b):
                k = i * 2 + b
                o = xr[:, k, 3:515] if isinstance(k, int) else xr[:, bass.ds(k, 1), 3:515].rearrange("p a t -> p (a t)")
                return dve.tensor_copy(o, bank[2 * b][:, :])

            loop_tiles("in_b", RC, 2, put_x)
            dve.memset(SM(312), 0.0).then_inc(S("pad_done"), n.up(S("pad_done")))
            dve.wait_ge(S("pad_done"), n.own(S("pad_done")))
            for c in range(RC):
                dve.tensor_scalar(W(21 + c), xr[:, c, 0:T], V("convw", c), V("convb", c), ALU.mult, ALU.add)\
                    .then_inc(chain, n.up(chain))
                dve.wait_ge(chain, n.own(chain))
                for k in range(1, 4):
                    sig = S("conv_done") if (c, k) == (RC - 1, 3) else chain
                    dve.scalar_tensor_tensor(W(21 + c), xr[:, c, k:k + T], V("convw", k * RC + c), W(21 + c),
                        ALU.mult, ALU.add)\
                        .then_inc(sig, n.up(sig))
                    dve.wait_ge(sig, n.own(sig))

            def softplus_tail(e, s, q, p, width, rows):
                v = lambda at: SM(at, width)[rows]
                dve.tensor_scalar(v(s), v(e), 2.0, None, ALU.add).then_inc(chain, n.up(chain))
                dve.wait_ge(chain, n.own(chain))
                dve.reciprocal(v(s), v(s)).then_inc(chain, n.up(chain))
                dve.wait_ge(chain, n.own(chain))
                dve.tensor_tensor(v(s), v(e), v(s), ALU.mult).then_inc(chain, n.up(chain))
                dve.wait_ge(chain, n.own(chain))
                dve.tensor_tensor(v(q), v(s), v(s), ALU.mult).then_inc(chain, n.up(chain))
                dve.wait_ge(chain, n.own(chain))
                dve.tensor_scalar(v(p), v(q), 1.0 / 15, 1.0 / 13, ALU.mult, ALU.add).then_inc(chain, n.up(chain))
                dve.wait_ge(chain, n.own(chain))
                for d in (11, 9, 7, 5, 3, 1):
                    dve.tensor_tensor(v(p), v(p), v(q), ALU.mult).then_inc(chain, n.up(chain))
                    dve.wait_ge(chain, n.own(chain))
                    dve.tensor_scalar(v(p), v(p), 1.0 / d, None, ALU.add).then_inc(chain, n.up(chain))
                    dve.wait_ge(chain, n.own(chain))
                dve.scalar_tensor_tensor(v(p), v(p), 2.0, v(s), ALU.mult, ALU.mult).then_inc(chain, n.up(chain))
                dve.wait_ge(chain, n.own(chain))

            dve.wait_ge(S("lam_exp"), n.next(S("lam_exp")))
            allp = slice(0, P)
            softplus_tail(0, 10, 20, 30, RC, allp)
            dve.tensor_scalar(SM(10, RC), vec[:, VEC["lam"][0]:VEC["lam"][0] + RC], -1.0, 0.0, ALU.mult, ALU.max)\
                .then_inc(chain, n.up(chain))
            dve.wait_ge(chain, n.own(chain))
            dve.tensor_tensor(SM(30, RC), SM(30, RC), SM(10, RC), ALU.add).then_inc(chain, n.up(chain))
            dve.wait_ge(chain, n.own(chain))
            dve.tensor_scalar(SM(20, RC), SM(30, RC), 8.0, None, ALU.mult).then_inc(chain, n.up(chain))
            dve.wait_ge(chain, n.own(chain))
            dve.tensor_scalar(SM(30, RC), SM(30, RC), -8.0, None, ALU.mult)\
                .then_inc(S("softplus_ready"), n.up(S("softplus_ready")))
            dve.wait_ge(S("softplus_ready"), n.own(S("softplus_ready")))
            for c in range(RC):
                dve.wait_ge(evac_by["act"], handed_at["lru"]["act"] + 2 * c + 2)
                dve.tensor_tensor(W(c), W(c), W(21 + c), ALU.mult).then_inc(chain, n.up(chain))
                dve.wait_ge(chain, n.own(chain))
            for c in range(RC):
                dve.wait_ge(S("a_square"), n.next(S("a_square")))
                dve.scalar_tensor_tensor(W(41 + c), W(51 + c), 1.0, W(41 + c), ALU.add, ALU.mult)\
                    .then_inc(S("norm_square"), n.up(S("norm_square")))
            for c in range(RC):
                dve.wait_ge(S("lru_norm"), n.next(S("lru_norm")))
                dve.tensor_tensor(W(c), W(41 + c), W(c), ALU.mult).then_inc(chain, n.up(chain))
                dve.wait_ge(chain, n.own(chain))
                dve.tensor_tensor_scan(W(21 + c), W(31 + c), W(c), 0.0, ALU.mult, ALU.add)\
                    .then_inc(chain, n.up(chain))
                dve.wait_ge(chain, n.own(chain))
                sig = S("ya_ready") if c == RC - 1 else chain
                dve.tensor_tensor(W(11 + c), W(11 + c), W(21 + c), ALU.mult).then_inc(sig, n.up(sig))
                dve.wait_ge(sig, n.own(sig))
            dve.wait_ge(psum_for["dve"], n.next(psum_for["dve"]))
            dve.tensor_scalar(W(50), bank[4][:, :], -1.0 / D, None, ALU.mult).then_inc(evac, n.up(evac))
            dve.wait_ge(evac, n.own(evac))
            for c in range(8):
                dve.tensor_tensor(W(29 + c), W(29 + c), W(50), ALU.add).then_inc(S("v_centred"), n.up(S("v_centred")))
                dve.wait_ge(S("v_centred"), n.own(S("v_centred")))
            dve.wait_ge(S("v_rstd"), n.next(S("v_rstd")))
            for c in range(8):
                dve.scalar_tensor_tensor(W(29 + c), W(29 + c), V("lng2", c), W(45), ALU.mult, ALU.mult)\
                    .then_inc(chain, n.up(chain))
                dve.wait_ge(chain, n.own(chain))
                sig = S("v_normed") if c == 7 else chain
                dve.tensor_scalar(W(29 + c), W(29 + c), V("lnb2", c), None, ALU.add).then_inc(sig, n.up(sig))
                dve.wait_ge(sig, n.own(sig))
            dve.wait_ge(S("sgu_ready"), n.next(S("sgu_ready")))
            for g in range(8):
                dve.wait_ge(psum_for["dve"], n.next(psum_for["dve"]))
                bs = W(48, 2)[:, g * P:(g + 1) * P].unsqueeze(1).broadcast_to([P, NT, P])
                dve.tensor_tensor(W(50 + g % 2).rearrange("p (n t) -> p n t", n=NT), bank[4 + g % 2][:,
                    :].rearrange("p (n t) -> p n t", n=NT), bs, ALU.add)\
                    .then_inc(evac, n.up(evac))
                dve.wait_ge(evac, n.own(evac))
                sig = S("branches_ready") if g == 7 else chain
                dve.tensor_tensor(W(21 + g), W(21 + g), W(50 + g % 2), ALU.mult).then_inc(sig, n.up(sig))
                dve.wait_ge(sig, n.own(sig))
            merge("w_merge2", 2, 51, 37, 57)
            residual("w_out2", 4)
            norm_at[0] = 51
            norm("ffn2", xn, "xn_ready")
            squared_relu("up2", 0)
            residual("down2", 2)
            norm("fin2", xt, "x_ready")

            norm("mix3", xn, "xn_ready")
            r4 = slice(0, 4)
            dve.memset(W(23)[r4, :], 0.0).then_inc(chain, n.up(chain))
            dve.wait_ge(chain, n.own(chain))
            dve.wait_ge(S("lf_parts"), n.next(S("lf_parts")))
            dve.scalar_tensor_tensor(W(19)[r4, :], W(19)[r4, :], 0.0, W(20)[r4, :], ALU.min, ALU.subtract)\
                .then_inc(chain, n.up(chain))
            dve.wait_ge(chain, n.own(chain))
            dve.tensor_tensor_scan(W(20)[r4, :], C("ones", 0, 1)[r4].broadcast_to([4, T]), W(19)[r4, :], 0.0,
                ALU.mult, ALU.add)\
                .then_inc(chain, n.up(chain))
            dve.wait_ge(chain, n.own(chain))
            dve.tensor_tensor(W(21)[r4, :], W(18)[r4, :], W(20)[r4, :], ALU.subtract)\
                .then_inc(S("gates_ready"), n.up(S("gates_ready")))
            dve.wait_ge(S("gates_ready"), n.own(S("gates_ready")))
            dve.tensor_tensor_scan(W(22)[r4, :], W(21)[r4, :], W(23)[r4, :], 0.0, ALU.max, ALU.max)\
                .then_inc(chain, n.up(chain))
            dve.wait_ge(chain, n.own(chain))
            dve.tensor_tensor(W(24)[r4, :], W(20)[r4, :], W(22)[r4, :], ALU.add)\
                .then_inc(S("m_sum"), n.up(S("m_sum")))
            dve.wait_ge(S("m_sum"), n.own(S("m_sum")))
            dve.wait_ge(evac_by["act"], handed_at["c_turned"]["act"])
            for h in range(4):
                dve.wait_ge(psum_for["dve"], n.next(psum_for["dve"]))
                dve.tensor_copy(W(45), bank[5][:, :]).then_inc(evac, n.up(evac))
                dve.wait_ge(evac, n.own(evac))
                for s in range(NT):
                    dve.tensor_scalar(W(29 + s)[:, s * P:T], W(45)[:, s * P:T], SM(100 + 4 * s + h), 0.0,
                        ALU.subtract, ALU.max)\
                        .then_inc(S("exponent_ready"), n.up(S("exponent_ready")))
                for s in range(NT):
                    dve.wait_ge(S("exps3_ready"), n.next(S("exps3_ready")))
                    dve.wait_ge(psum_for["dve"], n.next(psum_for["dve"]))
                    dve.scalar_tensor_tensor(W(33 + s)[:, s * P:T], bank[6 + s % 2][:, s * P:T], float(P) ** (-0.5),
                        W(29 + s)[:, s * P:T], ALU.mult, ALU.mult)\
                        .then_inc(evac, n.up(evac))
                    dve.wait_ge(evac, n.own(evac))
                    dg = W(33 + s)[:, s * P:(s + 1) * P]
                    sig = S("weights_ready") if s == NT - 1 else chain
                    dve.tensor_tensor(dg, dg, C("incl"), ALU.mult).then_inc(sig, n.up(sig))
                    dve.wait_ge(sig, n.own(sig))
                dve.wait_ge(evac_by["act"], handed_at[f"floor{h}"]["act"])
                dve.wait_ge(psum_for["dve"], n.next(psum_for["dve"]))
                dve.tensor_copy(W(42), bank[5][:, :]).then_inc(evac, n.up(evac))
                dve.wait_ge(evac, n.own(evac))
                dve.scalar_tensor_tensor(W(42), W(42), -1.0, W(42), ALU.mult, ALU.max).then_inc(chain, n.up(chain))
                dve.wait_ge(chain, n.own(chain))
                dve.tensor_tensor(W(42), W(42), W(41), ALU.max).then_inc(chain, n.up(chain))
                dve.wait_ge(chain, n.own(chain))
                dve.reciprocal(W(42), W(42)).then_inc(chain, n.up(chain))
                dve.wait_ge(chain, n.own(chain))
                dve.wait_ge(psum_for["dve"], n.next(psum_for["dve"]))
                dve.tensor_tensor(W(43), bank[4][:, :], W(42), ALU.mult).then_inc(evac, n.up(evac))
                dve.wait_ge(evac, n.own(evac))
                dve.tensor_tensor(W(43), W(43), W(12 + h), ALU.mult).then_inc(S("h_ready"), n.up(S("h_ready")))
                dve.wait_ge(S("h_ready"), n.own(S("h_ready")))
                dve.wait_ge(S("h_rstd"), n.next(S("h_rstd")))
                sig = S("m_done") if h == 3 else chain
                dve.scalar_tensor_tensor(W(50 + h), W(43), V("hm", h), W(44), ALU.mult, ALU.mult)\
                    .then_inc(sig, n.up(sig))
                dve.wait_ge(sig, n.own(sig))

            dve.wait_ge(S("lf_parts"), n.next(S("lf_parts")))
            dve.scalar_tensor_tensor(W(18, 4), W(26, 4), 0.0, W(18, 4), ALU.min, ALU.subtract)\
                .then_inc(chain, n.up(chain))
            dve.wait_ge(chain, n.own(chain))
            for c in range(4):
                dve.tensor_tensor_scan(W(18 + c), C("ones", 0, 1).broadcast_to([P, T]), W(18 + c), 0.0, ALU.mult,
                    ALU.add)\
                    .then_inc(chain, n.up(chain))
                dve.wait_ge(chain, n.own(chain))
            halves = (256, 128, 64, 32, 16, 8, 4, 2, 1)
            todo = [(h, half) for h in range(4) for half in halves]
            diag = work[:, 32 * T:32 * T + 4 * 640].rearrange("p (s t) -> p s t", t=640)[:, :, 0:P]

            def differences(l):
                h, half = todo[l]
                b4 = W(18 + h).rearrange("p (n t) -> p n t", t=2 * half)
                dve.tensor_tensor(W(26 + l % 2).rearrange("p (n t) -> p n t", t=2 * half), b4, b4[:, :,
                    half - 1:half].broadcast_to([P, T // (2 * half), 2 * half]), ALU.subtract)\
                    .then_inc(S("exponent_ready"), n.up(S("exponent_ready")))

            def decayed(l):
                h, half = todo[l]
                dve.wait_ge(S("exps3_ready"), n.next(S("exps3_ready")))
                v = lambda i: W(i).rearrange("p (n s t) -> p n s t", s=2, t=half)
                dve.tensor_tensor(v(30 + l % 2)[:, :, 0, :], v(28 + l % 2)[:, :, 0, :], v(4 + h)[:, :, 0, :],
                    ALU.mult)\
                    .then_inc(chain, n.up(chain))
                dve.tensor_tensor(v(30 + l % 2)[:, :, 1, :], v(28 + l % 2)[:, :, 1, :], v(h)[:, :, 1, :], ALU.mult)\
                    .then_inc(S("level_ready"), n.up(S("level_ready")))

            def collect(b, half):
                dve.wait_ge(psum_for["dve"], n.next(psum_for["dve"]))
                b4 = bank[b][:, :].rearrange("p (s t) -> p s t", s=NT)
                if half == 256:
                    dve.tensor_copy(W3(32, 2)[:, :, 256:T], bank[b][:, :].rearrange("p (s t) -> p s t", s=2))\
                        .then_inc(evac, n.up(evac))
                    dve.wait_ge(evac, n.own(evac))
                elif half == 128:
                    o = work[:, 32 * T:36 * T].rearrange("p (s t) -> p s t", s=2)
                    dve.tensor_copy(o[:, 0, P:2 * P], bank[b][:, 0:P]).then_inc(chain, n.up(chain))
                    dve.wait_ge(chain, n.own(chain))
                    dve.tensor_copy(o[:, 1, 3 * P:4 * P], bank[b][:, P:2 * P]).then_inc(evac, n.up(evac))
                    dve.wait_ge(evac, n.own(evac))
                elif half == 64:
                    dve.tensor_tensor(diag, b4, C("level", 6 * P, P).unsqueeze(1).broadcast_to([P, NT, P]), ALU.mult)\
                        .then_inc(evac, n.up(evac))
                    dve.wait_ge(evac, n.own(evac))
                else:
                    m = C("level", (half.bit_length() - 1) * P, P) if half else ident
                    w3 = W(37).rearrange("p (s t) -> p s t", s=NT)
                    dve.tensor_tensor(w3, b4, m.unsqueeze(1).broadcast_to([P, NT, P]), ALU.mult)\
                        .then_inc(evac, n.up(evac))
                    dve.wait_ge(evac, n.own(evac))
                    sig = S("weights_ready") if half == 0 else chain
                    dve.tensor_tensor(diag, diag, w3, ALU.add).then_inc(sig, n.up(sig))
                    dve.wait_ge(sig, n.own(sig))

            differences(0)
            for l in range(len(todo)):
                h, half = todo[l]
                if l + 1 < len(todo):
                    differences(l + 1)
                decayed(l)
                if half != 256:
                    collect(4 + (l - 1) % 2, todo[l - 1][1])
                if half == 1:
                    collect(4 + l % 2, 1)
                    collect(4 + (l + 1) % 2, 0)
                    dve.wait_ge(S("h_rstd"), n.next(S("h_rstd")))
                    dve.scalar_tensor_tensor(W(54 + h), W(41), V("hl", h), W(43), ALU.mult, ALU.mult)\
                        .then_inc(chain, n.up(chain))
                    dve.wait_ge(chain, n.own(chain))
                    dve.tensor_tensor(W(54 + h), W(54 + h), W(12 + h), ALU.mult)\
                        .then_inc(S("h_used"), n.up(S("h_used")))
                    dve.wait_ge(S("h_used"), n.own(S("h_used")))

            dve.wait_ge(evac_by["act"], handed_at["gdn"]["act"])
            for c in range(12):
                dve.tensor_scalar(W(18 + c), W(c), V("conv3", 36 + c), None, ALU.mult).then_inc(chain, n.up(chain))
                dve.wait_ge(chain, n.own(chain))
                for k in (2, 1, 0):
                    sh = 3 - k
                    sig = S("conv3_done") if (c, k) == (11, 0) else chain
                    dve.scalar_tensor_tensor(W(18 + c)[:, sh:T], W(c)[:, 0:T - sh], V("conv3", 12 * k + c),
                        W(18 + c)[:, sh:T], ALU.mult, ALU.add)\
                        .then_inc(sig, n.up(sig))
                    dve.wait_ge(sig, n.own(sig))
            r = slice(32, 36)
            dve.wait_ge(S("lf_parts"), n.next(S("lf_parts")))
            dve.scalar_tensor_tensor(W(49)[r, :], W(48)[r, :], 0.0, W(49)[r, :], ALU.max, ALU.add)\
                .then_inc(chain, n.up(chain))
            dve.wait_ge(chain, n.own(chain))
            dve.tensor_scalar(W(49)[r, :], W(49)[r, :], SM(60)[r], -1.0, ALU.mult, ALU.mult)\
                .then_inc(chain, n.up(chain))
            dve.wait_ge(chain, n.own(chain))
            dve.tensor_tensor_scan(W(48)[r, :], C("reset")[r, :], W(49)[r, :], 0.0, ALU.mult, ALU.add)\
                .then_inc(S("decay_row"), n.up(S("decay_row")))
            dve.wait_ge(S("decay_row"), n.own(S("decay_row")))
            for c in range(8):
                dve.wait_ge(S("qk_rstd"), n.next(S("qk_rstd")))
                if c < 4:
                    dve.scalar_tensor_tensor(W(18 + c), W(18 + c), float(P) ** (-0.5), W(c), ALU.mult, ALU.mult)\
                        .then_inc(chain, n.up(chain))
                else:
                    dve.tensor_tensor(W(18 + c), W(18 + c), W(c), ALU.mult).then_inc(chain, n.up(chain))
                    dve.wait_ge(chain, n.own(chain))
            dve.wait_ge(psum_for["dve"], n.next(psum_for["dve"]))
            dve.tensor_copy(SM(100, 16), bank[4][:, 0:16]).then_inc(evac, n.up(evac))
            dve.wait_ge(evac, n.own(evac))
            kq = W(0, 8).rearrange("p (h n s t) -> p h n s t", h=4, n=NT, s=2)
            v3 = lambda i: W(i).rearrange("p (n t) -> p n t", n=NT)
            for h in range(4):
                dve.wait_ge(psum_for["dve"], n.next(psum_for["dve"]))
                dve.tensor_copy(W(42 + h), bank[5][:, :]).then_inc(evac, n.up(evac))
                dve.wait_ge(psum_for["dve"], n.next(psum_for["dve"]))
                dve.tensor_copy(W(8 + h), bank[6 + h % 2][:, :]).then_inc(evac, n.up(evac))
                dve.wait_ge(evac, n.own(evac))
                dve.tensor_tensor(kq[:, h, :, 0, :], v3(22 + h), v3(8 + h), ALU.mult).then_inc(chain, n.up(chain))
                dve.tensor_copy(kq[:, h, :, 1, :], v3(18 + h)).then_inc(chain, n.up(chain))
                dve.tensor_tensor(W(26 + h), W(26 + h), W(8 + h), ALU.mult).then_inc(chain, n.up(chain))
                dve.wait_ge(chain, n.own(chain))
            for h in range(4):
                dve.tensor_tensor(v3(46 + h), v3(42 + h)[:, :, 127:128].broadcast_to([P, NT, P]), v3(42 + h),
                    ALU.subtract)\
                    .then_inc(chain, n.up(chain))
                for ch in range(NT):
                    cs = slice(ch * P, (ch + 1) * P)
                    sig = S("b_rows") if (h, ch) == (3, 3) else chain
                    dve.tensor_scalar(W(38 + h)[:, cs], W(42 + h)[:, cs], SM(100 + 4 * ch + h), 0.0, ALU.subtract,
                        ALU.min)\
                        .then_inc(sig, n.up(sig))
            dve.wait_ge(S("decays_ready"), n.next(S("decays_ready")))
            for h in range(4):
                dve.tensor_tensor(v3(8 + h), kq[:, h, :, 0, :], v3(42 + h), ALU.mult).then_inc(chain, n.up(chain))
                dve.tensor_tensor(W(30 + h), W(18 + h), W(42 + h), ALU.mult).then_inc(chain, n.up(chain))
                dve.tensor_tensor(W(34 + h), W(22 + h), W(46 + h), ALU.mult).then_inc(chain, n.up(chain))
            dve.tensor_copy(SM(120, 16).rearrange("p (h n) -> p h n", h=4), W(42,
                4).rearrange("p (h n t) -> p h n t", h=4, n=NT)[:, :, :, 127])\
                .then_inc(S("operands_ready"), n.up(S("operands_ready")))
            dve.wait_ge(S("operands_ready"), n.own(S("operands_ready")))
            mats = W(42, 8).rearrange("p (h n s t) -> p h n s t", h=4, n=NT, s=2)
            m2 = C("strict", 0, 2 * P).rearrange("p (s t) -> p s t", s=2)
            for h in range(4):
                for ch in range(NT):
                    m = h * NT + ch
                    dve.wait_ge(psum_for["dve"], n.next(psum_for["dve"]))
                    dve.tensor_tensor(mats[:, h, ch], bank[6 + m % 2][:, 0:2 * P].rearrange("p (s t) -> p s t", s=2),
                        m2, ALU.mult)\
                        .then_inc(evac, n.up(evac))
                    dve.wait_ge(evac, n.own(evac))
                    dve.tensor_tensor(mats[:, h, ch], mats[:, h, ch], W(38 + h)[:,
                        ch * P:(ch + 1) * P].unsqueeze(1).broadcast_to([P, 2, P]), ALU.mult)\
                        .then_inc(chain, n.up(chain))
                    dve.wait_ge(chain, n.own(chain))
            for ch in range(NT):
                inverse_start(mats[:, :, ch, 0, :], W(22 + ch).rearrange("p (h t) -> p h t", h=4), 4)
                inverse_levels(lambda hf: W(26), lambda hf, ch=ch: W(22 + ch), 1)
            for ch in range(NT):
                if ch:
                    dve.wait_ge(psum_for["dve"], n.next(psum_for["dve"]))
                    dve.tensor_tensor(W(39), W(34 + ch), bank[4][:, :], ALU.subtract).then_inc(evac, n.up(evac))
                    dve.wait_ge(evac, n.own(evac))
                if ch < NT - 1:
                    dve.wait_ge(psum_for["dve"], n.next(psum_for["dve"]))
                    if ch == 0:
                        dve.tensor_copy(W(41), bank[7][:, :]).then_inc(evac, n.up(evac))
                        dve.wait_ge(evac, n.own(evac))
                    else:
                        for h in range(4):
                            hs = slice(h * P, (h + 1) * P)
                            sig = evac if h == 3 else chain
                            dve.scalar_tensor_tensor(W(41)[:, hs], W(41)[:, hs], SM(120 + 4 * h + ch), bank[7][:,
                                hs], ALU.mult, ALU.add)\
                                .then_inc(sig, n.up(sig))
                            dve.wait_ge(sig, n.own(sig))
            for c in range(4):
                dve.wait_ge(S("y_rstd"), n.next(S("y_rstd")))
                dve.scalar_tensor_tensor(W(58 + c), W(4 + c), V("hd", c), W(c), ALU.mult, ALU.mult)\
                    .then_inc(chain, n.up(chain))
                dve.wait_ge(chain, n.own(chain))
                sig = S("branches_ready") if c == 3 else chain
                dve.tensor_tensor(W(58 + c), W(58 + c), W(12 + c), ALU.mult).then_inc(sig, n.up(sig))
                dve.wait_ge(sig, n.own(sig))
            merge("w_merge3", 3, 26, 18, 32)
            residual("w_out3", 4)
            norm_at[0] = 26
            norm("ffn3", xn, "xn_ready")
            squared_relu("up3", 0)
            residual("down3", 2)
            norm_at[0] = 51
            norm("fin3", xt, "result_ready")

        @block.gpsimd
        def _(pool):
            n = Count()
            chain = S("pool_chain")

            def masked_levels(at, am, heads):
                pool.wait_ge(S("inverse_start"), n.next(S("inverse_start")))
                for lv in range(1, 7):
                    if lv >= 3:
                        pool.wait_ge(S("level_begun"), n.next(S("level_begun"), 2 if lv == 3 else 1))
                    pool.tensor_tensor(am(lv), at, C("level", lv * P, P).unsqueeze(1).broadcast_to([P, heads, P]),
                        ALU.mult)\
                        .then_inc(S("level_masked"), n.up(S("level_masked")))
                pool.wait_ge(S("level_begun"), n.next(S("level_begun")))

            pool.dma_start(work[0:BUCKETS, 59 * T:59 * T + NREL], a["buckets"]).then_inc(S("bias_loads"), 16)
            pool.dma_start(W(61)[0:BUCKETS, 0:8], a["rel_bias"]).then_inc(S("bias_loads"), 16)
            pool.wait_ge(S("loads_ready"), n.next(S("loads_ready"), 48))
            mask_at = {1: 52 * T, 2: 52 * T + 256, 3: 52 * T + 640}
            pool.wait_ge(evac_by["act"], handed_at["flipped"]["act"])
            g = 0
            for i in range(NT):
                w = (i + 1) * P
                if i == 0:
                    pool.wait_ge(S("mask_ready"), n.next(S("mask_ready"), 3))
                for h in range(8):
                    if g >= 2:
                        pool.wait_ge(evac_by["dve"], handed_at["attention"]["dve"] + g - 1)
                    m = C("caus") if i == 0 else work[:, mask_at[i]:mask_at[i] + w]
                    pool.tensor_tensor(W(55 + g % 2)[:, 0:w], W(40 + h)[:, 3 * P - i * P:3 * P - i * P + w], m,
                        ALU.add)\
                        .then_inc(S("bias_ready"), n.up(S("bias_ready")))
                    g += 1
            pool.wait_ge(evac_by["act"], handed_at["attention"]["act"])
            for k, t in enumerate(list(range(16, 30)) + [31]):
                if k >= 2:
                    pool.wait_ge(S("shift_done"), n.next(S("shift_done")))
                o = W(38 + k % 2)
                pool.tensor_scalar(o[:, 0:1], W(t)[:, 0:1], -1.0, None, ALU.mult).then_inc(chain, n.up(chain))
                pool.tensor_tensor(o[:, 1:T], W(t)[:, 0:T - 1], W(t)[:, 1:T], ALU.subtract)\
                    .then_inc(S("shift_diff"), n.up(S("shift_diff")))
            pool.wait_ge(evac_by["act"], handed_at["rwkv"]["act"])
            pool.dma_start(W(59), a["w2a2"]).then_inc(S("lora_loads"), 16)
            pool.dma_start(W(60), a["g2a"]).then_inc(S("lora_loads"), 16)
            pool.dma_start(W(61)[0:32, :], a["g2b"]).then_inc(S("lora_loads"), 16)
            pool.wait_ge(S("kb_ready"), n.next(S("kb_ready")))
            pool.wait_ge(S("decays_ready"), n.next(S("decays_ready")))
            pool.tensor_tensor(W(8, 4), W(52, 4), W(48, 4), ALU.mult).then_inc(chain, n.up(chain))
            pool.tensor_tensor(W(12, 4), W(20, 4), W(48, 4), ALU.mult)\
                .then_inc(S("operands_ready_2"), n.up(S("operands_ready_2")))
            pool.wait_ge(S("operands_ready_2"), n.own(S("operands_ready_2")))
            for ch in range(NT):
                masked_levels(W3(40, 8)[:, :, 0:P], lambda lv: W(54 + 2 * (lv % 2), 2).rearrange("p (h t) -> p h t", h=8), 8)
            pool.wait_ge(S("x_ready"), n.next(S("x_ready"), 2))
            pool.memset(W(51, 10), 0.0).then_inc(chain, n.up(chain))
            pool.wait_ge(chain, n.own(chain))
            for w, name in ((51, "lru_a"), (56, "lru_x")):
                o = W(w, 5)[:, 0:RC * P].rearrange("p (c j) -> p c j", j=P)
                for e in range(2):
                    rows = slice(e * HD, (e + 1) * HD)
                    pool.dma_start(o[rows, :, rows], a[name][rows, :, :]).then_inc(S("gate_loads"), 16)
            pool.wait_ge(S("ya_ready"), n.next(S("ya_ready")))
            pool.dma_start(W(46, 2), a["sgu_w"]).then_inc(S("sgu_loads"), 16)
            pool.dma_start(W(48, 2), a["sgu_b"].partition_broadcast(P)).then_inc(S("sgu_loads"), 16)
            pool.wait_ge(S("sgu_loads"), n.next(S("sgu_loads"), 32))
            pool.memset(W(46, 2).rearrange("p (g t) -> p g t", g=8)[64:P, :, 0:64], 0.0)\
                .then_inc(S("sgu_ready"), n.up(S("sgu_ready")))
            pool.wait_ge(S("sgu_ready"), n.own(S("sgu_ready")))
            pool.wait_ge(S("m_done"), n.next(S("m_done")))
            pool.dma_start(W(40)[64:80, :], a["gla_lr"]).then_inc(S("gla_load"), 16)
            mats = W(42, 8).rearrange("p (h n s t) -> p h n s t", h=4, n=NT, s=2)
            for ch in range(NT):
                masked_levels(mats[:, :, ch, 0, :], lambda lv: W(28 + lv % 2).rearrange("p (h t) -> p h t", h=4), 4)


def _tile(w, cols, width=P):
    blocks = w[:, cols].reshape(-1, P, width)
    if width < P:
        blocks = np.concatenate([blocks, np.zeros((blocks.shape[0], P, P - width), np.float32)], axis=2)
    return blocks.transpose(1, 0, 2).reshape(P, -1)


def _slabs(tiles, per):
    n = len(tiles) // per
    return np.stack([np.concatenate(tiles[i * per:(i + 1) * per], axis=1) for i in range(n)])


def _plain(w, per=2, start=0, count=None):
    count = w.shape[1] // P if count is None else count
    return _slabs([_tile(w, slice(start + i * P, start + (i + 1) * P)) for i in range(count)], per)


def _halves(w):
    out = []
    for i in range(w.shape[1] // P):
        t = _tile(w, slice(i * P, (i + 1) * P))
        out += [t[:, :t.shape[1] // 2], t[:, t.shape[1] // 2:]]
    return np.stack(out)


def _merge(w_in, gates, branches):
    return np.stack([np.concatenate([_tile(w_in, slice(g + j * P, g + (j + 1) * P)) for g in gates] +
                                    [_tile(b, slice(j * P, (j + 1) * P)) for b in branches], axis=1)
                     for j in range(DC)])


def _odd(w, parts):
    t = np.zeros((w.shape[0], P), np.float32)
    for at, c, k in parts:
        t[:, at:at + k] = w[:, c:c + k]
    return _tile(t, slice(0, P))


def arrays_of(i):
    A, R = {}, {k: np.asarray(v) for k, v in i.items()}
    A["x"] = R["x"][0].T.reshape(DC, P, T).transpose(1, 0, 2)
    vec = np.zeros((P, NVEC), np.float32)

    def put(name, v, k=0):
        v = np.asarray(v).reshape(-1, P).T
        vec[:, VEC[name][0] + k:VEC[name][0] + k + v.shape[1]] = v

    def rows(name, v, at):
        vec[at:at + v.shape[0], VEC[name][0]] = v

    w = R["w_in"][0]
    rk = 4 * 512 + 64 + 8
    gate = rk + 3 * 512 + 64 + 64 + 160
    tiles = [_tile(w, slice(c * P, (c + 1) * P)) for c in range(16)]
    tiles += [_tile(w, slice(rk + c * P, rk + (c + 1) * P)) for c in range(14)]
    tiles += [_odd(w, [(0, 2048, 64), (64, 2048, 64)]), _odd(w, [(0, rk + 14 * P, 32), (32, 2112, 8)])]
    A["w_in_a"] = _slabs(tiles, 2)
    A["w_merge1"] = _merge(w, [gate, gate + D], [R["w_branch_attn"][0], R["w_branch_rwkv"][0]])
    A["w_out1"] = _plain(R["w_out"][0])
    gu = R["w_gate_up"][0]
    A["w_gu"] = _slabs([_tile(gu, slice((s * FFN1 + c) * P, (s * FFN1 + c + 1) * P)) for c in range(FFN1) for s in range(2)], 2)
    A["w_down1"] = _halves(R["w_down"][0])
    put("mix1", R["mix_norm"])
    put("qg", np.concatenate([R["attn_q_norm"][0]] * 2))
    put("kg", np.concatenate([R["attn_k_norm"][0]] * 2))
    mu = R["rwkv_mu"][0]
    put("mu", mu[:14 * P])
    rows_at = VEC["mu"][0] + 15
    vec[0:32, rows_at] = mu[14 * P:14 * P + 32]
    for name, key in (("w0", "rwkv_w0"), ("a0", "rwkv_a0"), ("kk", "rwkv_k_k"), ("ka", "rwkv_k_a"), ("rk", "rwkv_r_k"),
                      ("lnw", "rwkv_ln_w"), ("lnb", "rwkv_ln_b"), ("ffn1", "ffn_norm"), ("mix2", "norm_mix_g_2"),
                      ("convb", "conv_b_2"), ("convw", "conv_w_2"), ("ba", "lru_b_a_2"), ("bx", "lru_b_x_2"),
                      ("lam", "lru_lambda_2"), ("lng2", "sgu_ln_g_2"), ("lnb2", "sgu_ln_b_2"), ("ffn2", "norm_ffn_g_2"),
                      ("fin2", "final_norm_g_2"), ("mix3", "g_norm_mix_3"), ("bgla", "b_gla_3"), ("conv3", "conv_gdn_3"),
                      ("hm", "g_head_mlstm_3"), ("hl", "g_head_gla_3"), ("hd", "g_head_gdn_3"), ("ffn3", "g_norm_mlp_3"),
                      ("fin3", "g_final_3")):
        put(name, R[key])
    rows("bi", R["b_if_3"][0, 0:4], 0)
    rows("bf", R["b_if_3"][0, 4:8], 0)
    rows("alog", R["a_log_3"][0], 32)
    rows("dtb", R["dt_bias_3"][0], 32)
    A["vec"] = vec
    A["cst"] = constants()
    A["buckets"] = bucket_table()
    A["rel_bias"] = R["rel_bias"]
    A["w2a2"] = np.concatenate([R["rwkv_w2"][0], R["rwkv_a2"][0]], axis=0)
    A["g2a"], A["g2b"] = R["rwkv_g2"][0, :P], R["rwkv_g2"][0, P:]
    w = R["w_in_2"][0]
    A["w_in_b"] = _slabs([_tile(w, slice((s * RC + c) * P, (s * RC + c + 1) * P)) for c in range(RC) for s in range(2)], 2)
    u = 2 * RC * P
    A["w_uv"] = _plain(w, 2, u, 16)
    A["w_merge2"] = _merge(w, [u + 2 * D, u + 3 * D], [R["w_branch_a_2"][0], R["w_branch_b_2"][0]])
    A["w_out2"] = _plain(R["w_out_2"][0])
    A["w_up2"] = _plain(R["w_up_2"][0])
    A["w_down2"] = _halves(R["w_down_2"][0])
    for name, key in (("lru_a", "lru_w_a_2"), ("lru_x", "lru_w_x_2")):
        A[name] = R[key][0].reshape(RC, P, HD).transpose(1, 0, 2)
    A["sgu_w"] = R["sgu_w_s_2"][0].transpose(2, 0, 1).reshape(P, 8 * P)
    A["sgu_b"] = R["sgu_b_s_2"][0].reshape(8 * P)
    w = R["w_in_3"][0]
    W_ = 512
    m0, l0 = 0, 4 * W_ + 8
    d0 = l0 + 4 * W_ + 16
    g0 = d0 + 4 * W_ + 8
    odd = [_odd(w, [(0, 4 * W_, 4), (32, d0 + 4 * W_ + 4, 4), (64, l0 + 4 * W_, 16)]),
           _odd(w, [(0, 4 * W_ + 4, 4), (32, d0 + 4 * W_, 4)])]
    A["w_in_m"] = _slabs([_tile(w, slice(c * P, (c + 1) * P)) for c in range(16)] + odd, 2)
    A["w_in_l"] = _plain(w, 2, l0, 16)
    A["w_in_d"] = _plain(w, 2, d0, 16)
    A["w_merge3"] = _merge(w, [g0, g0 + D, g0 + 2 * D], [R["w_up_3"][0, b] for b in range(3)])
    A["w_out3"] = _plain(R["w_out_3"][0])
    A["w_up3"] = _plain(R["w_mlp_in_3"][0])
    A["w_down3"] = _halves(R["w_mlp_out_3"][0])
    A["gla_lr"] = R["w_gla_lr_3"][0]
    return {k: np.ascontiguousarray(v, dtype=np.float32) for k, v in A.items()}


def build(nc, shapes):
    a = {k: nc.dram_tensor(f"in_{k}", s, F32, kind="ExternalInput").ap() for k, s in shapes.items()}
    a["scratch"] = nc.dram_tensor("bias_scratch", (8, NREL), F32, kind="Internal").ap()
    out = nc.dram_tensor("out_dram", (P, DC, T), F32, kind="ExternalOutput").ap()
    program(nc, a, out)


def kernel(**inputs):
    import concourse.bacc as bacc
    from concourse.bass_utils import run_bass_kernel_spmd

    nc = bacc.Bacc("TRN2", target_bir_lowering=False, num_devices=1)
    arrays = arrays_of(inputs)
    build(nc, {k: v.shape for k, v in arrays.items()})
    r = run_bass_kernel_spmd(nc, [{f"in_{k}": v for k, v in arrays.items()}], core_ids=[0])
    y = r.results[0]["out_dram"]
    return y.transpose(1, 0, 2).reshape(D, T).T.reshape(1, T, D)
```

```python
from contextlib import ExitStack

import numpy as np

import concourse.bass as bass
from concourse import mybir

F32 = mybir.dt.float32
F32R = mybir.dt.float32r
ALU = mybir.AluOpType
ACT = mybir.ActivationFunctionType

P = 128
T = 512
NT = T // P
D = 1024
DC = D // P
HD = 64
RING = 4
SLAB = DC
LOOK = 2
NW = 62
GROUP = 8
TOPK = min(256, T // 4)
NEG = -1.0e30
PICKED = -3.0e38
EXPM05 = float(np.exp(-0.5))
LN2 = float(np.log(2.0))
FFN1 = ((8 * D + 3 * 256 - 1) // (3 * 256)) * 256 // P
FFN2 = 4 * D // P
PARTS1 = [8, 8, 6]
PARTS2 = [8, 8, 8, 8]
HIDDEN = 8
RC = 1280 // P
MERGE_SLABS = {"w_merge1": [8], "w_merge2": [6, 6, 6], "w_merge3": [6, 6]}
GATES = {1: 2, 2: 2, 3: 3}
EARLY_2, EARLY_M, EARLY_L = 6, 3, 6
STAGING = 3
NREL = T + P
BUCKETS = 32

VEC = {}
_at = 0
for _name, _n in [
    ("mix1", DC), ("qg", 1), ("kg", 1), ("mu", 16), ("w0", 4), ("a0", 4), ("kk", 4), ("ka", 4), ("rk", 4),
    ("lnw", 4), ("lnb", 4), ("ffn1", DC),
    ("mix2", DC), ("convb", RC), ("convw", 4 * RC), ("ba", RC), ("bx", RC), ("lam", RC), ("lng2", DC), ("lnb2", DC),
    ("ffn2", DC), ("fin2", DC),
    ("mix3", DC), ("bi", 1), ("bf", 1), ("bgla", 4), ("conv3", 48), ("alog", 1), ("dtb", 1), ("hm", 4), ("hl", 4),
    ("hd", 4), ("ffn3", DC), ("fin3", DC),
]:
    VEC[_name] = (_at, _n)
    _at += _n
NVEC = _at

CST = {}
_at = 0
for _name, _n in [("ident", P), ("ones", P), ("pair", P), ("flip", P), ("level", 7 * P), ("strict", P),
                  ("incl", P), ("caus", P), ("reset", T), ("sel", 4 * P)]:
    CST[_name] = (_at, _n)
    _at += _n
NCST = _at


def constants():
    c = np.zeros((P, NCST), np.float32)
    i = np.arange(P)

    def put(name, a):
        c[:, CST[name][0]:CST[name][0] + a.shape[1]] = a

    put("ident", np.eye(P))
    put("ones", np.ones((P, P)))
    put("pair", (i[:, None] // HD == i[None] // HD) * 1.0)
    put("flip", (i[:, None] + i[None] == P - 1) * 1.0)
    for n in range(7):
        h = 1 << n
        m = (i[:, None] // (2 * h) == i[None] // (2 * h)) & (i[:, None] % (2 * h) < h) & (i[None] % (2 * h) >= h)
        c[:, CST["level"][0] + n * P:CST["level"][0] + (n + 1) * P] = m
    put("strict", (i[:, None] < i[None]) * 1.0)
    put("incl", (i[:, None] <= i[None]) * 1.0)
    put("caus", np.where(i[None] <= i[:, None], 0.0, NEG))
    put("reset", np.broadcast_to((np.arange(T) % P != 0) * 1.0, (P, T)))
    sel = np.zeros((P, 4, P))
    for base in (0, 32):
        for h in range(4):
            sel[base + h, h] = 1.0
    put("sel", sel.reshape(P, 4 * P))
    return c


def bucket_table():
    d = np.maximum(T - 1 - np.arange(NREL), 0)
    half = BUCKETS // 2
    ratio = (np.log(np.maximum(d, 1).astype(np.float32) / half) / np.log(128 / half)).astype(np.float32)
    b = np.where(d < half, d, np.minimum(half + (ratio * half).astype(np.int32), BUCKETS - 1))
    return (np.arange(BUCKETS)[:, None] == b[None]).astype(np.float32)


class Count:

    def __init__(self):
        self.made, self.seen = {}, {}

    def up(self, sem):
        self.made[sem.name] = self.made.get(sem.name, 0) + 1
        return 1

    def own(self, sem):
        return self.made[sem.name]

    def next(self, sem, k=1):
        self.seen[sem.name] = self.seen.get(sem.name, 0) + k
        return self.seen[sem.name]


def program(nc, a, out):
    ctx = ExitStack()
    with ctx:
        def twice(name, shape):
            at = nc.sbuf_base
            plain = ctx.enter_context(nc.sbuf_tensor(name, shape, F32))
            return plain, nc.alloc_sbuf_tensor_at(f"{name}_r", shape, F32R, offset=at)

        xh = ctx.enter_context(nc.sbuf_tensor("xh", [P, DC, T], F32R))
        x_raw, xl = twice("x_raw", [P, DC, T])
        slab, slab_low = twice("slab", [P, RING, SLAB * P])
        slab_high = ctx.enter_context(nc.sbuf_tensor("slab_high", [P, RING, SLAB * P], F32R))
        staging = ctx.enter_context(nc.sbuf_tensor("staging", [P, STAGING, T], F32))
        cst = ctx.enter_context(nc.sbuf_tensor("cst", [P, NCST], F32))
        vec = ctx.enter_context(nc.sbuf_tensor("vec", [P, NVEC], F32))
        small = ctx.enter_context(nc.sbuf_tensor("small", [P, 320], F32))
        work_at = nc.sbuf_base
        work = ctx.enter_context(nc.sbuf_tensor("work", [P, NW * T], F32))
        work_r = [nc.alloc_sbuf_tensor_at(f"work_r{g}", [P, min(GROUP, NW - g * GROUP) * T], F32R,
                                          offset=work_at + g * GROUP * T * 4) for g in range(-(-NW // GROUP))]
        bank = [ctx.enter_context(nc.psum_tensor(f"bank{i}", [P, T], F32)) for i in range(8)]
        sems = {}

        def S(name):
            if name not in sems:
                sems[name] = ctx.enter_context(nc.semaphore(name))
            return sems[name]

        psum_for = {"act": S("psum_for_act"), "dve": S("psum_for_dve")}
        evac_by = {"act": S("evac_by_act"), "dve": S("evac_by_dve")}
        landed = [S(f"slab_landed_{i}") for i in range(RING)]

        def W(i, n=1):
            return work[:, i * T:(i + n) * T]

        def W3(i, n):
            return W(i, n).rearrange("p (c t) -> p c t", c=n)

        def WR(i, n=1):
            g, k = divmod(i, GROUP)
            assert k + n <= GROUP
            return work_r[g][:, k * T:(k + n) * T]

        def plain(ap):
            return ap.bitcast(F32)

        def X(c):
            return W(c)

        def C(name, i=0, n=None):
            at, w = CST[name]
            return cst[:, at + i:at + i + (n or w)]

        def V(name, i=0):
            at = VEC[name][0] + i
            return vec[:, at:at + 1]

        def SM(i, n=1):
            return small[:, i:i + n]

        def dyn(ap3, i):
            if isinstance(i, int):
                return ap3[:, i, :]
            return ap3[:, bass.ds(i, 1), :].rearrange("p a t -> p (a t)")

        ident = C("ident")
        ones = C("ones")
        pair = C("pair")

        def feed_forward(up, n_up, down, parts):
            ups = [(up, n_up * sum(parts[:p]), n_up * k, DC) for p, k in enumerate(parts)]
            downs = [(f"{down}_{p}", 0, DC, k) for p, k in enumerate(parts)]
            return [ups[0]] + [x for p in range(1, len(parts)) for x in (ups[p], downs[p - 1])] + [downs[-1]]

        stream = [("w_in_a", 0, 32, DC), ("w_gates1", 0, 16, DC), ("w_merge1", 0, 8, 0), ("w_out1", 0, DC, DC)]
        stream += feed_forward("w_gu", 2, "w_down1", PARTS1)
        stream += [("w_in_b", 0, 2 * RC, DC), ("w_gates2", 0, EARLY_2, DC), ("w_uv", 0, 16, DC),
                   ("w_gates2", EARLY_2, 16 - EARLY_2, DC), ("w_merge2", 0, 24, 0), ("w_out2", 0, DC, DC)]
        stream += feed_forward("w_up2", 1, "w_down2", PARTS2)
        stream += [("w_in_m", 0, 18, DC), ("w_gates3", 0, EARLY_M, DC), ("w_in_l", 0, 16, DC),
                   ("w_gates3", EARLY_M, EARLY_L, DC), ("w_in_d", 0, 16, DC),
                   ("w_gates3", EARLY_M + EARLY_L, 24 - EARLY_M - EARLY_L, DC), ("w_merge3", 0, 16, 0),
                   ("w_out3", 0, DC, DC)]
        stream += feed_forward("w_up3", 1, "w_down3", PARTS2)
        total_slabs = sum(x[2] for x in stream)
        merge_slabs = MERGE_SLABS

        def ffn_stages(name, parts):
            order = [("up", 0)] + [x for p in range(1, len(parts)) for x in (("up", p), ("down", p - 1))]
            order += [("down", len(parts) - 1)]
            return [(f"{kind}{name}_{p}", p, kind == "up") for kind, p in order]

        def hidden_at(p):
            return HIDDEN + 16 * (p % 2), HIDDEN + 16 * (p % 2) + 8

        def branch_bank(nb, j, g):
            return (nb * j + g) % 4

        def gate_place(t):
            n = 0
            for block_no, nb in GATES.items():
                if t < n + nb * DC:
                    j, g = divmod(t - n, nb)
                    return a[f"gates_{block_no}"][j, :, g * T:(g + 1) * T]
                n += nb * DC

        IN_ATTENTION, IN_RWKV, IN_MLSTM, IN_GLA, IN_LEVEL, IN_STATE = 3, 1, 6, 1, 3, 4
        AFTER_ATTENTION = 12
        IN_GDN = (16, 32)
        shift_tiles = list(range(16, 30)) + [31]
        TOPK_STEPS = 6
        SHIFT_FROM = 16
        handed_at = {}

        block = ctx.enter_context(nc.Block())

        @block.tensor
        def _(pe):
            n = Count()
            handed = {"act": 0, "dve": 0}
            last = [None] * 8
            slabs = [0]
            begun = S("slab_begun")

            def hand(b, who):
                handed[who] += 1
                last[b] = (evac_by[who], handed[who])
                return 1

            def mark(stage):
                handed_at[stage] = dict(handed)

            def product(b, weights, moving, start, stop):
                wh, wl = weights
                mh, ml = moving
                first = pe.matmul(bank[b][:, :], wh, mh, start=start, stop=False)
                pe.matmul(bank[b][:, :], wh, ml, start=False, stop=False)
                end = pe.matmul(bank[b][:, :], wl, mh, start=False, stop=stop)
                return first, end

            def dense(stage, n_slabs, kc, moving, whos, ready):
                handed_at[stage] = dict(handed)
                who_of = [whos[p % len(whos)] for p in range(RING)]
                each = {w: who_of.count(w) for w in ("act", "dve")}
                rank = [who_of[:p].count(who_of[p]) for p in range(RING)]
                base, hand0 = slabs[0], dict(handed)

                def some(i, count, first):
                    for j in range(count):
                        slot = (base + j) % RING
                        pe.wait_ge(S("slab_split"), i * RING + (base + j + 1))
                        if first:
                            if last[j]:
                                pe.wait_ge(*last[j])
                        else:
                            pe.wait_ge(evac_by[who_of[j]], hand0[who_of[j]] + rank[j] + 1 +
                                       each[who_of[j]] * (i - 1))
                        for k in range(kc):
                            if first and j == 0 and ready is not None:
                                pe.wait_ge(ready, n.next(ready))
                            at = slice(k * P, (k + 1) * P)
                            one, ins = product(j, (slab_high[:, slot, at], slab_low[:, slot, at]), moving(k),
                                               k == 0, k == kc - 1)
                            if k == 0:
                                one.then_inc(begun, 1)
                        ins.then_inc(psum_for[who_of[j]], 1)

                whole, rest = divmod(n_slabs, RING)
                some(0, RING, True)
                if whole > 1:
                    with pe.Fori(1, whole) as i:
                        some(i, RING, False)
                if rest:
                    some(whole, rest, False)
                slabs[0] += n_slabs
                for g in range(n_slabs):
                    w = who_of[g % RING]
                    handed[w] += 1
                    last[g % RING] = (evac_by[w], handed[w])

            early = [0]
            early_blocks = [None]

            def early_gates(products):
                for _ in range(products):
                    t, k = divmod(early[0], DC)
                    b = t % 4
                    if k == 0:
                        slot = slabs[0] % RING
                        slabs[0] += 1
                        pe.wait_ge(S("slab_split"), slabs[0])
                        if last[b]:
                            pe.wait_ge(*last[b])
                        early_blocks[0] = slot
                    slot, at = early_blocks[0], slice(k * P, (k + 1) * P)
                    one, ins = product(b, (slab_high[:, slot, at], slab_low[:, slot, at]), (xh[:, k, :], xl[:, k, :]),
                                       k == 0, k == DC - 1)
                    if k == 0:
                        one.then_inc(begun, 1)
                    if k == DC - 1:
                        ins.then_inc(S("gate_done"), 1)
                        last[b] = (S("gate_out"), t + 1)
                    early[0] += 1

            def merge(name, nb, high, low, n_tiles):
                layout = merge_slabs[name]
                mark(name)
                for j in range(DC):
                    at, left, c = -1, 0, 0
                    for g, width in enumerate(n_tiles):
                        b = branch_bank(nb, j, g)
                        if last[b]:
                            pe.wait_ge(*last[b])
                        for k in range(width):
                            fresh = left == 0
                            if fresh:
                                at += 1
                                left, pos = layout[at], 0
                                slot = slabs[0] % RING
                                slabs[0] += 1
                                pe.wait_ge(S("slab_split"), slabs[0])
                            if j == 0:
                                pe.wait_ge(S("branch_split"), n.next(S("branch_split")))
                            col = slice(pos * P, (pos + 1) * P)
                            one, ins = product(b, (slab_high[:, slot, col], slab_low[:, slot, col]),
                                               (WR(high + c), WR(low + c)), k == 0, k == width - 1)
                            pos, left, c = pos + 1, left - 1, c + 1
                            if fresh:
                                one.then_inc(begun, 1)
                        ins.then_inc(psum_for["dve"], hand(b, "dve"))

            def sum_tiles(tiles, b, who, lhsT, ready=None):
                if last[b]:
                    pe.wait_ge(*last[b])
                for k, t in enumerate(tiles):
                    if ready is not None:
                        pe.wait_ge(ready, n.next(ready))
                    ins = pe.matmul(bank[b][:, :], lhsT, t, start=(k == 0), stop=(k == len(tiles) - 1))
                ins.then_inc(psum_for[who], hand(b, who))
                return last[b]

            def turn(parts, b, who, row=0):
                if last[b]:
                    pe.wait_ge(*last[b])
                for in_, at in parts:
                    m, f = in_.shape[0], in_.shape[-1]
                    ins = pe.transpose(bank[b][0:f, at:at + m], in_, ident[row:row + m, row:row + m])
                ins.then_inc(psum_for[who], hand(b, who))
                return last[b]

            def norm(sq, summed=False):
                if summed:
                    return sum_tiles([W(sq)], 4, "act", ones, S("squares_ready"))
                sum_tiles([W(sq + c) for c in range(DC)], 4, "act", ones, S("squares_ready"))

            def merge_levels(group, heads, ready_x, starts=1, fill=0):
                am, x, xT, tt = group
                halves = heads // 4
                pe.wait_ge(ready_x, n.next(ready_x, starts))
                waits = [turn([(xT(4 * hf + q), q * P) for q in range(4)], 4 + hf, "act") for hf in range(halves)]
                for lv in range(1, 7):
                    pe.wait_ge(S("level_masked"), n.next(S("level_masked")))
                    for w in waits:
                        pe.wait_ge(*w)
                    waits, products = [], []
                    for hf in range(halves):
                        if last[4 + hf]:
                            pe.wait_ge(*last[4 + hf])
                        for q in range(4):
                            h = 4 * hf + q
                            ins = pe.matmul(bank[4 + hf][:, q * P:(q + 1) * P], am(lv, h), x(h), start=True, stop=True)
                            if h == 0:
                                ins.then_inc(S("level_begun"), 1)
                        ins.then_inc(psum_for["act"], hand(4 + hf, "act"))
                        products.append(last[4 + hf])
                    early_gates(fill)
                    for hf in range(halves):
                        pe.wait_ge(*products[hf])
                        for kind in ((1,) if lv == 6 else (0, 1)):
                            b = (6 if kind == 0 else 4) + hf
                            if last[b]:
                                pe.wait_ge(*last[b])
                            for q in range(4):
                                h = 4 * hf + q
                                if kind == 0:
                                    ins = pe.matmul(bank[b][:, q * P:(q + 1) * P], xT(h), tt(h), start=True, stop=True)
                                else:
                                    ins = pe.matmul(bank[b][:, q * P:(q + 1) * P], tt(h), xT(h), start=True, stop=True)
                            ins.then_inc(psum_for["dve"], hand(b, "dve"))
                            waits.append(last[b])
                for w in waits:
                    pe.wait_ge(*w)

            xnk = lambda k: (xh[:, k, :], xl[:, k, :])
            xn_split = S("xn_split")
            pe.wait_ge(S("loads_ready"), n.next(S("loads_ready"), 32))

            norm(48)
            dense("in_a", 32, DC, xnk, ["act"], xn_split)
            pe.wait_ge(S("bias_loads"), n.next(S("bias_loads"), 32))
            for b, (at, w) in ((6, (0, T)), (7, (T, P))):
                if last[b]:
                    pe.wait_ge(*last[b])
                pe.matmul(bank[b][0:8, 0:w], W(61)[0:BUCKETS, 0:8], work[0:BUCKETS, 59 * T + at:59 * T + at + w],
                    start=True, stop=True)\
                    .then_inc(psum_for["act"], hand(b, "act"))
            for c in range(8):
                sum_tiles([W(48 + c)], 4 + c % 2, "act", pair, S("qk_square"))
            pe.wait_ge(S("table_back"), n.next(S("table_back"), 16))
            for h in range(8):
                if last[6 + h % 2]:
                    pe.wait_ge(*last[6 + h % 2])
                pe.matmul(bank[6 + h % 2][:, :], C("flip"), W(40 + h), start=True, stop=True)\
                    .then_inc(psum_for["act"], hand(6 + h % 2, "act"))
            mark("flipped")
            turn([(W(31)[:, t * P:(t + 1) * P], t * P) for t in range(NT)], 4, "dve")
            pe.wait_ge(S("qk_normed"), n.next(S("qk_normed"), 8))
            for t in range(NT):
                turn([(W(8 + c)[:, t * P:(t + 1) * P], c * P) for c in range(4)], 4 + t % 2, "act")
            mark("scores")
            for i in range(1, NT):
                for h in range(8):
                    r = slice(HD * (h % 2), HD * (h % 2) + HD)
                    if last[4 + h % 2]:
                        pe.wait_ge(*last[4 + h % 2])
                    pe.matmul(bank[4 + h % 2][:, 0:(i + 1) * P], W(12 + h // 2)[r, i * P:(i + 1) * P], W(30)[r,
                        0:(i + 1) * P], start=True, stop=True)\
                        .then_inc(psum_for["act"], hand(4 + h % 2, "act"))
            mark("attention")
            turned = {}
            steps = [(i, h) for i in range(NT) for h in range(8)]

            def logits(g):
                i, h = steps[g]
                r = slice(HD * (h % 2), HD * (h % 2) + HD)
                if last[4 + g % 2]:
                    pe.wait_ge(*last[4 + g % 2])
                pe.matmul(bank[4 + g % 2][:, 0:(i + 1) * P], W(h // 2)[r, i * P:(i + 1) * P], W(4 + h // 2)[r,
                    0:(i + 1) * P], start=True, stop=True)\
                    .then_inc(psum_for["dve"], hand(4 + g % 2, "dve"))

            def turn_probs(g):
                i, h = steps[g]
                pe.wait_ge(S("probs_ready"), n.next(S("probs_ready")))
                turned[g] = turn([(W(57 + g % 2)[:, s * P:(s + 1) * P], s * P) for s in range(i + 1)], 6, "act")

            def values(g):
                i, h = steps[g]
                r = slice(HD * (h % 2), HD * (h % 2) + HD)
                pe.wait_ge(*turned[g])
                if last[7]:
                    pe.wait_ge(*last[7])
                for s in range(i + 1):
                    ins = pe.matmul(bank[7][r, 0:P], W(48 + s)[:, h * HD:(h + 1) * HD],
                                    W(59 + g % 2)[:, s * P:(s + 1) * P], start=(s == 0), stop=(s == i))
                ins.then_inc(psum_for["act"], hand(7, "act"))

            logits(0)
            for g in range(len(steps) + 1):
                if g + 1 < len(steps):
                    logits(g + 1)
                if g < len(steps):
                    early_gates(IN_ATTENTION)
                    turn_probs(g)
                if g >= 1:
                    values(g - 1)

            mark("rwkv")
            pe.wait_ge(S("lora_ready"), n.next(S("lora_ready"), 3))
            pe.wait_ge(S("lora_loads"), n.next(S("lora_loads"), 48))
            for c in range(4):
                s = slice(c * P, (c + 1) * P)
                if last[4]:
                    pe.wait_ge(*last[4])
                pe.matmul(bank[4][:, :], W(59)[0:HD, s], W(28)[0:HD, :], start=True, stop=True)\
                    .then_inc(psum_for["act"], hand(4, "act"))
                if last[5]:
                    pe.wait_ge(*last[5])
                pe.matmul(bank[5][:, :], W(59)[HD:P, s], W(28)[HD:P, :], start=True, stop=True)\
                    .then_inc(psum_for["act"], hand(5, "act"))
                if last[6]:
                    pe.wait_ge(*last[6])
                pe.matmul(bank[6][:, :], W(60)[:, s], W(29), start=True, stop=False)
                pe.matmul(bank[6][:, :], W(61)[0:32, s], W(31)[0:32, :], start=False, stop=True)\
                    .then_inc(psum_for["act"], hand(6, "act"))
            mark("lora_end")
            for c in range(4):
                sum_tiles([W(28 + c)], 4 + c % 2, "dve", pair, S("kk_square"))
            for c in range(4):
                sum_tiles([W(28 + c)], 4 + c, "dve", pair, S("rk_ready"))
            pe.wait_ge(S("operands_ready"), n.next(S("operands_ready")))
            pe.wait_ge(S("operands_ready_2"), n.next(S("operands_ready_2")))
            ar = W(0, 8).rearrange("p (c n s t) -> p c n s t", c=4, n=NT, s=2)
            for ch in range(NT):
                cs = slice(ch * P, (ch + 1) * P)
                for src, b in ((8, 4), (12, 5), (24, 6)):
                    tokens = turn([(W(src + c)[:, cs], c * P) for c in range(4)], b, "act")
                for h in range(8):
                    r = slice(HD * (h % 2), HD * (h % 2) + HD)
                    b = 4 + h % 2
                    if last[b]:
                        pe.wait_ge(*last[b])
                    rhs = ar[r, h // 2, ch].rearrange("p s t -> p (s t)")
                    pe.matmul(bank[b][:, 0:2 * P], W(8 + h // 2)[r, cs], rhs, start=True, stop=True)
                    pe.matmul(bank[b][:, 2 * P:4 * P], W(12 + h // 2)[r, cs], rhs, start=True, stop=True)\
                        .then_inc(psum_for["dve"], hand(b, "dve"))
                v8 = lambda t, h: W(t, 2)[:, h * P:(h + 1) * P]
                merge_levels((lambda lv, h: v8(54 + 2 * (lv % 2), h), lambda h: v8(48, h), lambda h: v8(50, h),
                              lambda h: v8(52, h)), 8, S("inverse_start"), 1, IN_RWKV)
                if ch:
                    pe.wait_ge(S("state_ready"), n.next(S("state_ready")))
                pe.wait_ge(*tokens)
                for par in range(2):
                    r = slice(HD * par, HD * par + HD)
                    if last[4 + par]:
                        pe.wait_ge(*last[4 + par])
                    for c in range(4):
                        h = 2 * c + par
                        o = bank[4 + par][:, c * HD:(c + 1) * HD]
                        if ch:
                            pe.matmul(o, ar[r, c, ch, 0, :], W(31)[r, c * HD:(c + 1) * HD], start=True, stop=False)
                        ins = pe.matmul(o, W(40 + h)[:, 2 * P:3 * P], W(30)[:, h * HD:(h + 1) * HD],
                                        start=(ch == 0), stop=True)
                    ins.then_inc(psum_for["dve"], hand(4 + par, "dve"))
                    rhs_token = last[4 + par]
                pe.wait_ge(*rhs_token)
                if last[6]:
                    pe.wait_ge(*last[6])
                for h in range(8):
                    ins = pe.matmul(bank[6][:, h * HD:(h + 1) * HD], v8(50, h), W(57)[:, h * HD:(h + 1) * HD],
                                    start=True, stop=True)
                ins.then_inc(psum_for["act"], hand(6, "act"))
                pe.wait_ge(*last[6])
                for par in range(2):
                    r = slice(HD * par, HD * par + HD)
                    if last[4 + par]:
                        pe.wait_ge(*last[4 + par])
                    for c in range(4):
                        h = 2 * c + par
                        hs = slice(h * HD, (h + 1) * HD)
                        o = bank[4 + par][r, c * P:(c + 1) * P]
                        if ch:
                            pe.matmul(o, W(31)[r, c * HD:(c + 1) * HD], ar[r, c, ch, 1, :], start=True, stop=False)
                        pe.matmul(o, W(56)[:, hs], W(40 + h)[:, P:2 * P], start=(ch == 0), stop=False)
                        ins = pe.matmul(o, W(30)[:, hs], W(40 + h)[:, 3 * P:4 * P], start=False, stop=True)
                    ins.then_inc(psum_for["act"], hand(4 + par, "act"))
                    y_token = last[4 + par]
                if ch < NT - 1:
                    if last[7]:
                        pe.wait_ge(*last[7])
                    for h in range(8):
                        r = slice(HD * (h % 2), HD * (h % 2) + HD)
                        hs = slice(h * HD, (h + 1) * HD)
                        o = bank[7][r, (h // 2) * HD:(h // 2 + 1) * HD]
                        pe.matmul(o, W(28)[:, hs], W(56)[:, hs], start=True, stop=False)
                        ins = pe.matmul(o, W(29)[:, hs], W(30)[:, hs], start=False, stop=True)
                    ins.then_inc(psum_for["dve"], hand(7, "dve"))
            pe.wait_ge(*y_token)
            mark("groupnorm")
            for c in range(4):
                if last[4 + c % 2]:
                    pe.wait_ge(*last[4 + c % 2])
                pe.matmul(bank[4 + c % 2][:, :], pair, W(58 + c), start=True, stop=True)\
                    .then_inc(psum_for["dve"], hand(4 + c % 2, "dve"))
            for c in range(4):
                sum_tiles([W(40 + c)], 6 + c % 2, "act", pair, S("y_square"))
            early_gates(16 * DC - early[0])
            merge("w_merge1", 2, 16, 32, [4, 4])

            def tail(name, high, low, sq, parts, whos):
                dense(f"out{name}", DC, DC, lambda k: (WR(high + k), WR(low + k)), ["dve"], S("merged_split"))
                norm(sq, True)
                for stage, p, up in ffn_stages(name, parts):
                    h, l = hidden_at(p)
                    if up:
                        dense(stage, parts[p] * len(whos), DC, xnk, whos, xn_split if p == 0 else None)
                    else:
                        dense(stage, DC, parts[p], lambda k: (WR(h + k), WR(l + k)), ["dve"], S("hidden_split"))

            tail("1", 24, 40, 48, PARTS1, ["act", "dve"])

            norm(40, True)
            dense("in_b", 2 * RC, DC, xnk, ["dve", "act"], xn_split)
            pe.wait_ge(S("gate_loads"), n.next(S("gate_loads"), 64))
            pe.wait_ge(S("conv_done"), n.next(S("conv_done")))
            mark("lru")
            for c in range(RC):
                for w, b in ((51, 4), (56, 5)):
                    if last[b]:
                        pe.wait_ge(*last[b])
                    pe.matmul(bank[b][:, :], W(w, 5)[:, c * P:(c + 1) * P], W(21 + c), start=True, stop=True)\
                        .then_inc(psum_for["act"], hand(b, "act"))
            early_gates(EARLY_2 * DC)
            dense("uv", 16, DC, xnk, ["act"], None)
            mark("sgu")
            pe.wait_ge(evac_by["act"], handed["act"])
            sum_tiles([W(29 + c) for c in range(8)], 4, "dve", ones)
            sum_tiles([W(37 + c) for c in range(8)], 5, "act", ones, S("v_square"))
            early_gates(2 * DC)
            pe.wait_ge(S("v_normed"), n.next(S("v_normed")))
            pe.wait_ge(S("sgu_ready"), n.next(S("sgu_ready")))
            for t in range(NT):
                for hf in range(2):
                    v_token = turn([(W(29 + 4 * hf + q)[:, t * P:(t + 1) * P], q * P) for q in range(4)], 6 + hf, "act")
            pe.wait_ge(*v_token)
            for g in range(8):
                b = 4 + g % 2
                if last[b]:
                    pe.wait_ge(*last[b])
                for t in range(NT):
                    ins = pe.matmul(bank[b][:, t * P:(t + 1) * P], W(37 + 2 * t, 2)[:, g * P:(g + 1) * P],
                                    W(46, 2)[:, g * P:(g + 1) * P], start=True, stop=True)
                ins.then_inc(psum_for["dve"], hand(b, "dve"))
            early_gates(32 * DC - early[0])
            merge("w_merge2", 2, 29, 11, [RC, 8])
            tail("2", 29, 50, 40, PARTS2, ["act"])
            norm(48, True)

            norm(40)
            dense("in_m", 18, DC, xnk, ["act"], xn_split)
            pe.wait_ge(S("gates_ready"), n.next(S("gates_ready")))
            turn([(W(21)[0:4, t * P:(t + 1) * P], 4 * t) for t in range(NT)], 4, "act")
            mark("c_turned")
            for t in range(NT):
                turn([(W(8 + c)[:, t * P:(t + 1) * P], c * P) for c in range(4)], 4 + t % 2, "act")
            pe.wait_ge(S("decay_row"), n.next(S("decay_row")))
            for h in range(4):
                sel = C("sel", h * P, P)
                if last[5]:
                    pe.wait_ge(*last[5])
                pe.matmul(bank[5][:, :], sel[0:4, :], W(22)[0:4, :], start=True, stop=True)\
                    .then_inc(psum_for["dve"], hand(5, "dve"))
                for s in range(NT):
                    if last[6 + s % 2]:
                        pe.wait_ge(*last[6 + s % 2])
                    pe.matmul(bank[6 + s % 2][:, s * P:T], W(4 + h)[:, s * P:(s + 1) * P], W(h)[:, s * P:T],
                        start=True, stop=True)\
                        .then_inc(psum_for["dve"], hand(6 + s % 2, "dve"))
                if last[6]:
                    pe.wait_ge(*last[6])
                pe.matmul(bank[6][:, :], sel[0:4, :], W(24)[0:4, :], start=True, stop=True)\
                    .then_inc(psum_for["act"], hand(6, "act"))
                mark(f"floor{h}")
                pe.wait_ge(S("weights_ready"), n.next(S("weights_ready")))
                for lhs, b in ((ones, 5), (None, 4)):
                    if last[b]:
                        pe.wait_ge(*last[b])
                    for s in range(NT):
                        ins = pe.matmul(bank[b][:, s * P:T], W(25 + s)[:, h * P:(h + 1) * P] if lhs is None else lhs,
                                        W(33 + s)[:, s * P:T], start=(s == 0), stop=(s == NT - 1))
                    ins.then_inc(psum_for["dve"], hand(b, "dve"))
                early_gates(IN_MLSTM)
                pe.wait_ge(S("h_square"), n.next(S("h_square")))
                if last[7]:
                    pe.wait_ge(*last[7])
                pe.matmul(bank[7][:, :], ones, W(44), start=True, stop=True).then_inc(psum_for["act"], hand(7, "act"))

            dense("in_l", 16, DC, xnk, ["act"], None)
            pe.wait_ge(S("gla_load"), n.next(S("gla_load"), 16))
            for c in range(4):
                if last[4 + c % 2]:
                    pe.wait_ge(*last[4 + c % 2])
                pe.matmul(bank[4 + c % 2][:, :], W(40)[64:80, c * P:(c + 1) * P], W(16)[64:80, :], start=True,
                    stop=True)\
                    .then_inc(psum_for["act"], hand(4 + c % 2, "act"))
            for t in range(NT):
                turn([(W(8 + c)[:, t * P:(t + 1) * P], c * P) for c in range(4)], 6 + t % 2, "act")
            lvl = 0
            for h in range(4):
                for half in (256, 128, 64, 32, 16, 8, 4, 2, 1, 0):
                    b = 4 + lvl % 2
                    qk = W(30 + lvl % 2)
                    if last[b]:
                        pe.wait_ge(*last[b])
                    early_gates(IN_GLA)
                    if half:
                        pe.wait_ge(S("level_ready"), n.next(S("level_ready")))
                    if half == 256:
                        for s in range(2):
                            ins = pe.matmul(bank[b][:, s * 256:(s + 1) * 256], qk[:, s * P:(s + 1) * P], qk[:, 256:512],
                                            start=True, stop=True)
                    elif half == 128:
                        for s in range(2):
                            ins = pe.matmul(bank[b][:, s * P:(s + 1) * P], qk[:, 2 * s * P:(2 * s + 1) * P],
                                            qk[:, (2 * s + 1) * P:(2 * s + 2) * P], start=True, stop=True)
                    else:
                        for s in range(NT):
                            sl = slice(s * P, (s + 1) * P)
                            if half:
                                ins = pe.matmul(bank[b][:, sl], qk[:, sl], qk[:, sl], start=True, stop=True)
                            else:
                                ins = pe.matmul(bank[b][:, sl], W(4 + h)[:, sl], W(h)[:, sl], start=True, stop=True)
                    ins.then_inc(psum_for["dve"], hand(b, "dve"))
                    lvl += 1 if half else 0
                pe.wait_ge(S("weights_ready"), n.next(S("weights_ready")))
                if last[6]:
                    pe.wait_ge(*last[6])
                for s in range(NT):
                    ins = pe.matmul(bank[6][:, s * P:T], W(22 + s)[:, h * P:(h + 1) * P], W(32 + s)[:, s * P:T],
                                    start=(s == 0), stop=(s == NT - 1))
                ins.then_inc(psum_for["act"], hand(6, "act"))
                early_gates(EARLY_L * DC // 4 - 10 * IN_GLA)
                pe.wait_ge(S("h_square"), n.next(S("h_square")))
                if last[7]:
                    pe.wait_ge(*last[7])
                pe.matmul(bank[7][:, :], ones, W(42), start=True, stop=True).then_inc(psum_for["act"], hand(7, "act"))

            dense("in_d", 16, DC, xnk, ["act"], None)
            mark("gdn")
            early_gates(IN_GDN[0])
            for c in range(8):
                sum_tiles([W(0 + c)], 4 + c % 2, "act", ones, S("qk_square"))
            pe.wait_ge(S("decay_row"), n.next(S("decay_row")))
            pe.wait_ge(S("beta_ready"), n.next(S("beta_ready")))
            turn([(W(48)[32:36, t * P:(t + 1) * P], 4 * t) for t in range(NT)], 4, "dve", row=32)
            for h in range(4):
                sel = C("sel", h * P, P)
                if last[5]:
                    pe.wait_ge(*last[5])
                pe.matmul(bank[5][:, :], sel[32:36, :], W(48)[32:36, :], start=True, stop=True)\
                    .then_inc(psum_for["dve"], hand(5, "dve"))
                if last[6 + h % 2]:
                    pe.wait_ge(*last[6 + h % 2])
                pe.matmul(bank[6 + h % 2][:, :], sel[32:36, :], W(17)[32:36, :], start=True, stop=True)\
                    .then_inc(psum_for["dve"], hand(6 + h % 2, "dve"))
            early_gates(IN_GDN[1])
            pe.wait_ge(S("operands_ready"), n.next(S("operands_ready")))
            kq = W(0, 8).rearrange("p (h n s t) -> p h n s t", h=4, n=NT, s=2)
            for t in range(NT):
                cs = slice(t * P, (t + 1) * P)
                turn([(W(34 + c)[:, cs], c * P) for c in range(4)], 4 + t % 2, "act")
            for t in range(NT):
                cs = slice(t * P, (t + 1) * P)
                tokens = turn([(W(26 + c)[:, cs], c * P) for c in range(4)], 4 + t % 2, "act")
            for h in range(4):
                for ch in range(NT):
                    m = h * NT + ch
                    b = 6 + m % 2
                    if last[b]:
                        pe.wait_ge(*last[b])
                    pe.matmul(bank[b][:, 0:2 * P], W(22 + h)[:, ch * P:(ch + 1) * P], kq[:, h,
                        ch].rearrange("p s t -> p (s t)"), start=True, stop=True)\
                        .then_inc(psum_for["dve"], hand(b, "dve"))
            for c0 in range(0, NT, 2):
                merge_levels((lambda lv, h: W(38 + 2 * (lv % 2), 2)[:, h * P:(h + 1) * P],
                              lambda h: W(26, 2)[:, h * P:(h + 1) * P],
                              lambda h, c0=c0: W(22 + c0, 2)[:, h * P:(h + 1) * P],
                              lambda h: W(28, 2)[:, h * P:(h + 1) * P]), 8, S("inverse_start"), 2, IN_LEVEL)
            pe.wait_ge(*tokens)
            mats = W(42, 8).rearrange("p (h n s t) -> p h n s t", h=4, n=NT, s=2)
            for ch in range(NT):
                cs = slice(ch * P, (ch + 1) * P)
                hs = [slice(h * P, (h + 1) * P) for h in range(4)]
                if ch:
                    pe.wait_ge(*state)
                    if last[4]:
                        pe.wait_ge(*last[4])
                    for h in range(4):
                        ins = pe.matmul(bank[4][:, hs[h]], W(8 + h)[:, cs], W(41)[:, hs[h]], start=True, stop=True)
                    ins.then_inc(psum_for["dve"], hand(4, "dve"))
                    pe.wait_ge(*last[4])
                if last[5]:
                    pe.wait_ge(*last[5])
                for h in range(4):
                    ins = pe.matmul(bank[5][:, hs[h]], W(22 + ch)[:, hs[h]], (W(39) if ch else W(34 + ch))[:, hs[h]],
                                    start=True, stop=True)
                ins.then_inc(psum_for["act"], hand(5, "act"))
                early_gates(IN_STATE)
                pe.wait_ge(*last[5])
                if last[6]:
                    pe.wait_ge(*last[6])
                for h in range(4):
                    if ch:
                        pe.matmul(bank[6][:, hs[h]], W(41)[:, hs[h]], W(30 + h)[:, cs], start=True, stop=False)
                    ins = pe.matmul(bank[6][:, hs[h]], W(40)[:, hs[h]], mats[:, h, ch, 1, :], start=(ch == 0), stop=True)
                ins.then_inc(psum_for["act"], hand(6, "act"))
                if ch < NT - 1:
                    if last[7]:
                        pe.wait_ge(*last[7])
                    for h in range(4):
                        ins = pe.matmul(bank[7][:, hs[h]], W(18 + ch)[:, hs[h]], W(40)[:, hs[h]], start=True, stop=True)
                    ins.then_inc(psum_for["dve"], hand(7, "dve"))
                    state = last[7]
            for c in range(4):
                sum_tiles([W(42 + c)], 4 + c % 2, "act", ones, S("y_square"))
            early_gates(56 * DC - early[0])
            merge("w_merge3", 3, 36, 50, [4, 4, 4])
            tail("3", 8, 18, 40, PARTS2, ["act"])
            norm(48, True)

        @block.sync
        def _(sp):
            for half in range(2):
                cs = slice(half * DC // 2, (half + 1) * DC // 2)
                sp.dma_start(W3(0, DC)[:, cs, :], a["x"][:, cs, :]).then_inc(S(f"x_loaded_{half}"), 16)
            sp.dma_start(cst[:, :], a["cst"]).then_inc(S("loads_ready"), 16)
            sp.dma_start(vec[:, :], a["vec"]).then_inc(S("loads_ready"), 16)
            begun = S("slab_begun")
            count = 0
            for name, row, slabs, blocks in stream:
                w = a[name]
                if name in merge_slabs:
                    col = 0
                    sizes = merge_slabs[name]
                    for j in range(DC):
                        col = 0
                        for size in sizes:
                            if count >= RING:
                                sp.wait_ge(begun, count - RING + 2)
                            sp.dma_start(slab[:, count % RING, :], w[j, :, col * P:(col + SLAB) * P])\
                              .then_inc(landed[count % RING], 16)
                            count += 1
                            col += SLAB
                    continue
                base = count

                def load(i, j):
                    slot = (base + j) % RING
                    idx = i * RING + j
                    if not (isinstance(i, int) and base + idx < RING):
                        sp.wait_ge(begun, idx + (base - RING + 2))
                    src = w[row + idx, :, :] if isinstance(idx, int) else \
                        w[bass.ds(idx + row, 1), :, :].rearrange("a p n -> (a p) n")
                    sp.dma_start(slab[:, slot, :], src).then_inc(landed[slot], 16)

                whole, rest = divmod(slabs, RING)
                for j in range(RING if whole else 0):
                    load(0, j)
                if whole > 1:
                    with sp.Fori(1, whole) as i:
                        for j in range(RING):
                            load(i, j)
                for j in range(rest):
                    load(whole, j)
                count += slabs
            for c in range(DC):
                sp.wait_ge(S("result_ready"), c + 1)
                sp.dma_start(out[:, c, :], X(c)).then_inc(S("result_stored"), 16)
            sp.wait_ge(S("result_stored"), 16 * DC)

        @block.scalar
        def _(act):
            n = Count()
            chain = S("act_chain")

            evac = evac_by["act"]

            to_split = [0]

            def high_part(s, i=0):
                slot = s % RING
                act.wait_ge(landed[slot], i * 16 + 16 * (s // RING + 1))
                act.copy(slab_high[:, slot, :], slab[:, slot, :]).then_inc(S("slab_high"), 1)

            def steps_of(stage, n_slabs, body=None, peel=False):
                s0 = to_split[0]
                whole, rest = divmod(n_slabs, RING)

                def some(i, count):
                    for j in range(count):
                        if not isinstance(i, int) or s0 + i * RING + j < total_slabs:
                            high_part(s0 + j, i)
                        if body:
                            body(i, j)

                first = 1 if peel else 0
                end = whole if s0 + n_slabs <= total_slabs else whole - 1
                if peel:
                    some(0, RING)
                if end > first:
                    with act.Fori(first, end) as i:
                        some(i, RING)
                if end < whole:
                    some(whole - 1, RING)
                if rest:
                    some(whole, rest)
                to_split[0] += n_slabs

            early = [0, 0]

            def send_gate():
                t = early[0]
                s = t % STAGING
                high_part(to_split[0])
                to_split[0] += 1
                act.wait_ge(S("gate_done"), t + 1)
                if t >= STAGING:
                    act.wait_ge(S(f"gate_stored_{s}"), 16 * (t // STAGING))
                act.copy(staging[:, s, :], bank[t % 4][:, :]).then_inc(S("gate_out"), 1)
                act.wait_ge(S("gate_out"), t + 1)
                act.dma_start(gate_place(t), staging[:, s, :]).then_inc(S(f"gate_stored_{s}"), 16)
                early[0] += 1

            def send_gates(products, until=None):
                ready = early[1] // DC
                early[1] += products
                while early[0] < (ready if until is None else until):
                    send_gate()

            def tiles(stage):
                base = n.seen.get(psum_for["act"].name, 0)
                assert base == handed_at[stage]["act"], (stage, base, handed_at[stage])
                return base

            def copy_tiles(stage, total, dst, fn=None):
                base = tiles(stage)

                def evacuate(i, b):
                    act.wait_ge(psum_for["act"], i * RING + (base + b + 1))
                    if fn is None:
                        act.copy(dyn(dst, i * RING + b), bank[b][:, :]).then_inc(evac, 1)
                    else:
                        act.activation(dyn(dst, i * RING + b), bank[b][:, :], fn).then_inc(evac, 1)

                steps_of(stage, total, evacuate)
                n.seen[psum_for["act"].name] = base + total
                n.made[evac.name] = base + total
                act.wait_ge(evac, base + total)

            def norm(sq, sem=None, value=0, step=1, split=True):
                for c in range(DC if sem else 0):
                    act.wait_ge(sem[c] if isinstance(sem, list) else sem, value + step * c)
                    act.activation(W(sq + c), X(c), ACT.Square)\
                        .then_inc(S("squares_ready"), n.up(S("squares_ready")))
                act.wait_ge(psum_for["act"], n.next(psum_for["act"]))
                act.activation(W(sq), bank[4][:, :], ACT.Ln, bias=eps[1e-06], scale=1.0 / D)\
                    .then_inc(evac, n.up(evac))
                act.wait_ge(evac, n.own(evac))
                act.activation(W(sq), W(sq), ACT.Exp, scale=-0.5).then_inc(S("rstd_ready"), n.up(S("rstd_ready")))
                act.wait_ge(S("rstd_ready"), n.own(S("rstd_ready")))
                if split:
                    for c in range(DC):
                        act.wait_ge(S("xn_raw"), n.next(S("xn_raw")))
                        act.copy(xh[:, c, :], x_raw[:, c, :]).then_inc(S("xn_high"), n.up(S("xn_high")))

            def relu_up(stage, k):
                base, h0 = tiles(stage), hidden[0]

                def relu(i, b):
                    act.wait_ge(psum_for["act"], i * RING + (base + b + 1))
                    if h0 or not isinstance(i, int):
                        act.wait_ge(S("hidden_split"), i * RING + (h0 + b - RING + 1))
                    act.activation(W(56 + b), bank[b][:, :], ACT.Relu).then_inc(evac, 1)

                steps_of(stage, k, relu, peel=not h0)
                hidden[0] += k
                n.seen[psum_for["act"].name] = base + k
                n.made[evac.name] = base + k

            def silu_up(stage, k):
                base, h0 = tiles(stage), hidden[0]

                def silu(i, b):
                    if b % 2:
                        return
                    q = b // 2
                    act.wait_ge(psum_for["act"], i * 2 + (base + q + 1))
                    if h0 or not isinstance(i, int):
                        act.wait_ge(S("hidden_split"), i * 2 + (h0 + q - 1))
                    act.activation(W(56 + q), bank[b][:, :], ACT.Silu).then_inc(evac, 1)

                steps_of(stage, 2 * k, silu, peel=not h0)
                hidden[0] += k
                n.seen[psum_for["act"].name] = base + k
                n.made[evac.name] = base + k

            def tail(name, merged, high, sq, parts, up_tiles):
                act.wait_ge(S("merged_ready"), n.next(S("merged_ready")))
                for c in range(DC):
                    act.copy(WR(high + c), W(merged + c)).then_inc(S("merged_high"), n.up(S("merged_high")))
                steps_of(f"out{name}", DC)
                norm(sq)
                for stage, p, up in ffn_stages(name, parts):
                    if up:
                        up_tiles(stage, parts[p])
                    else:
                        steps_of(stage, DC)

            hidden = [0]
            eps = {}
            act.wait_ge(S("small_consts"), n.next(S("small_consts")))
            eps[1e-6], eps[64e-6], eps[64e-5], eps["one"], eps["kk"] = SM(300), SM(301), SM(302), SM(303), SM(304)

            for s in range(LOOK):
                high_part(s)
            to_split[0] = LOOK

            norm(48, [S("x_loaded_0")] * 4 + [S("x_loaded_1")] * 4, 16, 0)
            act.wait_ge(S("loads_ready"), n.next(S("loads_ready"), 32))
            copy_tiles("in_a", 32, W3(0, 32))
            for c in range(8):
                act.activation(W(48 + c), W(c), ACT.Square).then_inc(S("qk_square"), n.up(S("qk_square")))
            act.wait_ge(psum_for["act"], n.next(psum_for["act"]))
            act.copy(W(57)[0:8, :], bank[6][0:8, :]).then_inc(evac, n.up(evac))
            act.wait_ge(evac, n.own(evac))
            act.wait_ge(psum_for["act"], n.next(psum_for["act"]))
            act.copy(W(58)[0:8, 0:P], bank[7][0:8, 0:P]).then_inc(evac, n.up(evac))
            act.wait_ge(evac, n.own(evac))
            act.dma_start(a["scratch"], work[0:8, 57 * T:57 * T + NREL]).then_inc(S("table_out"), 16)
            act.wait_ge(S("table_out"), 16)
            act.dma_start(W3(40, 8), bass.AP(tensor=a["scratch"].tensor, offset=0, ap=[[1, P], [NREL, 8], [1, T]]))\
               .then_inc(S("table_back"), 16)
            for c in range(8):
                act.wait_ge(psum_for["act"], n.next(psum_for["act"]))
                if c < 4:
                    act.activation(W(48 + c), bank[4 + c % 2][:, :], ACT.Ln, bias=eps[6.4e-05], scale=1.0)\
                        .then_inc(evac, n.up(evac))
                    act.wait_ge(evac, n.own(evac))
                else:
                    act.activation(W(48 + c), bank[4 + c % 2][:, :], ACT.Ln, bias=eps[1e-06], scale=1.0 / HD)\
                        .then_inc(evac, n.up(evac))
                    act.wait_ge(evac, n.own(evac))
            for c in range(8):
                act.activation(W(48 + c), W(48 + c), ACT.Exp, scale=-0.5).then_inc(S("qk_rstd"), n.up(S("qk_rstd")))
            for h in range(8):
                act.wait_ge(psum_for["act"], n.next(psum_for["act"]))
                act.copy(W(40 + h), bank[6 + h % 2][:, :]).then_inc(S("evac_by_act"), n.up(S("evac_by_act")))
            act.wait_ge(S("qk_normed"), n.next(S("qk_normed"), 8))
            for t in range(NT):
                act.wait_ge(psum_for["act"], n.next(psum_for["act"]))
                act.copy(W(48 + t), bank[4 + t % 2][:, :]).then_inc(evac, n.up(evac))
            k = 0
            for i in range(1, NT):
                for h in range(8):
                    act.wait_ge(psum_for["act"], n.next(psum_for["act"]))
                    if k >= 2:
                        act.wait_ge(S("relu_used"), n.next(S("relu_used")))
                    act.activation(W(55 + h % 2)[:, 0:(i + 1) * P], bank[4 + h % 2][:, 0:(i + 1) * P], ACT.Relu)\
                        .then_inc(evac, n.up(evac))
                    k += 1
            steps = [(i, h) for i in range(NT) for h in range(8)]
            act.wait_ge(S("relu_used"), n.next(S("relu_used"), 2))

            def exps(g):
                i, h = steps[g]
                b = g % 2
                act.wait_ge(S("logits_ready"), n.next(S("logits_ready")))
                act.activation(W(57 + b)[:, 0:(i + 1) * P], W(57 + b)[:, 0:(i + 1) * P], ACT.Exp, bias=SM(200 + b),
                    accum_out=SM(204 + b))\
                    .then_inc(S("exps_ready"), n.up(S("exps_ready")))
                act.wait_ge(S("exps_ready"), n.own(S("exps_ready")))

            def turned(g):
                i, h = steps[g]
                act.wait_ge(psum_for["act"], n.next(psum_for["act"]))
                act.copy(W(59 + g % 2)[:, 0:(i + 1) * P], bank[6][:, 0:(i + 1) * P]).then_inc(evac, n.up(evac))
                act.wait_ge(evac, n.own(evac))

            def valued(g):
                i, h = steps[g]
                r = slice(HD * (h % 2), HD * (h % 2) + HD)
                act.wait_ge(psum_for["act"], n.next(psum_for["act"]))
                act.copy(W(32 + h // 2)[r, i * P:(i + 1) * P], bank[7][r, 0:P]).then_inc(evac, n.up(evac))

            for g in range(len(steps) + 2):
                if g < len(steps):
                    exps(g)
                if 1 <= g <= len(steps):
                    turned(g - 1)
                if g >= 2:
                    valued(g - 2)
                send_gates(IN_ATTENTION if g < len(steps) else 0)
            send_gates(0, AFTER_ATTENTION)

            act.wait_ge(S("shift_done"), n.next(S("shift_done"), 15))
            act.activation(W(28)[0:HD, :], W(28)[0:HD, :], ACT.Tanh).then_inc(S("lora_ready"), n.up(S("lora_ready")))
            act.activation(W(29), W(29), ACT.Sigmoid).then_inc(S("lora_ready"), n.up(S("lora_ready")))
            act.activation(W(31)[0:32, :], W(31)[0:32, :], ACT.Sigmoid)\
                .then_inc(S("lora_ready"), n.up(S("lora_ready")))
            for c in range(4):
                act.wait_ge(psum_for["act"], n.next(psum_for["act"]))
                act.activation(W(40 + c), bank[4][:, :], ACT.Sigmoid, bias=V("w0", c)).then_inc(evac, n.up(evac))
                act.wait_ge(psum_for["act"], n.next(psum_for["act"]))
                act.activation(W(52 + c), bank[5][:, :], ACT.Sigmoid, bias=V("a0", c)).then_inc(evac, n.up(evac))
                act.wait_ge(psum_for["act"], n.next(psum_for["act"]))
                act.copy(W(36 + c), bank[6][:, :]).then_inc(evac, n.up(evac))
            for c in range(4):
                act.wait_ge(S("kk_raw"), n.next(S("kk_raw")))
                act.activation(W(28 + c), W(56 + c), ACT.Square).then_inc(S("kk_square"), n.up(S("kk_square")))
            for c in range(4):
                act.wait_ge(evac_by["dve"], handed_at["lora_end"]["dve"] + c + 1)
                act.activation(W(28 + c), W(28 + c), ACT.Ln).then_inc(chain, n.up(chain))
                act.wait_ge(chain, n.own(chain))
            for c in range(4):
                act.activation(W(28 + c), W(28 + c), ACT.Exp, bias=eps["kk"], scale=-0.5)\
                    .then_inc(S("kk_rstd"), n.up(S("kk_rstd")))
            act.wait_ge(S("decay_sums"), n.next(S("decay_sums")))
            act.activation(SM(0, 16).rearrange("p (c n) -> p c n", c=4), W(44, 4).rearrange("p (c n t) -> p c n t",
                c=4, n=NT)[:, :, :, 63], ACT.Exp, scale=-EXPM05)\
                .then_inc(chain, n.up(chain))
            act.wait_ge(chain, n.own(chain))
            act.activation(W(44, 4), W(48, 4), ACT.Exp, scale=-EXPM05).then_inc(chain, n.up(chain))
            act.wait_ge(chain, n.own(chain))
            act.activation(W(48, 4), W(48, 4), ACT.Exp, scale=EXPM05).then_inc(chain, n.up(chain))
            act.wait_ge(chain, n.own(chain))
            act.activation(W(40, 4), W(40, 4), ACT.Exp, scale=-EXPM05)\
                .then_inc(S("decays_ready"), n.up(S("decays_ready")))
            act.wait_ge(S("decays_ready"), n.own(S("decays_ready")))
            for ch in range(NT):
                for dst, b in ((28, 4), (29, 5), (30, 6)):
                    act.wait_ge(psum_for["act"], n.next(psum_for["act"]))
                    act.copy(W(dst), bank[b][:, :]).then_inc(evac, n.up(evac))
                for hf in range(2):
                    act.wait_ge(psum_for["act"], n.next(psum_for["act"]))
                    act.copy(W(48 + hf), bank[4 + hf][:, :]).then_inc(evac, n.up(evac))
                for lv in range(1, 7):
                    for hf in range(2):
                        act.wait_ge(psum_for["act"], n.next(psum_for["act"]))
                        act.copy(W(52 + hf), bank[4 + hf][:, :]).then_inc(evac, n.up(evac))
                    send_gates(IN_RWKV)
                act.wait_ge(psum_for["act"], n.next(psum_for["act"]))
                act.mul(W(56), bank[6][:, :], -1.0).then_inc(evac, n.up(evac))
                act.wait_ge(evac, n.own(evac))
                yv = W(58, 4).rearrange("p (c t) -> p c t", c=4)
                for par in range(2):
                    r = slice(HD * par, HD * par + HD)
                    act.wait_ge(psum_for["act"], n.next(psum_for["act"]))
                    act.copy(yv[r, :, ch * P:(ch + 1) * P], bank[4 + par][r, :].rearrange("p (c t) -> p c t", c=4))\
                        .then_inc(evac, n.up(evac))
                    act.wait_ge(evac, n.own(evac))
            for c in range(4):
                act.wait_ge(evac_by["dve"], handed_at["groupnorm"]["dve"] + c + 1)
                act.activation(W(40 + c), W(58 + c), ACT.Square).then_inc(S("y_square"), n.up(S("y_square")))
            for c in range(4):
                act.wait_ge(psum_for["act"], n.next(psum_for["act"]))
                act.activation(W(44 + c), bank[6 + c % 2][:, :], ACT.Ln, bias=eps[0.00064], scale=1.0 / HD)\
                    .then_inc(evac, n.up(evac))
                act.wait_ge(evac, n.own(evac))
            for c in range(4):
                act.activation(W(44 + c), W(44 + c), ACT.Exp, scale=-0.5).then_inc(S("y_rstd"), n.up(S("y_rstd")))

            def merge(name, block_no, sg, high, low, n_branch, x_from):
                nb = GATES[block_no]
                act.wait_ge(S("branches_ready"), n.next(S("branches_ready")))
                for s in range(STAGING):
                    act.wait_ge(S(f"gate_stored_{s}"), 16 * ((early[0] - s + STAGING - 1) // STAGING))
                act.dma_start(W(sg, nb), a[f"gates_{block_no}"][0]).then_inc(S("gates_back_0"), 16)
                act.dma_start(W3(0, DC), x_from).then_inc(S("x_back"), 16)
                for c in range(n_branch):
                    act.copy(WR(high + c), W(low + c)).then_inc(S("branch_high"), n.up(S("branch_high")))
                for j in range(DC):
                    for _ in merge_slabs[name]:
                        high_part(to_split[0])
                        to_split[0] += 1
                    if j + 1 < DC:
                        if j:
                            act.wait_ge(evac_by["dve"], handed_at[name]["dve"] + nb * j)
                        act.dma_start(W(sg + nb * ((j + 1) % 2), nb), a[f"gates_{block_no}"][j + 1])\
                            .then_inc(S(f"gates_back_{(j + 1) % 2}"), 16)
                    act.wait_ge(S(f"gates_back_{j % 2}"), n.next(S(f"gates_back_{j % 2}"), 16))
                    act.activation(W(sg + nb * (j % 2), nb), W(sg + nb * (j % 2), nb), ACT.Sigmoid)\
                        .then_inc(S("sigmoids_ready"), n.up(S("sigmoids_ready")))

            send_gates(0, 16)
            merge("w_merge1", 1, 8, 16, 32, 8, a["x"])
            tail("1", 40, 24, 48, PARTS1, silu_up)

            act.wait_ge(S("x_ready"), n.next(S("x_ready")))
            act.dma_start(a["x_kept_1"], W3(0, DC)).then_inc(S("x_stored"), 16)
            norm(40)
            b0 = tiles("in_b")
            G = W3(11, RC)

            def gelu(i, b):
                if b % 2:
                    act.wait_ge(psum_for["act"], i * 2 + (b0 + b // 2 + 1))
                    act.activation(dyn(G, i * 2 + b // 2), bank[b][:, :], ACT.Gelu_apprx_tanh).then_inc(evac, 1)

            steps_of("in_b", 2 * RC, gelu)
            n.seen[psum_for["act"].name] = b0 + RC
            n.made[evac.name] = b0 + RC
            act.wait_ge(evac, b0 + RC)
            act.activation(SM(0, RC), vec[:, VEC["lam"][0]:VEC["lam"][0] + RC], ACT.Abs).then_inc(chain, n.up(chain))
            act.wait_ge(chain, n.own(chain))
            act.activation(SM(0, RC), SM(0, RC), ACT.Exp, scale=-1.0).then_inc(S("lam_exp"), n.up(S("lam_exp")))
            act.wait_ge(S("lam_exp"), n.own(S("lam_exp")))
            act.wait_ge(S("conv_done"), n.next(S("conv_done")))
            for c in range(RC):
                act.wait_ge(psum_for["act"], n.next(psum_for["act"]))
                act.activation(W(31 + c), bank[4][:, :], ACT.Sigmoid, bias=V("ba", c)).then_inc(evac, n.up(evac))
                act.wait_ge(psum_for["act"], n.next(psum_for["act"]))
                act.activation(W(c), bank[5][:, :], ACT.Sigmoid, bias=V("bx", c)).then_inc(evac, n.up(evac))
            act.wait_ge(evac, n.own(evac))
            act.wait_ge(S("softplus_ready"), n.next(S("softplus_ready")))
            for c in range(RC):
                act.activation(W(41 + c), W(31 + c), ACT.Tanh, scale=SM(20 + c)).then_inc(chain, n.up(chain))
            act.wait_ge(chain, n.own(chain))
            send_gates(0, 16 + 1)
            for c in range(RC):
                act.activation(W(31 + c), W(31 + c), ACT.Exp, scale=SM(30 + c)).then_inc(chain, n.up(chain))
            act.wait_ge(chain, n.own(chain))
            send_gates(0, 16 + 2)
            for c in range(RC):
                act.activation(W(51 + c), W(31 + c), ACT.Square).then_inc(S("a_square"), n.up(S("a_square")))
            send_gates(0, 16 + 3)
            for c in range(RC):
                act.wait_ge(S("norm_square"), n.next(S("norm_square")))
                act.activation(W(41 + c), W(41 + c), ACT.Sqrt).then_inc(S("lru_norm"), n.up(S("lru_norm")))
            send_gates(0, 16 + EARLY_2)
            act.wait_ge(S("ya_ready"), n.next(S("ya_ready")))
            copy_tiles("uv", 16, W3(21, 16), ACT.Gelu_apprx_tanh)
            for c in range(8):
                act.wait_ge(S("v_centred"), n.next(S("v_centred")))
                act.activation(W(37 + c), W(29 + c), ACT.Square).then_inc(S("v_square"), n.up(S("v_square")))
            act.wait_ge(psum_for["act"], n.next(psum_for["act"]))
            act.activation(W(45), bank[5][:, :], ACT.Ln, bias=eps[1e-06], scale=1.0 / D).then_inc(evac, n.up(evac))
            act.wait_ge(evac, n.own(evac))
            act.activation(W(45), W(45), ACT.Exp, scale=-0.5).then_inc(S("v_rstd"), n.up(S("v_rstd")))
            act.wait_ge(S("v_rstd"), n.own(S("v_rstd")))
            send_gates(0, 16 + EARLY_2 + 2)
            for t in range(NT):
                for hf in range(2):
                    act.wait_ge(psum_for["act"], n.next(psum_for["act"]))
                    act.copy(W(37 + 2 * t + hf), bank[6 + hf][:, :]).then_inc(evac, n.up(evac))
            send_gates(0, 32)
            early[1] = 32 * DC
            merge("w_merge2", 2, 58, 29, 11, RC + 8, a["x_kept_1"])
            tail("2", 50, 29, 40, PARTS2, relu_up)
            norm(48, split=False)

            norm(40, S("x_normed"), 1)
            act.dma_start(a["x_kept_2"], W3(0, DC)).then_inc(S("x_stored"), 16)
            act.wait_ge(S("x_stored"), 32)
            copy_tiles("in_m", 18, W3(0, 18))
            act.activation(W(18)[0:4, :], W(16)[0:4, :], ACT.Identity, bias=V("bi")[0:4]).then_inc(chain, n.up(chain))
            act.activation(W(19)[0:4, :], W(17)[0:4, :], ACT.Identity, bias=V("bf")[0:4]).then_inc(chain, n.up(chain))
            act.wait_ge(chain, n.own(chain))
            act.activation(W(20)[0:4, :], W(19)[0:4, :], ACT.Abs).then_inc(chain, n.up(chain))
            act.wait_ge(chain, n.own(chain))
            act.activation(W(20)[0:4, :], W(20)[0:4, :], ACT.Exp, scale=-1.0).then_inc(chain, n.up(chain))
            act.wait_ge(chain, n.own(chain))
            act.activation(W(20)[0:4, :], W(20)[0:4, :], ACT.Ln, bias=eps["one"][0:4])\
                .then_inc(S("lf_parts"), n.up(S("lf_parts")))
            act.wait_ge(S("lf_parts"), n.own(S("lf_parts")))
            for c in range(4):
                act.activation(W(12 + c), W(12 + c), ACT.Sigmoid).then_inc(chain, n.up(chain))
            act.wait_ge(psum_for["act"], n.next(psum_for["act"]))
            act.copy(SM(100, 16), bank[4][:, 0:16]).then_inc(evac, n.up(evac))
            act.wait_ge(evac, n.own(evac))
            for t in range(NT):
                act.wait_ge(psum_for["act"], n.next(psum_for["act"]))
                act.copy(W(25 + t), bank[4 + t % 2][:, :]).then_inc(evac, n.up(evac))
                act.wait_ge(evac, n.own(evac))
            act.wait_ge(S("m_sum"), n.next(S("m_sum")))
            act.activation(W(24)[0:4, :], W(24)[0:4, :], ACT.Exp, scale=-1.0)\
                .then_inc(S("decay_row"), n.up(S("decay_row")))
            act.wait_ge(S("decay_row"), n.own(S("decay_row")))
            for h in range(4):
                for s in range(NT):
                    act.wait_ge(S("exponent_ready"), n.next(S("exponent_ready")))
                    act.activation(W(29 + s)[:, s * P:T], W(29 + s)[:, s * P:T], ACT.Exp, scale=-1.0)\
                        .then_inc(S("exps3_ready"), n.up(S("exps3_ready")))
                act.wait_ge(psum_for["act"], n.next(psum_for["act"]))
                act.copy(W(41), bank[6][:, :]).then_inc(evac, n.up(evac))
                act.wait_ge(evac, n.own(evac))
                act.wait_ge(S("h_ready"), n.next(S("h_ready")))
                act.activation(W(44), W(43), ACT.Square).then_inc(S("h_square"), n.up(S("h_square")))
                act.wait_ge(psum_for["act"], n.next(psum_for["act"]))
                act.activation(W(44), bank[7][:, :], ACT.Ln, bias=eps[1e-06], scale=1.0 / P)\
                    .then_inc(evac, n.up(evac))
                act.wait_ge(evac, n.own(evac))
                act.activation(W(44), W(44), ACT.Exp, scale=-0.5).then_inc(S("h_rstd"), n.up(S("h_rstd")))
                act.wait_ge(S("h_rstd"), n.own(S("h_rstd")))
                send_gates(IN_MLSTM)
                send_gates(0)
            send_gates(0, 32 + EARLY_M)

            act.wait_ge(S("m_done"), n.next(S("m_done")))
            copy_tiles("in_l", 16, W3(0, 16))
            for c in range(4):
                act.wait_ge(psum_for["act"], n.next(psum_for["act"]))
                act.activation(W(26 + c), bank[4 + c % 2][:, :], ACT.Identity, bias=V("bgla", c))\
                    .then_inc(evac, n.up(evac))
                act.wait_ge(evac, n.own(evac))
            act.activation(W(18, 4), W(26, 4), ACT.Abs).then_inc(chain, n.up(chain))
            act.wait_ge(chain, n.own(chain))
            act.activation(W(18, 4), W(18, 4), ACT.Exp, scale=-1.0).then_inc(chain, n.up(chain))
            act.wait_ge(chain, n.own(chain))
            act.activation(W(18, 4), W(18, 4), ACT.Ln, bias=eps["one"]).then_inc(S("lf_parts"), n.up(S("lf_parts")))
            act.wait_ge(S("lf_parts"), n.own(S("lf_parts")))
            act.activation(W(12, 4), W(12, 4), ACT.Silu).then_inc(chain, n.up(chain))
            act.wait_ge(chain, n.own(chain))
            for t in range(NT):
                act.wait_ge(psum_for["act"], n.next(psum_for["act"]))
                act.copy(W(22 + t), bank[6 + t % 2][:, :]).then_inc(evac, n.up(evac))
                act.wait_ge(evac, n.own(evac))
            lvl = 0
            for h in range(4):
                for half in (256, 128, 64, 32, 16, 8, 4, 2, 1):
                    act.wait_ge(S("exponent_ready"), n.next(S("exponent_ready")))
                    e = W(28 + lvl % 2).rearrange("p (n s t) -> p n s t", s=2, t=half)
                    dd = W(26 + lvl % 2).rearrange("p (n s t) -> p n s t", s=2, t=half)
                    act.activation(e[:, :, 0, :], dd[:, :, 0, :], ACT.Exp, scale=-1.0 / 16)\
                        .then_inc(chain, n.up(chain))
                    act.activation(e[:, :, 1, :], dd[:, :, 1, :], ACT.Exp, scale=1.0 / 16)\
                        .then_inc(S("exps3_ready"), n.up(S("exps3_ready")))
                    send_gates(IN_GLA)
                    lvl += 1
                act.wait_ge(psum_for["act"], n.next(psum_for["act"]))
                if h:
                    act.wait_ge(S("h_used"), n.next(S("h_used")))
                act.mul(W(41), bank[6][:, :], float(P) ** (-0.5)).then_inc(evac, n.up(evac))
                act.wait_ge(evac, n.own(evac))
                act.activation(W(42), W(41), ACT.Square).then_inc(S("h_square"), n.up(S("h_square")))
                act.wait_ge(psum_for["act"], n.next(psum_for["act"]))
                act.activation(W(43), bank[7][:, :], ACT.Ln, bias=eps[1e-06], scale=1.0 / P)\
                    .then_inc(evac, n.up(evac))
                act.wait_ge(evac, n.own(evac))
                act.activation(W(43), W(43), ACT.Exp, scale=-0.5).then_inc(S("h_rstd"), n.up(S("h_rstd")))
                act.wait_ge(S("h_rstd"), n.own(S("h_rstd")))
                send_gates(EARLY_L * DC // 4 - 9 * IN_GLA)
                send_gates(0)
            send_gates(0, 32 + EARLY_M + EARLY_L)

            act.wait_ge(S("h_used"), n.next(S("h_used")))
            copy_tiles("in_d", 16, W3(0, 16))
            act.activation(W(17)[32:36, :], W(17)[32:36, :], ACT.Sigmoid)\
                .then_inc(S("beta_ready"), n.up(S("beta_ready")))
            act.wait_ge(S("beta_ready"), n.own(S("beta_ready")))
            act.activation(W(48)[32:36, :], W(16)[32:36, :], ACT.Identity, bias=V("dtb")[32:36])\
                .then_inc(chain, n.up(chain))
            act.wait_ge(chain, n.own(chain))
            act.activation(W(49)[32:36, :], W(48)[32:36, :], ACT.Abs).then_inc(chain, n.up(chain))
            act.wait_ge(chain, n.own(chain))
            act.activation(W(49)[32:36, :], W(49)[32:36, :], ACT.Exp, scale=-1.0).then_inc(chain, n.up(chain))
            act.wait_ge(chain, n.own(chain))
            act.activation(W(49)[32:36, :], W(49)[32:36, :], ACT.Ln, bias=eps["one"][32:36])\
                .then_inc(chain, n.up(chain))
            act.wait_ge(chain, n.own(chain))
            act.activation(SM(60)[32:36], V("alog")[32:36], ACT.Exp).then_inc(S("lf_parts"), n.up(S("lf_parts")))
            act.wait_ge(S("lf_parts"), n.own(S("lf_parts")))
            act.wait_ge(S("conv3_done"), n.next(S("conv3_done")))
            act.activation(W(18, 12), W(18, 12), ACT.Silu).then_inc(chain, n.up(chain))
            act.wait_ge(chain, n.own(chain))
            for c in range(8):
                act.activation(W(c), W(18 + c), ACT.Square).then_inc(S("qk_square"), n.up(S("qk_square")))
            send_gates(0, 41 + IN_GDN[0] // DC)
            for c in range(8):
                act.wait_ge(psum_for["act"], n.next(psum_for["act"]))
                act.activation(W(c), bank[4 + c % 2][:, :], ACT.Ln, bias=eps[1e-06]).then_inc(evac, n.up(evac))
                act.wait_ge(evac, n.own(evac))
            for c in range(8):
                act.activation(W(c), W(c), ACT.Exp, scale=-0.5).then_inc(S("qk_rstd"), n.up(S("qk_rstd")))
            act.activation(W(12, 4), W(12, 4), ACT.Silu).then_inc(chain, n.up(chain))
            act.wait_ge(chain, n.own(chain))
            act.wait_ge(S("b_rows"), n.next(S("b_rows")))
            act.activation(W(42, 4), W(42, 4), ACT.Exp).then_inc(chain, n.up(chain))
            act.activation(W(46, 4), W(46, 4), ACT.Exp).then_inc(chain, n.up(chain))
            act.activation(W(38, 4), W(38, 4), ACT.Exp).then_inc(S("decays_ready"), n.up(S("decays_ready")))
            act.wait_ge(S("decays_ready"), n.own(S("decays_ready")))
            send_gates(0, 41 + sum(IN_GDN) // DC)
            early[1] = 41 * DC + sum(IN_GDN)
            for t in range(NT):
                act.wait_ge(psum_for["act"], n.next(psum_for["act"]))
                act.copy(W(18 + t), bank[4 + t % 2][:, :]).then_inc(evac, n.up(evac))
                act.wait_ge(evac, n.own(evac))
            for t in range(NT):
                act.wait_ge(psum_for["act"], n.next(psum_for["act"]))
                act.copy(W(34 + t), bank[4 + t % 2][:, :]).then_inc(evac, n.up(evac))
                act.wait_ge(evac, n.own(evac))
            for c0 in range(0, NT, 2):
                for hf in range(2):
                    act.wait_ge(psum_for["act"], n.next(psum_for["act"]))
                    act.copy(W(26 + hf), bank[4 + hf][:, :]).then_inc(evac, n.up(evac))
                for lv in range(1, 7):
                    for hf in range(2):
                        act.wait_ge(psum_for["act"], n.next(psum_for["act"]))
                        act.copy(W(28 + hf), bank[4 + hf][:, :]).then_inc(evac, n.up(evac))
                    send_gates(IN_LEVEL)
            for ch in range(NT):
                act.wait_ge(psum_for["act"], n.next(psum_for["act"]))
                act.copy(W(40), bank[5][:, :]).then_inc(evac, n.up(evac))
                act.wait_ge(evac, n.own(evac))
                act.wait_ge(psum_for["act"], n.next(psum_for["act"]))
                act.copy(W3(4, 4)[:, :, ch * P:(ch + 1) * P], bank[6][:, :].rearrange("p (c t) -> p c t", c=4))\
                    .then_inc(evac, n.up(evac))
                act.wait_ge(evac, n.own(evac))
                send_gates(IN_STATE)
            for c in range(4):
                act.activation(W(42 + c), W(4 + c), ACT.Square).then_inc(S("y_square"), n.up(S("y_square")))
            for c in range(4):
                act.wait_ge(psum_for["act"], n.next(psum_for["act"]))
                act.activation(W(c), bank[4 + c % 2][:, :], ACT.Ln, bias=eps[1e-06], scale=1.0 / P)\
                    .then_inc(evac, n.up(evac))
                act.wait_ge(evac, n.own(evac))
            for c in range(4):
                act.activation(W(c), W(c), ACT.Exp, scale=-0.5).then_inc(S("y_rstd"), n.up(S("y_rstd")))
            send_gates(0, 56)
            merge("w_merge3", 3, 26, 36, 50, 12, a["x_kept_2"])
            tail("3", 18, 8, 40, PARTS2, relu_up)
            norm(48, split=False)

        @block.vector
        def _(dve):
            n = Count()
            chain = S("dve_chain")
            evac = evac_by["dve"]

            def norm(gain, sq):
                dve.wait_ge(S("rstd_ready"), n.next(S("rstd_ready")))
                for c in range(DC + 1):
                    if c < DC:
                        dve.scalar_tensor_tensor(x_raw[:, c, :], X(c), V(gain, c), W(sq), ALU.mult, ALU.mult)\
                            .then_inc(S("xn_raw"), n.up(S("xn_raw")))
                    if c:
                        dve.wait_ge(S("xn_high"), n.next(S("xn_high")))
                        dve.tensor_tensor(xl[:, c - 1, :], x_raw[:, c - 1, :], plain(xh[:, c - 1, :]), ALU.subtract)\
                            .then_inc(S("xn_split"), n.up(S("xn_split")))
                dve.wait_ge(S("xn_split"), n.own(S("xn_split")))

            def final_norm(gain, sq, sem):
                dve.wait_ge(S("rstd_ready"), n.next(S("rstd_ready")))
                for c in range(DC):
                    dve.scalar_tensor_tensor(X(c), X(c), V(gain, c), W(sq), ALU.mult, ALU.mult)\
                        .then_inc(S(sem), n.up(S(sem)))
                dve.wait_ge(S(sem), n.own(S(sem)))

            def low_parts(first, high, count, has_high, done):
                for c in range(count):
                    dve.wait_ge(has_high, n.next(has_high))
                    dve.tensor_tensor(WR(first + c), W(first + c), plain(WR(high + c)), ALU.subtract)\
                        .then_inc(done, n.up(done))
                dve.wait_ge(done, n.own(done))

            def loop_tiles(stage, total, per, fn):
                base = n.seen.get(psum_for["dve"].name, 0)
                assert base == handed_at[stage]["dve"], (stage, base, handed_at[stage])
                whole, rest = divmod(total, per)

                def some(i, count):
                    for b in range(count):
                        dve.wait_ge(psum_for["dve"], i * per + (base + b + 1))
                        fn(i, b).then_inc(evac, 1)

                with dve.Fori(0, whole) as i:
                    some(i, per)
                if rest:
                    some(whole, rest)
                n.seen[psum_for["dve"].name] = base + total
                n.made[evac.name] = base + total
                dve.wait_ge(evac, base + total)

            def residual_squared(stage, sq):
                for c in range(DC):
                    dve.wait_ge(psum_for["dve"], n.next(psum_for["dve"]))
                    dve.tensor_tensor(X(c), X(c), bank[c % RING][:, :], ALU.add).then_inc(evac, n.up(evac))
                    dve.wait_ge(evac, n.own(evac))
                    o = W(sq + 1) if c else W(sq)
                    dve.tensor_tensor(o, X(c), X(c), ALU.mult).then_inc(chain, n.up(chain))
                    dve.wait_ge(chain, n.own(chain))
                    if c:
                        sig = S("squares_ready") if c == DC - 1 else chain
                        dve.tensor_tensor(W(sq), W(sq), W(sq + 1), ALU.add).then_inc(sig, n.up(sig))
                        dve.wait_ge(sig, n.own(sig))

            def residual(stage):
                def add(i, b):
                    t = dyn(W3(0, DC), i * RING + b)
                    return dve.tensor_tensor(t, t, bank[b][:, :], ALU.add)
                loop_tiles(stage, DC, RING, add)

            def split_hidden(p, h0, i, per, b):
                h, l = hidden_at(p)
                high, low = [dyn(WR(t, 8).rearrange("p (c t) -> p c t", c=8), i * per + b) for t in (h, l)]
                raw = dyn(W3(l, 8), i * per + b)
                dve.tensor_copy(high, raw).then_inc(S("hidden_high"), 1)
                dve.wait_ge(S("hidden_high"), i * per + (h0 + b + 1))
                dve.tensor_tensor(low, raw, plain(high), ALU.subtract).then_inc(S("hidden_split"), 1)

            def squared_up(stage, p, k):
                a0, h0 = handed_at[stage]["act"], hidden[0]
                low = W3(hidden_at(p)[1], 8)
                s0 = n.made.get(S("hidden_square").name, 0)
                with dve.Fori(0, k // RING) as i:
                    for b in range(RING):
                        dve.wait_ge(evac_by["act"], i * RING + (a0 + b + 1))
                        dve.tensor_tensor(dyn(low, i * RING + b), W(56 + b), W(56 + b), ALU.mult)\
                            .then_inc(S("hidden_square"), 1)
                        dve.wait_ge(S("hidden_square"), i * RING + (s0 + b + 1))
                        split_hidden(p, h0, i, RING, b)
                n.made[S("hidden_square").name] = s0 + k
                hidden[0] += k

            def gated_up(stage, p, k):
                a0, h0, base = handed_at[stage]["act"], hidden[0], handed_at[stage]["dve"]
                low = W3(hidden_at(p)[1], 8)
                with dve.Fori(0, k // 2) as i:
                    for q in range(2):
                        dve.wait_ge(evac_by["act"], i * 2 + (a0 + q + 1))
                        dve.wait_ge(psum_for["dve"], i * 2 + (base + q + 1))
                        dve.tensor_tensor(dyn(low, i * 2 + q), W(56 + q), bank[2 * q + 1][:, :], ALU.mult)\
                            .then_inc(evac, 1)
                        dve.wait_ge(evac, i * 2 + (base + q + 1))
                        split_hidden(p, h0, i, 2, q)
                n.seen[psum_for["dve"].name] = base + k
                n.made[evac.name] = base + k
                hidden[0] += k

            hidden = [0]

            def tail(name, merged, high, gain, sq, next_sq, parts, up_tiles):
                low_parts(merged, high, DC, S("merged_high"), S("merged_split"))
                dve.wait_ge(S("x_back"), n.next(S("x_back"), 16))
                residual_squared(f"out{name}", sq)
                norm(gain, sq)
                for stage, p, up in ffn_stages(name, parts):
                    if up:
                        up_tiles(stage, p, parts[p])
                    elif p < len(parts) - 1:
                        residual(stage)
                    else:
                        residual_squared(stage, next_sq)

            def merge(name, nb, sg, out_at, tmp):
                for j in range(DC):
                    dve.wait_ge(S("sigmoids_ready"), n.next(S("sigmoids_ready")))
                    for g in range(nb):
                        dve.wait_ge(psum_for["dve"], n.next(psum_for["dve"]))
                        b = branch_bank(nb, j, g)
                        o = W(out_at + j) if g == 0 else W(tmp)
                        dve.tensor_tensor(o, W(sg + nb * (j % 2) + g), bank[b][:, :], ALU.mult)\
                            .then_inc(evac, n.up(evac))
                        dve.wait_ge(evac, n.own(evac))
                        if g:
                            end = j == DC - 1 and g == nb - 1
                            sig = S("merged_ready") if end else chain
                            dve.tensor_tensor(W(out_at + j), W(out_at + j), W(tmp), ALU.add).then_inc(sig, n.up(sig))
                            dve.wait_ge(sig, n.own(sig))

            def inverse_start(at, xT, heads):
                lv = C("level", 0, P).unsqueeze(1).broadcast_to([P, heads, P])
                ts3 = ident.unsqueeze(1).broadcast_to([P, heads, P])
                dve.tensor_tensor(xT, at, lv, ALU.mult).then_inc(chain, n.up(chain))
                dve.wait_ge(chain, n.own(chain))
                dve.tensor_tensor(xT, ts3, xT, ALU.subtract).then_inc(S("inverse_start"), n.up(S("inverse_start")))
                dve.wait_ge(S("inverse_start"), n.own(S("inverse_start")))

            def inverse_levels(x, xT, halves):
                for lv in range(1, 7):
                    for hf in range(halves):
                        if lv < 6:
                            dve.wait_ge(psum_for["dve"], n.next(psum_for["dve"]))
                            dve.tensor_tensor(x(hf), x(hf), bank[6 + hf][:, :], ALU.subtract)\
                                .then_inc(evac, n.up(evac))
                        dve.wait_ge(psum_for["dve"], n.next(psum_for["dve"]))
                        dve.tensor_tensor(xT(hf), xT(hf), bank[4 + hf][:, :], ALU.subtract).then_inc(evac, n.up(evac))

            for col, val in ((300, 1e-6), (301, 64e-6), (302, 64e-5), (303, 1.0), (304, 15 * LN2)):
                dve.memset(SM(col), val).then_inc(chain, n.up(chain))
            dve.memset(SM(312), 0.0).then_inc(S("small_consts"), n.up(S("small_consts")))
            dve.wait_ge(S("small_consts"), n.own(S("small_consts")))
            dve.wait_ge(S("loads_ready"), n.next(S("loads_ready"), 32))

            dve.wait_ge(S("x_loaded_0"), 16)
            dve.wait_ge(S("x_loaded_1"), 16)
            norm("mix1", 48)
            for c in range(8):
                dve.wait_ge(S("qk_rstd"), n.next(S("qk_rstd")))
                dve.scalar_tensor_tensor(W(c), W(c), V("qg" if c < 4 else "kg"), W(48 + c), ALU.mult, ALU.mult)\
                    .then_inc(S("qk_normed"), n.up(S("qk_normed")))
            dve.wait_ge(psum_for["dve"], n.next(psum_for["dve"]))
            dve.tensor_copy(SM(210, 32).rearrange("p (t h) -> p t h", t=NT), bank[4][:,
                :].rearrange("p (t c) -> p t c", t=NT)[:, :, 32:40])\
                .then_inc(evac, n.up(evac))
            dve.wait_ge(evac, n.own(evac))
            k = 0
            mask_at = {1: 52 * T, 2: 52 * T + 256, 3: 52 * T + 640}
            for i in range(1, NT):
                w = (i + 1) * P
                sc = work[:, mask_at[i]:mask_at[i] + w]
                for h in range(8):
                    k += 1
                    dve.wait_ge(evac_by["act"], handed_at["scores"]["act"] + k)
                    if h == 0:
                        dve.tensor_scalar(sc, W(55)[:, 0:w], SM(210 + 8 * i), None, ALU.mult)\
                            .then_inc(S("relu_used"), n.up(S("relu_used")))
                        dve.wait_ge(S("relu_used"), n.own(S("relu_used")))
                    else:
                        dve.scalar_tensor_tensor(sc, W(55 + h % 2)[:, 0:w], SM(210 + 8 * i + h), sc, ALU.mult,
                            ALU.add)\
                            .then_inc(S("relu_used"), n.up(S("relu_used")))
                        dve.wait_ge(S("relu_used"), n.own(S("relu_used")))
                dve.tensor_tensor(sc[:, i * P:w], sc[:, i * P:w], C("caus"), ALU.add).then_inc(chain, n.up(chain))
                dve.wait_ge(chain, n.own(chain))
            steps = [(i, h) for i in range(NT) for h in range(8)]

            def add_max(g):
                i, h = steps[g]
                w, b = (i + 1) * P, g % 2
                dve.wait_ge(psum_for["dve"], n.next(psum_for["dve"]))
                dve.wait_ge(S("bias_ready"), n.next(S("bias_ready")))
                dve.tensor_tensor_reduce(out=W(57 + b)[:, 0:w], in0=bank[4 + b][:, 0:w], in1=W(55 + b)[:, 0:w],
                    scale=1.0, scalar=-3e+38, op0=ALU.add, op1=ALU.max, accum_out=SM(208 + b))\
                    .then_inc(evac, n.up(evac))
                dve.wait_ge(evac, n.own(evac))
                dve.tensor_scalar(SM(200 + b), SM(208 + b), -1.0, None, ALU.mult)\
                    .then_inc(S("logits_ready"), n.up(S("logits_ready")))
                dve.wait_ge(S("logits_ready"), n.own(S("logits_ready")))

            def scale_probs(g):
                i, h = steps[g]
                w, b = (i + 1) * P, g % 2
                dve.wait_ge(S("exps_ready"), n.next(S("exps_ready")))
                dve.reciprocal(SM(202 + b), SM(204 + b)).then_inc(chain, n.up(chain))
                dve.wait_ge(chain, n.own(chain))
                dve.tensor_scalar(W(57 + b)[:, 0:w], W(57 + b)[:, 0:w], SM(202 + b), None, ALU.mult)\
                    .then_inc(S("probs_ready"), n.up(S("probs_ready")))

            def top_k(g):
                i, h = steps[g][0] + 1, steps[g][1]
                if i == NT or h >= TOPK_STEPS:
                    return
                w, rounds = (i + 1) * P, TOPK // 8
                sc = work[:, mask_at[i]:mask_at[i] + w]
                for _ in range(rounds * h // TOPK_STEPS, rounds * (h + 1) // TOPK_STEPS):
                    dve.max(SM(250, 8), sc).then_inc(chain, n.up(chain))
                    dve.wait_ge(chain, n.own(chain))
                    dve.match_replace(sc, SM(250, 8), sc, PICKED).then_inc(chain, n.up(chain))
                    dve.wait_ge(chain, n.own(chain))
                if h == TOPK_STEPS - 1:
                    dve.tensor_scalar(sc, sc, PICKED / 3 * 2, NEG, ALU.is_gt, ALU.mult)\
                        .then_inc(S("mask_ready"), n.up(S("mask_ready")))
                    dve.wait_ge(S("mask_ready"), n.own(S("mask_ready")))

            add_max(0)
            for g in range(len(steps)):
                if g + 1 < len(steps):
                    add_max(g + 1)
                scale_probs(g)
                top_k(g)
                k = g - SHIFT_FROM
                if 0 <= k < len(shift_tiles):
                    t = shift_tiles[k]
                    dve.wait_ge(S("shift_diff"), n.next(S("shift_diff")))
                    dve.scalar_tensor_tensor(W(t), W(38 + k % 2), V("mu", t - 16), W(t), ALU.mult, ALU.add)\
                        .then_inc(S("shift_done"), n.up(S("shift_done")))
            dve.wait_ge(evac_by["act"], handed_at["rwkv"]["act"] + 12)
            for c in range(4):
                dve.tensor_tensor_scan(W(44 + c), C("reset"), W(40 + c), 0.0, ALU.mult, ALU.add)\
                    .then_inc(chain, n.up(chain))
                dve.wait_ge(chain, n.own(chain))
            c4 = lambda i: W(i, 4).rearrange("p (c n t) -> p c n t", c=4, n=NT)
            dve.tensor_tensor(c4(48), c4(44), c4(44)[:, :, :, 63:64].broadcast_to([P, 4, NT, P]), ALU.subtract)\
                .then_inc(chain, n.up(chain))
            dve.wait_ge(chain, n.own(chain))
            dve.tensor_tensor(W(40, 4), W(48, 4), W(40, 4), ALU.subtract)\
                .then_inc(S("decay_sums"), n.up(S("decay_sums")))
            dve.wait_ge(S("decay_sums"), n.own(S("decay_sums")))
            for c in range(4):
                dve.tensor_scalar(W(56 + c), W(20 + c), V("kk", c), None, ALU.mult)\
                    .then_inc(S("kk_raw"), n.up(S("kk_raw")))
            for c in range(4):
                dve.wait_ge(psum_for["dve"], n.next(psum_for["dve"]))
                dve.tensor_scalar(W(28 + c), bank[4 + c % 2][:, :], 1e-24, 2.0 ** 30, ALU.max, ALU.mult)\
                    .then_inc(evac, n.up(evac))
            dve.tensor_scalar(SM(40, 4), vec[:, VEC["ka"][0]:VEC["ka"][0] + 4], -1.0, 1.0, ALU.mult, ALU.add)\
                .then_inc(chain, n.up(chain))
            dve.wait_ge(chain, n.own(chain))
            for c in range(4):
                dve.wait_ge(S("kk_rstd"), n.next(S("kk_rstd")))
                dve.tensor_tensor(W(56 + c), W(56 + c), W(28 + c), ALU.mult).then_inc(chain, n.up(chain))
                dve.wait_ge(chain, n.own(chain))
                dve.tensor_scalar(W(60 + c % 2), W(52 + c), V("ka", c), SM(40 + c), ALU.mult, ALU.add)\
                    .then_inc(chain, n.up(chain))
                dve.wait_ge(chain, n.own(chain))
                dve.tensor_tensor(W(20 + c), W(20 + c), W(60 + c % 2), ALU.mult).then_inc(chain, n.up(chain))
                dve.wait_ge(chain, n.own(chain))
                dve.tensor_tensor(W(52 + c), W(56 + c), W(52 + c), ALU.mult).then_inc(chain, n.up(chain))
                dve.wait_ge(chain, n.own(chain))
                dve.scalar_tensor_tensor(W(28 + c), W(16 + c), V("rk", c), W(20 + c), ALU.mult, ALU.mult)\
                    .then_inc(S("rk_ready"), n.up(S("rk_ready")))
            dve.memset(SM(312), 0.0).then_inc(S("kb_ready"), n.up(S("kb_ready")))
            dve.wait_ge(S("kb_ready"), n.own(S("kb_ready")))
            dve.wait_ge(S("decays_ready"), n.next(S("decays_ready")))
            ar = W(0, 8).rearrange("p (c n s t) -> p c n s t", c=4, n=NT, s=2)
            for c in range(4):
                w3 = lambda i: W(i).rearrange("p (n t) -> p n t", n=NT)
                dve.tensor_tensor(ar[:, c, :, 0, :], w3(56 + c), w3(40 + c), ALU.mult).then_inc(chain, n.up(chain))
                dve.tensor_tensor(ar[:, c, :, 1, :], w3(16 + c), w3(44 + c), ALU.mult).then_inc(chain, n.up(chain))
            dve.tensor_tensor(SM(20, 12).rearrange("p (c n) -> p c n", c=4), c4(44)[:, :, 0:3, 127], SM(0,
                16).rearrange("p (c n) -> p c n", c=4)[:, :, 1:4], ALU.mult)\
                .then_inc(S("operands_ready"), n.up(S("operands_ready")))
            dve.wait_ge(S("operands_ready"), n.own(S("operands_ready")))
            for c in range(4):
                dve.wait_ge(psum_for["dve"], n.next(psum_for["dve"]))
                dve.tensor_tensor(W(16 + c), bank[4 + c][:, :], W(24 + c), ALU.mult).then_inc(evac, n.up(evac))
                dve.wait_ge(evac, n.own(evac))
            two = lambda name: C(name, 0, 2 * P).unsqueeze(1).broadcast_to([P, 2, 2 * P])
            s3 = W(31)[:, 0:4 * HD].rearrange("p (c v) -> p c v", c=4)
            for ch in range(NT):
                for h in range(8):
                    dve.wait_ge(psum_for["dve"], n.next(psum_for["dve"]))
                    dve.tensor_tensor(W(40 + h).rearrange("p (a b) -> p a b", a=2), bank[4 + h % 2][:,
                        :].rearrange("p (a b) -> p a b", a=2), two("strict"), ALU.mult)\
                        .then_inc(evac, n.up(evac))
                dve.wait_ge(evac, n.made[evac.name])
                at = W3(40, 8)[:, :, 0:P]
                inverse_start(at, W(50, 2).rearrange("p (h t) -> p h t", h=8), 8)
                inverse_levels(lambda hf: W(48 + hf), lambda hf: W(50 + hf), 2)
                r4 = W(57).rearrange("p (c s v) -> p c s v", c=4, s=2)
                for par in range(2):
                    dve.wait_ge(psum_for["dve"], n.next(psum_for["dve"]))
                    dve.tensor_copy(r4[:, :, par, :], bank[4 + par][:, 0:4 * HD].rearrange("p (c v) -> p c v", c=4))\
                        .then_inc(evac, n.up(evac))
                if ch < NT - 1:
                    dve.wait_ge(psum_for["dve"], n.next(psum_for["dve"]))
                    u3 = bank[7][:, 0:4 * HD].rearrange("p (c v) -> p c v", c=4)
                    gg = SM(20, 12).rearrange("p (c n) -> p c n", c=4)[:, :, ch:ch + 1].broadcast_to([P, 4, HD])
                    if ch == 0:
                        dve.tensor_copy(s3, u3).then_inc(evac, n.up(evac))
                        dve.wait_ge(evac, n.own(evac))
                    else:
                        dve.tensor_tensor(s3, s3, u3, ALU.add).then_inc(evac, n.up(evac))
                        dve.wait_ge(evac, n.own(evac))
                    dve.tensor_tensor(s3, s3, gg, ALU.mult).then_inc(S("state_ready"), n.up(S("state_ready")))
                    dve.wait_ge(S("state_ready"), n.own(S("state_ready")))
            for c in range(4):
                dve.wait_ge(psum_for["dve"], n.next(psum_for["dve"]))
                dve.scalar_tensor_tensor(W(58 + c), bank[4 + c % 2][:, :], -1.0 / HD, W(58 + c), ALU.mult, ALU.add)\
                    .then_inc(evac, n.up(evac))
                dve.wait_ge(evac, n.own(evac))
            for c in range(4):
                dve.wait_ge(S("y_rstd"), n.next(S("y_rstd")))
                dve.scalar_tensor_tensor(W(58 + c), W(58 + c), V("lnw", c), W(44 + c), ALU.mult, ALU.mult)\
                    .then_inc(chain, n.up(chain))
                dve.wait_ge(chain, n.own(chain))
                dve.scalar_tensor_tensor(W(58 + c), W(58 + c), V("lnb", c), W(16 + c), ALU.add, ALU.add)\
                    .then_inc(chain, n.up(chain))
                dve.wait_ge(chain, n.own(chain))
                sig = S("branches_ready") if c == 3 else chain
                dve.tensor_tensor(W(36 + c), W(58 + c), W(36 + c), ALU.mult).then_inc(sig, n.up(sig))
                dve.wait_ge(sig, n.own(sig))

            low_parts(32, 16, 8, S("branch_high"), S("branch_split"))
            merge("w_merge1", 2, 8, 40, 12)
            tail("1", 40, 24, "ffn1", 48, 40, PARTS1, gated_up)
            dve.memset(SM(312), 0.0).then_inc(S("x_ready"), n.up(S("x_ready")))

            norm("mix2", 40)
            dve.wait_ge(S("x_stored"), 16)
            xr = work[:, 0:RC * 515].rearrange("p (c t) -> p c t", c=RC)
            dve.memset(xr[:, :, 0:3], 0.0).then_inc(chain, n.up(chain))

            dve.wait_ge(chain, n.own(chain))
            for c in range(RC):
                dve.wait_ge(psum_for["dve"], n.next(psum_for["dve"]))
                dve.tensor_copy(xr[:, c, 3:515], bank[2 * (c % 2)][:, :]).then_inc(evac, n.up(evac))
                dve.wait_ge(evac, n.own(evac))
                dve.tensor_scalar(W(21 + c), xr[:, c, 0:T], V("convw", c), V("convb", c), ALU.mult, ALU.add)\
                    .then_inc(chain, n.up(chain))
                dve.wait_ge(chain, n.own(chain))
                for k in range(1, 4):
                    sig = S("conv_done") if (c, k) == (RC - 1, 3) else chain
                    dve.scalar_tensor_tensor(W(21 + c), xr[:, c, k:k + T], V("convw", k * RC + c), W(21 + c),
                        ALU.mult, ALU.add)\
                        .then_inc(sig, n.up(sig))
                    dve.wait_ge(sig, n.own(sig))

            def softplus_tail(e, s, q, p, width, rows):
                v = lambda at: SM(at, width)[rows]
                dve.tensor_scalar(v(s), v(e), 2.0, None, ALU.add).then_inc(chain, n.up(chain))
                dve.wait_ge(chain, n.own(chain))
                dve.reciprocal(v(s), v(s)).then_inc(chain, n.up(chain))
                dve.wait_ge(chain, n.own(chain))
                dve.tensor_tensor(v(s), v(e), v(s), ALU.mult).then_inc(chain, n.up(chain))
                dve.wait_ge(chain, n.own(chain))
                dve.tensor_tensor(v(q), v(s), v(s), ALU.mult).then_inc(chain, n.up(chain))
                dve.wait_ge(chain, n.own(chain))
                dve.tensor_scalar(v(p), v(q), 1.0 / 15, 1.0 / 13, ALU.mult, ALU.add).then_inc(chain, n.up(chain))
                dve.wait_ge(chain, n.own(chain))
                for d in (11, 9, 7, 5, 3, 1):
                    dve.tensor_tensor(v(p), v(p), v(q), ALU.mult).then_inc(chain, n.up(chain))
                    dve.wait_ge(chain, n.own(chain))
                    dve.tensor_scalar(v(p), v(p), 1.0 / d, None, ALU.add).then_inc(chain, n.up(chain))
                    dve.wait_ge(chain, n.own(chain))
                dve.scalar_tensor_tensor(v(p), v(p), 2.0, v(s), ALU.mult, ALU.mult).then_inc(chain, n.up(chain))
                dve.wait_ge(chain, n.own(chain))

            dve.wait_ge(S("lam_exp"), n.next(S("lam_exp")))
            allp = slice(0, P)
            softplus_tail(0, 10, 20, 30, RC, allp)
            dve.tensor_scalar(SM(10, RC), vec[:, VEC["lam"][0]:VEC["lam"][0] + RC], -1.0, 0.0, ALU.mult, ALU.max)\
                .then_inc(chain, n.up(chain))
            dve.wait_ge(chain, n.own(chain))
            dve.tensor_tensor(SM(30, RC), SM(30, RC), SM(10, RC), ALU.add).then_inc(chain, n.up(chain))
            dve.wait_ge(chain, n.own(chain))
            dve.tensor_scalar(SM(20, RC), SM(30, RC), 8.0, None, ALU.mult).then_inc(chain, n.up(chain))
            dve.wait_ge(chain, n.own(chain))
            dve.tensor_scalar(SM(30, RC), SM(30, RC), -8.0, None, ALU.mult)\
                .then_inc(S("softplus_ready"), n.up(S("softplus_ready")))
            dve.wait_ge(S("softplus_ready"), n.own(S("softplus_ready")))
            for c in range(RC):
                dve.wait_ge(evac_by["act"], handed_at["lru"]["act"] + 2 * c + 2)
                dve.tensor_tensor(W(c), W(c), W(21 + c), ALU.mult).then_inc(chain, n.up(chain))
                dve.wait_ge(chain, n.own(chain))
            for c in range(RC):
                dve.wait_ge(S("a_square"), n.next(S("a_square")))
                dve.scalar_tensor_tensor(W(41 + c), W(51 + c), 1.0, W(41 + c), ALU.add, ALU.mult)\
                    .then_inc(S("norm_square"), n.up(S("norm_square")))
            for c in range(RC):
                dve.wait_ge(S("lru_norm"), n.next(S("lru_norm")))
                dve.tensor_tensor(W(c), W(41 + c), W(c), ALU.mult).then_inc(chain, n.up(chain))
                dve.wait_ge(chain, n.own(chain))
                dve.tensor_tensor_scan(W(21 + c), W(31 + c), W(c), 0.0, ALU.mult, ALU.add)\
                    .then_inc(chain, n.up(chain))
                dve.wait_ge(chain, n.own(chain))
                sig = S("ya_ready") if c == RC - 1 else chain
                dve.tensor_tensor(W(11 + c), W(11 + c), W(21 + c), ALU.mult).then_inc(sig, n.up(sig))
                dve.wait_ge(sig, n.own(sig))
            dve.wait_ge(psum_for["dve"], n.next(psum_for["dve"]))
            dve.tensor_scalar(W(50), bank[4][:, :], -1.0 / D, None, ALU.mult).then_inc(evac, n.up(evac))
            dve.wait_ge(evac, n.own(evac))
            for c in range(8):
                dve.tensor_tensor(W(29 + c), W(29 + c), W(50), ALU.add).then_inc(S("v_centred"), n.up(S("v_centred")))
                dve.wait_ge(S("v_centred"), n.own(S("v_centred")))
            dve.wait_ge(S("v_rstd"), n.next(S("v_rstd")))
            for c in range(8):
                dve.scalar_tensor_tensor(W(29 + c), W(29 + c), V("lng2", c), W(45), ALU.mult, ALU.mult)\
                    .then_inc(chain, n.up(chain))
                dve.wait_ge(chain, n.own(chain))
                sig = S("v_normed") if c == 7 else chain
                dve.tensor_scalar(W(29 + c), W(29 + c), V("lnb2", c), None, ALU.add).then_inc(sig, n.up(sig))
                dve.wait_ge(sig, n.own(sig))
            dve.wait_ge(S("sgu_ready"), n.next(S("sgu_ready")))
            for g in range(8):
                dve.wait_ge(psum_for["dve"], n.next(psum_for["dve"]))
                bs = W(48, 2)[:, g * P:(g + 1) * P].unsqueeze(1).broadcast_to([P, NT, P])
                dve.tensor_tensor(W(50 + g % 2).rearrange("p (n t) -> p n t", n=NT), bank[4 + g % 2][:,
                    :].rearrange("p (n t) -> p n t", n=NT), bs, ALU.add)\
                    .then_inc(evac, n.up(evac))
                dve.wait_ge(evac, n.own(evac))
                sig = S("branches_ready") if g == 7 else chain
                dve.tensor_tensor(W(21 + g), W(21 + g), W(50 + g % 2), ALU.mult).then_inc(sig, n.up(sig))
                dve.wait_ge(sig, n.own(sig))
            low_parts(11, 29, RC + 8, S("branch_high"), S("branch_split"))
            merge("w_merge2", 2, 58, 50, 8)
            tail("2", 50, 29, "ffn2", 40, 48, PARTS2, squared_up)
            final_norm("fin2", 48, "x_normed")

            norm("mix3", 40)
            r4 = slice(0, 4)
            dve.memset(W(23)[r4, :], 0.0).then_inc(chain, n.up(chain))
            dve.wait_ge(chain, n.own(chain))
            dve.wait_ge(S("lf_parts"), n.next(S("lf_parts")))
            dve.scalar_tensor_tensor(W(19)[r4, :], W(19)[r4, :], 0.0, W(20)[r4, :], ALU.min, ALU.subtract)\
                .then_inc(chain, n.up(chain))
            dve.wait_ge(chain, n.own(chain))
            dve.tensor_tensor_scan(W(20)[r4, :], C("ones", 0, 1)[r4].broadcast_to([4, T]), W(19)[r4, :], 0.0,
                ALU.mult, ALU.add)\
                .then_inc(chain, n.up(chain))
            dve.wait_ge(chain, n.own(chain))
            dve.tensor_tensor(W(21)[r4, :], W(18)[r4, :], W(20)[r4, :], ALU.subtract)\
                .then_inc(S("gates_ready"), n.up(S("gates_ready")))
            dve.wait_ge(S("gates_ready"), n.own(S("gates_ready")))
            dve.tensor_tensor_scan(W(22)[r4, :], W(21)[r4, :], W(23)[r4, :], 0.0, ALU.max, ALU.max)\
                .then_inc(chain, n.up(chain))
            dve.wait_ge(chain, n.own(chain))
            dve.tensor_tensor(W(24)[r4, :], W(20)[r4, :], W(22)[r4, :], ALU.add)\
                .then_inc(S("m_sum"), n.up(S("m_sum")))
            dve.wait_ge(S("m_sum"), n.own(S("m_sum")))
            dve.wait_ge(evac_by["act"], handed_at["c_turned"]["act"])
            for h in range(4):
                dve.wait_ge(psum_for["dve"], n.next(psum_for["dve"]))
                dve.tensor_copy(W(45), bank[5][:, :]).then_inc(evac, n.up(evac))
                dve.wait_ge(evac, n.own(evac))
                for s in range(NT):
                    dve.tensor_scalar(W(29 + s)[:, s * P:T], W(45)[:, s * P:T], SM(100 + 4 * s + h), 0.0,
                        ALU.subtract, ALU.max)\
                        .then_inc(S("exponent_ready"), n.up(S("exponent_ready")))
                for s in range(NT):
                    dve.wait_ge(S("exps3_ready"), n.next(S("exps3_ready")))
                    dve.wait_ge(psum_for["dve"], n.next(psum_for["dve"]))
                    dve.scalar_tensor_tensor(W(33 + s)[:, s * P:T], bank[6 + s % 2][:, s * P:T], float(P) ** (-0.5),
                        W(29 + s)[:, s * P:T], ALU.mult, ALU.mult)\
                        .then_inc(evac, n.up(evac))
                    dve.wait_ge(evac, n.own(evac))
                    dg = W(33 + s)[:, s * P:(s + 1) * P]
                    sig = S("weights_ready") if s == NT - 1 else chain
                    dve.tensor_tensor(dg, dg, C("incl"), ALU.mult).then_inc(sig, n.up(sig))
                    dve.wait_ge(sig, n.own(sig))
                dve.wait_ge(evac_by["act"], handed_at[f"floor{h}"]["act"])
                dve.wait_ge(psum_for["dve"], n.next(psum_for["dve"]))
                dve.tensor_copy(W(42), bank[5][:, :]).then_inc(evac, n.up(evac))
                dve.wait_ge(evac, n.own(evac))
                dve.scalar_tensor_tensor(W(42), W(42), -1.0, W(42), ALU.mult, ALU.max).then_inc(chain, n.up(chain))
                dve.wait_ge(chain, n.own(chain))
                dve.tensor_tensor(W(42), W(42), W(41), ALU.max).then_inc(chain, n.up(chain))
                dve.wait_ge(chain, n.own(chain))
                dve.reciprocal(W(42), W(42)).then_inc(chain, n.up(chain))
                dve.wait_ge(chain, n.own(chain))
                dve.wait_ge(psum_for["dve"], n.next(psum_for["dve"]))
                dve.tensor_tensor(W(43), bank[4][:, :], W(42), ALU.mult).then_inc(evac, n.up(evac))
                dve.wait_ge(evac, n.own(evac))
                dve.tensor_tensor(W(43), W(43), W(12 + h), ALU.mult).then_inc(S("h_ready"), n.up(S("h_ready")))
                dve.wait_ge(S("h_ready"), n.own(S("h_ready")))
                dve.wait_ge(S("h_rstd"), n.next(S("h_rstd")))
                sig = S("m_done") if h == 3 else chain
                dve.scalar_tensor_tensor(W(50 + h), W(43), V("hm", h), W(44), ALU.mult, ALU.mult)\
                    .then_inc(sig, n.up(sig))
                dve.wait_ge(sig, n.own(sig))

            dve.wait_ge(S("lf_parts"), n.next(S("lf_parts")))
            dve.scalar_tensor_tensor(W(18, 4), W(26, 4), 0.0, W(18, 4), ALU.min, ALU.subtract)\
                .then_inc(chain, n.up(chain))
            dve.wait_ge(chain, n.own(chain))
            for c in range(4):
                dve.tensor_tensor_scan(W(18 + c), C("ones", 0, 1).broadcast_to([P, T]), W(18 + c), 0.0, ALU.mult,
                    ALU.add)\
                    .then_inc(chain, n.up(chain))
                dve.wait_ge(chain, n.own(chain))
            halves = (256, 128, 64, 32, 16, 8, 4, 2, 1)
            todo = [(h, half) for h in range(4) for half in halves]
            diag = work[:, 32 * T:32 * T + 4 * 640].rearrange("p (s t) -> p s t", t=640)[:, :, 0:P]

            def differences(l):
                h, half = todo[l]
                b4 = W(18 + h).rearrange("p (n t) -> p n t", t=2 * half)
                dve.tensor_tensor(W(26 + l % 2).rearrange("p (n t) -> p n t", t=2 * half), b4, b4[:, :,
                    half - 1:half].broadcast_to([P, T // (2 * half), 2 * half]), ALU.subtract)\
                    .then_inc(S("exponent_ready"), n.up(S("exponent_ready")))

            def decayed(l):
                h, half = todo[l]
                dve.wait_ge(S("exps3_ready"), n.next(S("exps3_ready")))
                v = lambda i: W(i).rearrange("p (n s t) -> p n s t", s=2, t=half)
                dve.tensor_tensor(v(30 + l % 2)[:, :, 0, :], v(28 + l % 2)[:, :, 0, :], v(4 + h)[:, :, 0, :],
                    ALU.mult)\
                    .then_inc(chain, n.up(chain))
                dve.tensor_tensor(v(30 + l % 2)[:, :, 1, :], v(28 + l % 2)[:, :, 1, :], v(h)[:, :, 1, :], ALU.mult)\
                    .then_inc(S("level_ready"), n.up(S("level_ready")))

            def collect(b, half):
                dve.wait_ge(psum_for["dve"], n.next(psum_for["dve"]))
                b4 = bank[b][:, :].rearrange("p (s t) -> p s t", s=NT)
                if half == 256:
                    dve.tensor_copy(W3(32, 2)[:, :, 256:T], bank[b][:, :].rearrange("p (s t) -> p s t", s=2))\
                        .then_inc(evac, n.up(evac))
                    dve.wait_ge(evac, n.own(evac))
                elif half == 128:
                    o = work[:, 32 * T:36 * T].rearrange("p (s t) -> p s t", s=2)
                    dve.tensor_copy(o[:, 0, P:2 * P], bank[b][:, 0:P]).then_inc(chain, n.up(chain))
                    dve.wait_ge(chain, n.own(chain))
                    dve.tensor_copy(o[:, 1, 3 * P:4 * P], bank[b][:, P:2 * P]).then_inc(evac, n.up(evac))
                    dve.wait_ge(evac, n.own(evac))
                elif half == 64:
                    dve.tensor_tensor(diag, b4, C("level", 6 * P, P).unsqueeze(1).broadcast_to([P, NT, P]), ALU.mult)\
                        .then_inc(evac, n.up(evac))
                    dve.wait_ge(evac, n.own(evac))
                else:
                    m = C("level", (half.bit_length() - 1) * P, P) if half else ident
                    w3 = W(37).rearrange("p (s t) -> p s t", s=NT)
                    dve.tensor_tensor(w3, b4, m.unsqueeze(1).broadcast_to([P, NT, P]), ALU.mult)\
                        .then_inc(evac, n.up(evac))
                    dve.wait_ge(evac, n.own(evac))
                    sig = S("weights_ready") if half == 0 else chain
                    dve.tensor_tensor(diag, diag, w3, ALU.add).then_inc(sig, n.up(sig))
                    dve.wait_ge(sig, n.own(sig))

            differences(0)
            for l in range(len(todo)):
                h, half = todo[l]
                if l + 1 < len(todo):
                    differences(l + 1)
                decayed(l)
                if half != 256:
                    collect(4 + (l - 1) % 2, todo[l - 1][1])
                if half == 1:
                    collect(4 + l % 2, 1)
                    collect(4 + (l + 1) % 2, 0)
                    dve.wait_ge(S("h_rstd"), n.next(S("h_rstd")))
                    dve.scalar_tensor_tensor(W(54 + h), W(41), V("hl", h), W(43), ALU.mult, ALU.mult)\
                        .then_inc(chain, n.up(chain))
                    dve.wait_ge(chain, n.own(chain))
                    dve.tensor_tensor(W(54 + h), W(54 + h), W(12 + h), ALU.mult)\
                        .then_inc(S("h_used"), n.up(S("h_used")))
                    dve.wait_ge(S("h_used"), n.own(S("h_used")))

            for c in range(12):
                dve.wait_ge(evac_by["act"], handed_at["in_d"]["act"] + c + 1)
                dve.tensor_scalar(W(18 + c), W(c), V("conv3", 36 + c), None, ALU.mult).then_inc(chain, n.up(chain))
                dve.wait_ge(chain, n.own(chain))
                for k in (2, 1, 0):
                    sh = 3 - k
                    sig = S("conv3_done") if (c, k) == (11, 0) else chain
                    dve.scalar_tensor_tensor(W(18 + c)[:, sh:T], W(c)[:, 0:T - sh], V("conv3", 12 * k + c),
                        W(18 + c)[:, sh:T], ALU.mult, ALU.add)\
                        .then_inc(sig, n.up(sig))
                    dve.wait_ge(sig, n.own(sig))
            r = slice(32, 36)
            dve.wait_ge(S("lf_parts"), n.next(S("lf_parts")))
            dve.scalar_tensor_tensor(W(49)[r, :], W(48)[r, :], 0.0, W(49)[r, :], ALU.max, ALU.add)\
                .then_inc(chain, n.up(chain))
            dve.wait_ge(chain, n.own(chain))
            dve.tensor_scalar(W(49)[r, :], W(49)[r, :], SM(60)[r], -1.0, ALU.mult, ALU.mult)\
                .then_inc(chain, n.up(chain))
            dve.wait_ge(chain, n.own(chain))
            dve.tensor_tensor_scan(W(48)[r, :], C("reset")[r, :], W(49)[r, :], 0.0, ALU.mult, ALU.add)\
                .then_inc(S("decay_row"), n.up(S("decay_row")))
            dve.wait_ge(S("decay_row"), n.own(S("decay_row")))
            for c in range(8):
                dve.wait_ge(S("qk_rstd"), n.next(S("qk_rstd")))
                if c < 4:
                    dve.scalar_tensor_tensor(W(18 + c), W(18 + c), float(P) ** (-0.5), W(c), ALU.mult, ALU.mult)\
                        .then_inc(chain, n.up(chain))
                else:
                    dve.tensor_tensor(W(18 + c), W(18 + c), W(c), ALU.mult).then_inc(chain, n.up(chain))
                    dve.wait_ge(chain, n.own(chain))
            dve.wait_ge(psum_for["dve"], n.next(psum_for["dve"]))
            dve.tensor_copy(SM(100, 16), bank[4][:, 0:16]).then_inc(evac, n.up(evac))
            dve.wait_ge(evac, n.own(evac))
            kq = W(0, 8).rearrange("p (h n s t) -> p h n s t", h=4, n=NT, s=2)
            v3 = lambda i: W(i).rearrange("p (n t) -> p n t", n=NT)
            for h in range(4):
                dve.wait_ge(psum_for["dve"], n.next(psum_for["dve"]))
                dve.tensor_copy(W(42 + h), bank[5][:, :]).then_inc(evac, n.up(evac))
                dve.wait_ge(psum_for["dve"], n.next(psum_for["dve"]))
                dve.tensor_copy(W(8 + h), bank[6 + h % 2][:, :]).then_inc(evac, n.up(evac))
                dve.wait_ge(evac, n.own(evac))
                dve.tensor_tensor(kq[:, h, :, 0, :], v3(22 + h), v3(8 + h), ALU.mult).then_inc(chain, n.up(chain))
                dve.tensor_copy(kq[:, h, :, 1, :], v3(18 + h)).then_inc(chain, n.up(chain))
                dve.tensor_tensor(W(26 + h), W(26 + h), W(8 + h), ALU.mult).then_inc(chain, n.up(chain))
                dve.wait_ge(chain, n.own(chain))
            for h in range(4):
                dve.tensor_tensor(v3(46 + h), v3(42 + h)[:, :, 127:128].broadcast_to([P, NT, P]), v3(42 + h),
                    ALU.subtract)\
                    .then_inc(chain, n.up(chain))
                for ch in range(NT):
                    cs = slice(ch * P, (ch + 1) * P)
                    sig = S("b_rows") if (h, ch) == (3, 3) else chain
                    dve.tensor_scalar(W(38 + h)[:, cs], W(42 + h)[:, cs], SM(100 + 4 * ch + h), 0.0, ALU.subtract,
                        ALU.min)\
                        .then_inc(sig, n.up(sig))
            dve.wait_ge(S("decays_ready"), n.next(S("decays_ready")))
            for h in range(4):
                dve.tensor_tensor(v3(8 + h), kq[:, h, :, 0, :], v3(42 + h), ALU.mult).then_inc(chain, n.up(chain))
                dve.tensor_tensor(W(30 + h), W(18 + h), W(42 + h), ALU.mult).then_inc(chain, n.up(chain))
                dve.tensor_tensor(W(34 + h), W(22 + h), W(46 + h), ALU.mult).then_inc(chain, n.up(chain))
            dve.tensor_copy(SM(120, 16).rearrange("p (h n) -> p h n", h=4), W(42,
                4).rearrange("p (h n t) -> p h n t", h=4, n=NT)[:, :, :, 127])\
                .then_inc(S("operands_ready"), n.up(S("operands_ready")))
            dve.wait_ge(S("operands_ready"), n.own(S("operands_ready")))
            mats = W(42, 8).rearrange("p (h n s t) -> p h n s t", h=4, n=NT, s=2)
            m2 = C("strict", 0, 2 * P).rearrange("p (s t) -> p s t", s=2)
            for h in range(4):
                for ch in range(NT):
                    m = h * NT + ch
                    dve.wait_ge(psum_for["dve"], n.next(psum_for["dve"]))
                    dve.tensor_tensor(mats[:, h, ch], bank[6 + m % 2][:, 0:2 * P].rearrange("p (s t) -> p s t", s=2),
                        m2, ALU.mult)\
                        .then_inc(evac, n.up(evac))
                    dve.wait_ge(evac, n.own(evac))
                    dve.tensor_tensor(mats[:, h, ch], mats[:, h, ch], W(38 + h)[:,
                        ch * P:(ch + 1) * P].unsqueeze(1).broadcast_to([P, 2, P]), ALU.mult)\
                        .then_inc(chain, n.up(chain))
                    dve.wait_ge(chain, n.own(chain))
            for c0 in range(0, NT, 2):
                for ch in (c0, c0 + 1):
                    inverse_start(mats[:, :, ch, 0, :], W(22 + ch).rearrange("p (h t) -> p h t", h=4), 4)
                inverse_levels(lambda hf: W(26 + hf), lambda hf, c0=c0: W(22 + c0 + hf), 2)
            for ch in range(NT):
                if ch:
                    dve.wait_ge(psum_for["dve"], n.next(psum_for["dve"]))
                    dve.tensor_tensor(W(39), W(34 + ch), bank[4][:, :], ALU.subtract).then_inc(evac, n.up(evac))
                    dve.wait_ge(evac, n.own(evac))
                if ch < NT - 1:
                    dve.wait_ge(psum_for["dve"], n.next(psum_for["dve"]))
                    if ch == 0:
                        dve.tensor_copy(W(41), bank[7][:, :]).then_inc(evac, n.up(evac))
                        dve.wait_ge(evac, n.own(evac))
                    else:
                        for h in range(4):
                            hs = slice(h * P, (h + 1) * P)
                            sig = evac if h == 3 else chain
                            dve.scalar_tensor_tensor(W(41)[:, hs], W(41)[:, hs], SM(120 + 4 * h + ch), bank[7][:,
                                hs], ALU.mult, ALU.add)\
                                .then_inc(sig, n.up(sig))
                            dve.wait_ge(sig, n.own(sig))
            for c in range(4):
                dve.wait_ge(S("y_rstd"), n.next(S("y_rstd")))
                dve.scalar_tensor_tensor(W(58 + c), W(4 + c), V("hd", c), W(c), ALU.mult, ALU.mult)\
                    .then_inc(chain, n.up(chain))
                dve.wait_ge(chain, n.own(chain))
                sig = S("branches_ready") if c == 3 else chain
                dve.tensor_tensor(W(58 + c), W(58 + c), W(12 + c), ALU.mult).then_inc(sig, n.up(sig))
                dve.wait_ge(sig, n.own(sig))
            low_parts(50, 36, 12, S("branch_high"), S("branch_split"))
            merge("w_merge3", 3, 26, 18, 32)
            tail("3", 18, 8, "ffn3", 40, 48, PARTS2, squared_up)
            final_norm("fin3", 48, "result_ready")

        @block.gpsimd
        def _(pool):
            n = Count()
            chain = S("pool_chain")

            done = [0]

            def low_parts(n_slabs):
                s0 = done[0]
                n_slabs = min(n_slabs, total_slabs - s0)
                whole, rest = divmod(n_slabs, RING)

                def some(i, count):
                    for j in range(count):
                        slot = (s0 + j) % RING
                        pool.wait_ge(S("slab_high"), i * RING + (s0 + j + 1))
                        pool.tensor_tensor(slab_low[:, slot, :], slab[:, slot, :], plain(slab_high[:, slot, :]),
                                           ALU.subtract).then_inc(S("slab_split"), 1)

                if whole:
                    with pool.Fori(0, whole) as i:
                        some(i, RING)
                if rest:
                    some(whole, rest)
                done[0] += n_slabs

            def masked_levels(sources, am, heads, fill=0):
                pool.wait_ge(S("inverse_start"), n.next(S("inverse_start"), len(sources)))
                for lv in range(1, 7):
                    if lv >= 3:
                        pool.wait_ge(S("level_begun"), n.next(S("level_begun"), 2 if lv == 3 else 1))
                    for k, at in enumerate(sources):
                        sig = S("level_masked") if k == len(sources) - 1 else chain
                        pool.tensor_tensor(am(lv, k), at, C("level", lv * P, P).unsqueeze(1).broadcast_to([P, heads, P]),
                                           ALU.mult).then_inc(sig, n.up(sig))
                    gate_lows(fill)
                pool.wait_ge(S("level_begun"), n.next(S("level_begun")))

            pool.dma_start(work[0:BUCKETS, 59 * T:59 * T + NREL], a["buckets"]).then_inc(S("bias_loads"), 16)
            pool.dma_start(W(61)[0:BUCKETS, 0:8], a["rel_bias"]).then_inc(S("bias_loads"), 16)
            pool.wait_ge(S("loads_ready"), n.next(S("loads_ready"), 32))
            low_parts(LOOK + 32)
            early = [0, 0, 0]

            def gate_lows(products):
                ready = early[2] // DC
                early[2] = early[1]
                early[1] += products
                while early[0] < ready:
                    low_parts(1)
                    early[0] += 1

            mask_at = {1: 52 * T, 2: 52 * T + 256, 3: 52 * T + 640}
            pool.wait_ge(evac_by["act"], handed_at["flipped"]["act"])
            g = 0
            for i in range(NT):
                w = (i + 1) * P
                if i == 0:
                    pool.wait_ge(S("relu_used"), n.next(S("relu_used"), 8 * (NT - 1)))
                else:
                    pool.wait_ge(S("mask_ready"), n.next(S("mask_ready")))
                for h in range(8):
                    if g >= 2:
                        pool.wait_ge(evac_by["dve"], handed_at["attention"]["dve"] + g - 1)
                    m = C("caus") if i == 0 else work[:, mask_at[i]:mask_at[i] + w]
                    pool.tensor_tensor(W(55 + g % 2)[:, 0:w], W(40 + h)[:, 3 * P - i * P:3 * P - i * P + w], m,
                        ALU.add)\
                        .then_inc(S("bias_ready"), n.up(S("bias_ready")))
                    k = g - (SHIFT_FROM - 1)
                    if 0 <= k < len(shift_tiles):
                        if k >= 2:
                            pool.wait_ge(S("shift_done"), n.next(S("shift_done")))
                        z, o = W(shift_tiles[k]), W(38 + k % 2)
                        pool.tensor_scalar(o[:, 0:1], z[:, 0:1], -1.0, None, ALU.mult).then_inc(chain, n.up(chain))
                        pool.tensor_tensor(o[:, 1:T], z[:, 0:T - 1], z[:, 1:T], ALU.subtract)\
                            .then_inc(S("shift_diff"), n.up(S("shift_diff")))
                    gate_lows(IN_ATTENTION)
                    g += 1
            low_parts(AFTER_ATTENTION - early[0])
            early = [AFTER_ATTENTION] + [AFTER_ATTENTION * DC] * 2
            pool.wait_ge(evac_by["act"], handed_at["rwkv"]["act"])
            pool.dma_start(W(59), a["w2a2"]).then_inc(S("lora_loads"), 16)
            pool.dma_start(W(60), a["g2a"]).then_inc(S("lora_loads"), 16)
            pool.dma_start(W(61)[0:32, :], a["g2b"]).then_inc(S("lora_loads"), 16)
            pool.wait_ge(S("kb_ready"), n.next(S("kb_ready")))
            pool.wait_ge(S("decays_ready"), n.next(S("decays_ready")))
            pool.tensor_tensor(W(8, 4), W(52, 4), W(48, 4), ALU.mult).then_inc(chain, n.up(chain))
            pool.tensor_tensor(W(12, 4), W(20, 4), W(48, 4), ALU.mult)\
                .then_inc(S("operands_ready_2"), n.up(S("operands_ready_2")))
            pool.wait_ge(S("operands_ready_2"), n.own(S("operands_ready_2")))
            for ch in range(NT):
                masked_levels([W3(40, 8)[:, :, 0:P]], lambda lv, k: W(54 + 2 * (lv % 2), 2).rearrange("p (h t) -> p h t", h=8), 8, IN_RWKV)
            low_parts(16 - early[0])
            low_parts(8 + DC + 2 * FFN1 + DC * len(PARTS1))
            low_parts(2 * RC)
            pool.wait_ge(S("slab_split"), done[0])
            pool.wait_ge(S("x_ready"), n.next(S("x_ready")))
            pool.memset(W(51, 10), 0.0).then_inc(chain, n.up(chain))
            pool.wait_ge(chain, n.own(chain))
            for w, name in ((51, "lru_a"), (56, "lru_x")):
                o = W(w, 5)[:, 0:RC * P].rearrange("p (c j) -> p c j", j=P)
                for e in range(2):
                    rows = slice(e * HD, (e + 1) * HD)
                    pool.dma_start(o[rows, :, rows], a[name][rows, :, :]).then_inc(S("gate_loads"), 16)
            low_parts(EARLY_2)
            pool.wait_ge(S("ya_ready"), n.next(S("ya_ready")))
            pool.dma_start(W(46, 2), a["sgu_w"]).then_inc(S("sgu_loads"), 16)
            pool.dma_start(W(48, 2), a["sgu_b"].partition_broadcast(P)).then_inc(S("sgu_loads"), 16)
            low_parts(16)
            pool.wait_ge(S("slab_split"), done[0])
            pool.wait_ge(S("sgu_loads"), n.next(S("sgu_loads"), 32))
            pool.memset(W(46, 2).rearrange("p (g t) -> p g t", g=8)[64:P, :, 0:64], 0.0)\
                .then_inc(S("sgu_ready"), n.up(S("sgu_ready")))
            pool.wait_ge(S("sgu_ready"), n.own(S("sgu_ready")))
            low_parts(16 - EARLY_2 + 24 + DC + FFN2 + DC * len(PARTS2))
            low_parts(18 + EARLY_M)
            pool.wait_ge(S("m_done"), n.next(S("m_done")))
            pool.dma_start(W(40)[64:80, :], a["gla_lr"]).then_inc(S("gla_load"), 16)
            low_parts(16 + EARLY_L + 16)
            low_parts(sum(IN_GDN) // DC)
            early = [0, 0, 0]
            mats = W(42, 8).rearrange("p (h n s t) -> p h n s t", h=4, n=NT, s=2)
            for c0 in range(0, NT, 2):
                masked_levels([mats[:, :, ch, 0, :] for ch in (c0, c0 + 1)],
                              lambda lv, k: W(38 + 2 * (lv % 2) + k).rearrange("p (h t) -> p h t", h=4), 4, IN_LEVEL)
            low_parts(24 - EARLY_M - EARLY_L - sum(IN_GDN) // DC - early[0])
            low_parts(16 + DC + FFN2 + DC * len(PARTS2))


def _tile(w, cols, width=P):
    blocks = w[:, cols].reshape(-1, P, width)
    if width < P:
        blocks = np.concatenate([blocks, np.zeros((blocks.shape[0], P, P - width), np.float32)], axis=2)
    return blocks.transpose(1, 0, 2).reshape(P, -1)


def _slabs(tiles, per):
    n = len(tiles) // per
    return np.stack([_filled(np.concatenate(tiles[i * per:(i + 1) * per], axis=1)) for i in range(n)])


def _plain(w, start=0, count=None):
    count = w.shape[1] // P if count is None else count
    return _slabs([_tile(w, slice(start + i * P, start + (i + 1) * P)) for i in range(count)], 1)


def _parts(w, parts):
    rows = [P * sum(parts[:p]) for p in range(len(parts) + 1)]
    return [_plain(w[rows[p]:rows[p + 1]]) for p in range(len(parts))]


def _gates(w_in, gates):
    return np.stack([_tile(w_in, slice(g + j * P, g + (j + 1) * P)) for j in range(DC) for g in gates])


def _merge(branches, layout):
    out = []
    for j in range(DC):
        t = np.concatenate([_tile(b, slice(j * P, (j + 1) * P)) for b in branches], axis=1)
        at = np.cumsum([0] + layout) * P
        out.append(np.concatenate([_filled(t[:, at[q]:at[q + 1]]) for q in range(len(layout))], axis=1))
    return np.stack(out)


def _filled(t):
    return np.concatenate([t, np.zeros((P, SLAB * P - t.shape[1]), np.float32)], axis=1)


def _odd(w, parts):
    t = np.zeros((w.shape[0], P), np.float32)
    for at, c, k in parts:
        t[:, at:at + k] = w[:, c:c + k]
    return _tile(t, slice(0, P))


def arrays_of(i):
    A, R = {}, {k: np.asarray(v) for k, v in i.items()}
    A["x"] = R["x"][0].T.reshape(DC, P, T).transpose(1, 0, 2)
    vec = np.zeros((P, NVEC), np.float32)

    def put(name, v, k=0):
        v = np.asarray(v).reshape(-1, P).T
        vec[:, VEC[name][0] + k:VEC[name][0] + k + v.shape[1]] = v

    def rows(name, v, at):
        vec[at:at + v.shape[0], VEC[name][0]] = v

    w = R["w_in"][0]
    rk = 4 * 512 + 64 + 8
    gate = rk + 3 * 512 + 64 + 64 + 160
    tiles = [_tile(w, slice(c * P, (c + 1) * P)) for c in range(16)]
    tiles += [_tile(w, slice(rk + c * P, rk + (c + 1) * P)) for c in range(14)]
    tiles += [_odd(w, [(0, 2048, 64), (64, 2048, 64)]), _odd(w, [(0, rk + 14 * P, 32), (32, 2112, 8)])]
    A["w_in_a"] = _slabs(tiles, 1)
    A["w_gates1"] = _gates(w, [gate, gate + D])
    A["w_merge1"] = _merge([R["w_branch_attn"][0], R["w_branch_rwkv"][0]], MERGE_SLABS["w_merge1"])
    A["w_out1"] = _plain(R["w_out"][0])
    gu = R["w_gate_up"][0]
    A["w_gu"] = _slabs([_tile(gu, slice((s * FFN1 + c) * P, (s * FFN1 + c + 1) * P)) for c in range(FFN1) for s in range(2)], 1)
    for p, part in enumerate(_parts(R["w_down"][0], PARTS1)):
        A[f"w_down1_{p}"] = part
    put("mix1", R["mix_norm"])
    put("qg", np.concatenate([R["attn_q_norm"][0]] * 2))
    put("kg", np.concatenate([R["attn_k_norm"][0]] * 2))
    mu = R["rwkv_mu"][0]
    put("mu", mu[:14 * P])
    rows_at = VEC["mu"][0] + 15
    vec[0:32, rows_at] = mu[14 * P:14 * P + 32]
    for name, key in (("w0", "rwkv_w0"), ("a0", "rwkv_a0"), ("kk", "rwkv_k_k"), ("ka", "rwkv_k_a"), ("rk", "rwkv_r_k"),
                      ("lnw", "rwkv_ln_w"), ("lnb", "rwkv_ln_b"), ("ffn1", "ffn_norm"), ("mix2", "norm_mix_g_2"),
                      ("convb", "conv_b_2"), ("convw", "conv_w_2"), ("ba", "lru_b_a_2"), ("bx", "lru_b_x_2"),
                      ("lam", "lru_lambda_2"), ("lng2", "sgu_ln_g_2"), ("lnb2", "sgu_ln_b_2"), ("ffn2", "norm_ffn_g_2"),
                      ("fin2", "final_norm_g_2"), ("mix3", "g_norm_mix_3"), ("bgla", "b_gla_3"), ("conv3", "conv_gdn_3"),
                      ("hm", "g_head_mlstm_3"), ("hl", "g_head_gla_3"), ("hd", "g_head_gdn_3"), ("ffn3", "g_norm_mlp_3"),
                      ("fin3", "g_final_3")):
        put(name, R[key])
    rows("bi", R["b_if_3"][0, 0:4], 0)
    rows("bf", R["b_if_3"][0, 4:8], 0)
    rows("alog", R["a_log_3"][0], 32)
    rows("dtb", R["dt_bias_3"][0], 32)
    A["vec"] = vec
    A["cst"] = constants()
    A["buckets"] = bucket_table()
    A["rel_bias"] = R["rel_bias"]
    A["w2a2"] = np.concatenate([R["rwkv_w2"][0], R["rwkv_a2"][0]], axis=0)
    A["g2a"], A["g2b"] = R["rwkv_g2"][0, :P], R["rwkv_g2"][0, P:]
    w = R["w_in_2"][0]
    A["w_in_b"] = _slabs([_tile(w, slice((s * RC + c) * P, (s * RC + c + 1) * P)) for c in range(RC) for s in range(2)], 1)
    u = 2 * RC * P
    A["w_uv"] = _plain(w, u, 16)
    A["w_gates2"] = _gates(w, [u + 2 * D, u + 3 * D])
    A["w_merge2"] = _merge([R["w_branch_a_2"][0], R["w_branch_b_2"][0]], MERGE_SLABS["w_merge2"])
    A["w_out2"] = _plain(R["w_out_2"][0])
    A["w_up2"] = _plain(R["w_up_2"][0])
    for p, part in enumerate(_parts(R["w_down_2"][0], PARTS2)):
        A[f"w_down2_{p}"] = part
    for name, key in (("lru_a", "lru_w_a_2"), ("lru_x", "lru_w_x_2")):
        A[name] = R[key][0].reshape(RC, P, HD).transpose(1, 0, 2)
    A["sgu_w"] = R["sgu_w_s_2"][0].transpose(2, 0, 1).reshape(P, 8 * P)
    A["sgu_b"] = R["sgu_b_s_2"][0].reshape(8 * P)
    w = R["w_in_3"][0]
    W_ = 512
    m0, l0 = 0, 4 * W_ + 8
    d0 = l0 + 4 * W_ + 16
    g0 = d0 + 4 * W_ + 8
    odd = [_odd(w, [(0, 4 * W_, 4), (32, d0 + 4 * W_ + 4, 4), (64, l0 + 4 * W_, 16)]),
           _odd(w, [(0, 4 * W_ + 4, 4), (32, d0 + 4 * W_, 4)])]
    A["w_in_m"] = _slabs([_tile(w, slice(c * P, (c + 1) * P)) for c in range(16)] + odd, 1)
    A["w_in_l"] = _plain(w, l0, 16)
    A["w_in_d"] = _plain(w, d0, 16)
    A["w_gates3"] = _gates(w, [g0, g0 + D, g0 + 2 * D])
    A["w_merge3"] = _merge([R["w_up_3"][0, b] for b in range(3)], MERGE_SLABS["w_merge3"])
    A["w_out3"] = _plain(R["w_out_3"][0])
    A["w_up3"] = _plain(R["w_mlp_in_3"][0])
    for p, part in enumerate(_parts(R["w_mlp_out_3"][0], PARTS2)):
        A[f"w_down3_{p}"] = part
    A["gla_lr"] = R["w_gla_lr_3"][0]
    return {k: np.ascontiguousarray(v, dtype=np.float32) for k, v in A.items()}


def build(nc, shapes):
    a = {k: nc.dram_tensor(f"in_{k}", s, F32, kind="ExternalInput").ap() for k, s in shapes.items()}
    a["scratch"] = nc.dram_tensor("bias_scratch", (8, NREL), F32, kind="Internal").ap()
    for k, nb in GATES.items():
        a[f"gates_{k}"] = nc.dram_tensor(f"gates_{k}", (DC, P, nb * T), F32, kind="Internal").ap()
    for k in (1, 2):
        a[f"x_kept_{k}"] = nc.dram_tensor(f"x_kept_{k}", (P, DC, T), F32, kind="Internal").ap()
    out = nc.dram_tensor("out_dram", (P, DC, T), F32, kind="ExternalOutput").ap()
    program(nc, a, out)


def kernel(**inputs):
    import concourse.bacc as bacc
    from concourse.bass_utils import run_bass_kernel_spmd

    nc = bacc.Bacc("TRN2", target_bir_lowering=False, num_devices=1)
    arrays = arrays_of(inputs)
    build(nc, {k: v.shape for k, v in arrays.items()})
    r = run_bass_kernel_spmd(nc, [{f"in_{k}": v for k, v in arrays.items()}], core_ids=[0])
    y = r.results[0]["out_dram"]
    return y.transpose(1, 0, 2).reshape(D, T).T.reshape(1, T, D)
```
